# Optimizing a Trainium2 kernel written in Bass

```python
import math
import jax
import jax.numpy as jnp
from jax import lax
import numpy as np

D_MODEL = 1024
BATCH = 1
SEQ = 256
DEPTH = 2

CHUNK = 64
HEAD_DIM = 64
ATTN_WIDTH = D_MODEL // 2
RWKV_WIDTH = D_MODEL - ATTN_WIDTH
N_Q_HEADS = ATTN_WIDTH // HEAD_DIM
N_KV_HEADS = 2
GQA_GROUP = N_Q_HEADS // N_KV_HEADS
KV_WIDTH = N_KV_HEADS * HEAD_DIM
WINDOW = 128
WINDOW_CHUNKS = WINDOW // CHUNK
N_RWKV_HEADS = RWKV_WIDTH // HEAD_DIM
DECAY_LORA = max(32, int(round(1.8 * D_MODEL ** 0.5 / 32)) * 32)
AAA_LORA = max(32, int(round(1.8 * D_MODEL ** 0.5 / 32)) * 32)
GATE_LORA = max(32, int(round(0.6 * D_MODEL ** 0.8 / 32)) * 32)
RWKV_LNX_EPS = 64e-5
PEER_HEADS = 8
PEER_TOPK = 16
N_SUBKEYS = 128
N_EXPERTS = N_SUBKEYS * N_SUBKEYS
PEER_HALF = 128
PEER_TOKEN_BLOCK = 128
PLE_DIM = 256
NORM_EPS = 1e-6
NEG_INF = -1e30

OFF_Q = 0
OFF_K = OFF_Q + ATTN_WIDTH
OFF_V = OFF_K + KV_WIDTH
OFF_RWKV = OFF_V + KV_WIDTH
RWKV_IN = 3 * RWKV_WIDTH + DECAY_LORA + AAA_LORA + GATE_LORA
IN_WIDTH = OFF_RWKV + RWKV_IN

kernel_name = "hybrid_swa_rwkv7_peer_block"

def _rmsnorm(x, g):
    xf = x.astype(jnp.float32)
    y = xf * lax.rsqrt(jnp.mean(xf * xf, axis=-1, keepdims=True) + NORM_EPS)
    return (y * g.astype(jnp.float32)).astype(x.dtype)

def _alibi_slopes(n):
    return 2.0 ** (-8.0 * jnp.arange(1, n + 1, dtype=jnp.float32) / n)

def _shift_chunks(a, n):
    if n == 0:
        return a
    nc = a.shape[1]
    pad = [(0, 0)] * a.ndim
    pad[1] = (n, 0)
    return jnp.pad(a, pad)[:, :nc]

def _swa_sink_attention(q, k, v, sinks):
    B, S, _ = q.shape
    nc = S // CHUNK
    q = q.reshape(B, nc, CHUNK, N_KV_HEADS, GQA_GROUP, HEAD_DIM)
    k = k.reshape(B, nc, CHUNK, N_KV_HEADS, HEAD_DIM)
    v = v.reshape(B, nc, CHUNK, N_KV_HEADS, HEAD_DIM)
    kb = jnp.concatenate([_shift_chunks(k, n) for n in range(WINDOW_CHUNKS - 1, -1, -1)], axis=2)
    vb = jnp.concatenate([_shift_chunks(v, n) for n in range(WINDOW_CHUNKS - 1, -1, -1)], axis=2)
    logits = jnp.einsum('bnqhgd,bnshd->bnhgqs', q, kb).astype(jnp.float32) * (HEAD_DIM ** -0.5)
    qi = jnp.arange(CHUNK)[:, None]
    kj = jnp.arange(WINDOW_CHUNKS * CHUNK)[None, :]
    dist = jnp.abs(qi - kj + (WINDOW_CHUNKS - 1) * CHUNK).astype(jnp.float32)
    slopes = _alibi_slopes(N_Q_HEADS).reshape(N_KV_HEADS, GQA_GROUP)
    logits = logits - slopes[:, :, None, None] * dist
    key_chunk = jnp.arange(nc)[:, None] - (WINDOW_CHUNKS - 1) + kj // CHUNK
    valid = key_chunk >= 0
    logits = jnp.where(valid[None, :, None, None, None, :], logits, NEG_INF)
    sink = jnp.broadcast_to(sinks.astype(jnp.float32).reshape(1, 1, N_KV_HEADS, GQA_GROUP, 1, 1),
                            logits.shape[:-1] + (1,))
    probs = jax.nn.softmax(jnp.concatenate([logits, sink], axis=-1), axis=-1)[..., :-1]
    out = jnp.einsum('bnhgqs,bnshd->bnqhgd', probs.astype(v.dtype), vb)
    return out.reshape(B, S, ATTN_WIDTH)

def _rwkv7_scan(r, w, k, v, a_, b_):
    B, S, H, N = r.shape

    def step(state, inp):
        rt, wt, kt, vt, at, bt = inp
        sa = jnp.einsum('bhvk,bhk->bhv', state, at)
        state = state * wt[:, :, None, :] + sa[..., None] * bt[:, :, None, :] + vt[..., None] * kt[:, :, None, :]
        y = jnp.einsum('bhvk,bhk->bhv', state, rt)
        return state, y

    xs = tuple(jnp.swapaxes(t, 0, 1) for t in (r, w, k, v, a_, b_))
    s0 = jnp.zeros((B, H, N, N), jnp.float32)
    _, ys = lax.scan(step, s0, xs)
    return jnp.swapaxes(ys, 0, 1)

def _rwkv7_mix(f, mu, w0, w_up, a0, a_up, g_up, k_k, k_a, r_k, lnx_w, lnx_b):
    B, S, _ = f.shape
    H, N = N_RWKV_HEADS, HEAD_DIM
    prev = jnp.pad(f, ((0, 0), (1, 0), (0, 0)))[:, :-1]
    f = f + (prev - f) * mu
    o1 = RWKV_WIDTH
    o2 = 2 * RWKV_WIDTH
    o3 = 3 * RWKV_WIDTH
    o4 = o3 + DECAY_LORA
    o5 = o4 + AAA_LORA
    r, k, v = f[..., :o1], f[..., o1:o2], f[..., o2:o3]
    xw, xa, xg = f[..., o3:o4], f[..., o4:o5], f[..., o5:]
    w = -jax.nn.softplus(-(w0 + jnp.tanh(xw) @ w_up)) - 0.5
    decay = jnp.exp(-jnp.exp(w.astype(jnp.float32)))
    a = jax.nn.sigmoid(a0 + xa @ a_up)
    g = jax.nn.sigmoid(xg) @ g_up
    kk = (k * k_k).astype(jnp.float32).reshape(B, S, H, N)
    kk = kk / jnp.maximum(jnp.linalg.norm(kk, axis=-1, keepdims=True), 1e-12)
    k = k * (1.0 + (a - 1.0) * k_a)
    hs = lambda t: t.astype(jnp.float32).reshape(B, S, H, N)
    rh, kh, vh, ah = hs(r), hs(k), hs(v), hs(a)
    y = _rwkv7_scan(rh, hs(decay), kh, vh, -kk, kk * ah)
    mean = jnp.mean(y, axis=-1, keepdims=True)
    var = jnp.mean(jnp.square(y - mean), axis=-1, keepdims=True)
    y = (y - mean) * lax.rsqrt(var + RWKV_LNX_EPS)
    y = y * lnx_w.astype(jnp.float32).reshape(H, N) + lnx_b.astype(jnp.float32).reshape(H, N)
    bonus = jnp.sum(rh * kh * r_k.astype(jnp.float32), axis=-1, keepdims=True)
    y = y + bonus * vh
    return (y.reshape(B, S, RWKV_WIDTH) * g.astype(jnp.float32)).astype(f.dtype)

def _peer(h, wq, keys, u_tab, v_tab):
    B, S, D = h.shape
    q = (h @ wq).reshape(B, S, PEER_HEADS, 2, PEER_HALF)
    sc = jnp.einsum('bshcd,cnd->bshcn', q, keys).astype(jnp.float32)
    top_v, top_i = lax.top_k(sc, PEER_TOPK)
    cand = (top_v[..., 0, :, None] + top_v[..., 1, None, :]).reshape(B, S, PEER_HEADS, PEER_TOPK * PEER_TOPK)
    best_v, best_c = lax.top_k(cand, PEER_TOPK)
    i1 = jnp.take_along_axis(top_i[..., 0, :], best_c // PEER_TOPK, axis=-1)
    i2 = jnp.take_along_axis(top_i[..., 1, :], best_c % PEER_TOPK, axis=-1)
    expert = i1 * N_SUBKEYS + i2
    gate = jax.nn.softmax(best_v, axis=-1).astype(h.dtype)
    nb = (B * S) // PEER_TOKEN_BLOCK
    hb = h.reshape(nb, PEER_TOKEN_BLOCK, D)
    eb = expert.reshape(nb, PEER_TOKEN_BLOCK, PEER_HEADS, PEER_TOPK)
    gb = gate.reshape(nb, PEER_TOKEN_BLOCK, PEER_HEADS, PEER_TOPK)

    def block(args):
        hx, ex, gx = args
        u = jnp.take(u_tab, ex, axis=0)
        act = jax.nn.gelu(jnp.einsum('thkd,td->thk', u, hx), approximate=False) * gx
        vv = jnp.take(v_tab, ex, axis=0)
        return jnp.einsum('thk,thkd->td', act, vv)

    out = lax.map(block, (hb, eb, gb))
    return out.reshape(B, S, D)

def setup_inputs(seed: int = 0) -> dict:
    key = jax.random.key(seed)
    ks = jax.random.split(key, 32)
    nrm = lambda i, shape, s: jax.random.normal(ks[i], shape, jnp.float32) * s
    gain = lambda i, shape: 1.0 + 0.02 * jax.random.normal(ks[i], shape, jnp.float32)
    return {
        "x": nrm(0, (BATCH, SEQ, D_MODEL), 1.0),
        "p": nrm(1, (DEPTH, BATCH, SEQ, PLE_DIM), 1.0),
        "norm_mix": gain(2, (DEPTH, D_MODEL)),
        "w_in": nrm(3, (DEPTH, D_MODEL, IN_WIDTH), D_MODEL ** -0.5),
        "b_in": nrm(4, (DEPTH, IN_WIDTH), 0.01),
        "attn_sinks": nrm(5, (DEPTH, N_Q_HEADS), 0.5),
        "attn_out_norm": gain(6, (DEPTH, ATTN_WIDTH)),
        "rwkv_mu": jax.random.uniform(ks[7], (DEPTH, RWKV_IN), jnp.float32),
        "rwkv_w0": jax.random.uniform(ks[8], (DEPTH, RWKV_WIDTH), jnp.float32, -3.0, 0.5),
        "rwkv_w_up": nrm(9, (DEPTH, DECAY_LORA, RWKV_WIDTH), 0.1),
        "rwkv_a0": nrm(10, (DEPTH, RWKV_WIDTH), 0.1),
        "rwkv_a_up": nrm(11, (DEPTH, AAA_LORA, RWKV_WIDTH), 0.5 * AAA_LORA ** -0.5),
        "rwkv_g_up": nrm(12, (DEPTH, GATE_LORA, RWKV_WIDTH), GATE_LORA ** -0.5),
        "rwkv_k_k": 0.85 + nrm(13, (DEPTH, RWKV_WIDTH), 0.02),
        "rwkv_k_a": gain(14, (DEPTH, RWKV_WIDTH)),
        "rwkv_r_k": nrm(15, (DEPTH, N_RWKV_HEADS, HEAD_DIM), 0.1),
        "rwkv_lnx_w": gain(16, (DEPTH, RWKV_WIDTH)),
        "rwkv_lnx_b": nrm(17, (DEPTH, RWKV_WIDTH), 0.01),
        "w_out": nrm(18, (DEPTH, D_MODEL, D_MODEL), D_MODEL ** -0.5),
        "norm_ffn": gain(19, (DEPTH, D_MODEL)),
        "peer_wq": nrm(20, (DEPTH, D_MODEL, PEER_HEADS * 2 * PEER_HALF), D_MODEL ** -0.5),
        "peer_keys": nrm(21, (DEPTH, 2, N_SUBKEYS, PEER_HALF), PEER_HALF ** -0.5),
        "peer_u": nrm(22, (DEPTH, N_EXPERTS, D_MODEL), D_MODEL ** -0.5),
        "peer_v": nrm(23, (DEPTH, N_EXPERTS, D_MODEL), PEER_HEADS ** -0.5),
        "norm_ple": gain(24, (DEPTH, D_MODEL)),
        "ple_proj": nrm(25, (DEPTH, PLE_DIM, D_MODEL), PLE_DIM ** -0.5),
        "ple_gate": nrm(26, (DEPTH, D_MODEL, D_MODEL), D_MODEL ** -0.5),
        "norm_final": gain(27, (D_MODEL,)),
    }

def reference(x, p, norm_mix, w_in, b_in, attn_sinks, attn_out_norm, rwkv_mu, rwkv_w0, rwkv_w_up,
              rwkv_a0, rwkv_a_up, rwkv_g_up, rwkv_k_k, rwkv_k_a, rwkv_r_k, rwkv_lnx_w, rwkv_lnx_b,
              w_out, norm_ffn, peer_wq, peer_keys, peer_u, peer_v, norm_ple, ple_proj, ple_gate,
              norm_final):
    for i in range(DEPTH):
        h = _rmsnorm(x, norm_mix[i])
        f = h @ w_in[i] + b_in[i]
        attn = _swa_sink_attention(f[..., OFF_Q:OFF_K], f[..., OFF_K:OFF_V], f[..., OFF_V:OFF_RWKV],
                                   attn_sinks[i])
        attn = _rmsnorm(attn, attn_out_norm[i])
        rw = _rwkv7_mix(f[..., OFF_RWKV:], rwkv_mu[i], rwkv_w0[i], rwkv_w_up[i], rwkv_a0[i],
                        rwkv_a_up[i], rwkv_g_up[i], rwkv_k_k[i], rwkv_k_a[i], rwkv_r_k[i],
                        rwkv_lnx_w[i], rwkv_lnx_b[i])
        x = x + jnp.concatenate([attn, rw], axis=-1) @ w_out[i]
        x = x + _peer(_rmsnorm(x, norm_ffn[i]), peer_wq[i], peer_keys[i], peer_u[i], peer_v[i])
        gate = jax.nn.sigmoid(_rmsnorm(x, norm_ple[i]) @ ple_gate[i])
        x = x + (p[i] @ ple_proj[i]) * gate
    return _rmsnorm(x, norm_final)


_drawn_inputs = setup_inputs


def setup_inputs(seed=0):
    import zlib

    import numpy as np

    out = dict(_drawn_inputs(seed))
    spreads = {}
    factors = {'rwkv_k_k': 20.391,
     'rwkv_k_a': 2.968,
     'rwkv_lnx_w': 3.107,
     'rwkv_lnx_b': 4.087,
     'norm_ple': 28.724,
     'norm_final': 9.775}
    for name, (base, spread) in spreads.items():
        noise = np.random.default_rng([zlib.crc32(name.encode()), seed]).standard_normal(out[name].shape)
        drawn = base * np.exp(spread * noise) if base else spread * noise
        out[name] = jnp.asarray(drawn.astype(out[name].dtype))
    for name, factor in factors.items():
        out[name] = (out[name] * factor).astype(out[name].dtype)
    return out
```

```python
from contextlib import ExitStack

import numpy as np

import concourse.bass as bass
from concourse import mybir

F32 = mybir.dt.float32
F32R = mybir.dt.float32r
U32 = mybir.dt.uint32
ALU = mybir.AluOpType
ACT = mybir.ActivationFunctionType
AX = mybir.AxisListType

P = 128
DEPTH, SEQ, D = 2, 256, 1024
TB = SEQ // P
KT = D // P
CHUNK, HD, NH, NKV = 64, 64, 8, 2
NCHUNK = SEQ // CHUNK
EPS, LNX_EPS = 1e-6, 64e-5
EXP_MINUS_HALF = float(np.exp(-0.5))
SLOPES = [float(2.0 ** (-8.0 * (h + 1) / NH)) for h in range(NH)]

RW_TILES, IN_TILES = 15, 21
T_LORA, T_GATE, T_Q, T_K, T_V = 12, 13, 15, 19, 20

PH, TOPK, NSUB = 8, 16, 128
HC = 2 * PH
SLOTS = PH * TOPK
HALVES = 2
I2H = NSUB // HALVES
GROUP = 8
NGROUPS = SEQ // GROUP

RING, SLABW = 4, 2048
S_IN, S_LORA, S_OUT, S_WQ, S_PEER, S_GATE, S_PLE, S_ALL = 0, 11, 12, 16, 24, 152, 156, 160
N_PROJ_SLABS = 29

C_GMIX, C_GFFN, C_GPLE, C_BIN, C_MU = 0, 8, 16, 24, 45
C_W0, C_A0, C_KK, C_KA, C_RK, C_LNW, C_LNB, C_AN, C_SINK, C_KEYS = 60, 64, 68, 72, 76, 80, 84, 88, 92, 100
NVEC = C_KEYS + 2 * NSUB
K_ID, K_ONES, K_PMASK, K_LMASK, K_RESET, K_DIST0, K_DIST1, K_IOTA, K_IOTA16 = 0, 128, 256, 512, 1280, 1536, 1664, 1920, 2048
NCONST = 2064
LEVELS = 6


def fills(layer, n):
    per_layer = S_ALL // RING - (1 if n % RING else 0)
    return layer * per_layer + n // RING + 1


def hybrid_encoder(nc, x, w_slabs, peer_slabs, vecs, consts, p_t, g_final, out):
    with ExitStack() as ctx:
        def sem(name):
            return ctx.enter_context(nc.semaphore(name))

        first = (nc.sbuf_base + 31) // 32 * 8

        def place(name, at, shape, dt=F32):
            return nc.alloc_sbuf_tensor_at(name, [P] + shape, dt, offset=4 * (first + at))

        xres = place("xres", 0, [TB, D])
        hT = place("hT", 2048, [KT, SEQ])
        ring = place("ring", 4096, [RING, SLABW])
        cst = place("cst", 12288, [NCONST])
        vec = place("vec", 14352, [DEPTH, NVEC])
        pT = place("pT", 15072, [DEPTH, 2, SEQ])
        stat = place("stat", 16096, [256])
        R = 16384
        xn = place("xn", R + 34304, [TB, D])
        obuf = place("obuf", R, [TB, D])
        gfin = place("gfin", R + 2048, [D])
        fpad = place("fpad", R + 10240, [RW_TILES, SEQ + 1])
        fm = place("fm", R + 14096, [RW_TILES, SEQ])
        prods = place("prods", R + 10240, [TB * NH, 512])
        sw = place("sw", R, [4, SEQ])
        csum = place("csum", R + 1024, [4, SEQ])
        cprev = place("cprev", R + 2048, [4, SEQ])
        winv = place("winv", R + 3072, [4, SEQ])
        wprev = place("wprev", R + 4096, [4, SEQ])
        kk = place("kk", R + 5120, [4, SEQ])
        sqk = place("sqk", R + 6144, [4, SEQ])
        kmod = place("kmod", R + 6144, [4, SEQ])
        rnorm = place("rnorm", R + 7168, [4, SEQ])
        bvec = place("bvec", R + 8192, [4, SEQ])
        rkprod = place("rkprod", R + 9216, [4, SEQ])
        Mt = place("Mt", R, [2, TB * NH, P])
        X = place("X", R + 4096, [TB * NH, P])
        XT = place("XT", R + 6144, [TB * NH, P])
        PX = place("PX", R + 8192, [TB * NH, P])
        ytok = place("ytok", R, [TB, 512])
        rhs = place("rhs", R + 1024, [512])
        sa = place("sa", R + 1536, [512])
        ST = place("ST", R + 2048, [2, 4, P])
        yc = place("yc", R + 3072, [TB, 512])
        ysq = place("ysq", R + 4096, [TB, 512])
        ytmp = place("ytmp", R + 8192, [4, SEQ])
        lg0 = place("lg0", R, [NH, P])
        lg1 = place("lg1", R + 1024, [NH, 2 * P])
        PT0 = place("PT0", R + 3072, [NH, P])
        PT1 = place("PT1", R + 4096, [NH, 2, P])
        wcum = place("wcum", R + 18432, [4, SEQ])
        ar = place("ar", R + 19456, [4, TB, 2, P])
        bt = place("bt", R + 21504, [4, SEQ])
        kt = place("kt", R + 22528, [4, SEQ])
        vtok = place("vtok", R + 23552, [TB, 512])
        btok = place("btok", R + 24576, [TB, 512])
        ktok = place("ktok", R + 25600, [TB, 512])
        avec = place("avec", R + 25600, [4, SEQ])
        bonus_v = place("bonus_v", R + 26624, [4, SEQ])
        gT = place("gT", R + 27648, [4, SEQ])
        aT = place("aT", R + 28672, [6, SEQ])
        vtA = place("vtA", R + 30208, [TB, P])
        ao = place("ao", R + 30464, [TB, 512])
        xw_t = place("xw_t", R + 31488, [SEQ])
        xg_s = place("xg_s", R + 31744, [2, SEQ])
        qT = place("qT", R, [HC, SEQ])
        sc = place("sc", R + 4096, [TB, HC, NSUB])
        topv = place("topv", R + 8192, [HC, TOPK])
        topi = place("topi", R + 8448, [HC, TOPK], U32)
        topf = place("topf", R + 8704, [HC, TOPK])
        cand = place("cand", R + 8960, [PH, TOPK * TOPK])
        bestv = place("bestv", R + 11008, [PH, TOPK])
        bestc = place("bestc", R + 11136, [PH, TOPK], U32)
        bestd = place("bestd", R + 11264, [2, PH * TOPK], U32)
        bestf = place("bestf", R + 11520, [2, PH, TOPK])
        onehot = place("onehot", R + 11776, [PH, TOPK, TOPK])
        picked = place("picked", R + 13824, [PH, TOPK, TOPK])
        slot = place("slot", R + 15872, [3, TB, SLOTS])
        G = place("G", R, [I2H, SEQ])
        UH = place("UH", R + 16384, [2, D], F32R)
        UL = place("UL", R + 18432, [2, D], F32R)
        VH = place("VH", R + 20480, [2, D], F32R)
        VL = place("VL", R + 22528, [2, D], F32R)
        ga = place("ga", R + 24576, [2, SEQ])
        Wt = place("Wt", R + 25088, [2, SEQ])
        WH = place("WH", R + 25600, [2, SEQ], F32R)
        WL = place("WL", R + 26112, [2, SEQ], F32R)
        hot1 = place("hot1", R + 26624, [GROUP, NSUB])
        hot2 = place("hot2", R + 27648, [GROUP, I2H])
        sT = place("sT", R + 28160, [3, SEQ])
        hTh = place("hTh", R + 28928, [KT, SEQ], F32R)
        hTl = place("hTl", R + 30976, [KT, SEQ], F32R)
        zeros = place("zeros", R + 33280, [512])
        sgm = place("sgm", R, [TB, D])
        ptmp = place("ptmp", R + 2048, [TB, D])

        PS = ctx.enter_context(nc.psum_tensor("PS", [P, 8, 512], F32))

        ident = cst[:, K_ID:K_ID + P]
        ones2 = cst[:, K_ONES:K_ONES + P]
        iota = cst[:, K_IOTA:K_IOTA + NSUB]
        iota16 = cst[:, K_IOTA16:K_IOTA16 + TOPK]
        ssq, rstd = stat[:, 0:2], stat[:, 2:4]
        amax, anm, arow, asink, aden = (stat[:, 8 + 16 * i:24 + 16 * i] for i in range(5))
        gmean, gvar = stat[:, 96:112], stat[:, 112:128]
        assq, arstd = stat[:, 128:130], stat[:, 130:132]
        gsum = stat[:, 136:144]
        bq8 = stat[:, 144:148]
        junk = PS

        in_x, in_c, in_v, in_p, in_g = (sem(n) for n in ("in_x", "in_c", "in_v", "in_p", "in_g"))
        filled = [sem(f"filled{i}") for i in range(RING)]
        slab_used = sem("slab_used")
        zeros_made = sem("zeros_made")
        sumsq, mean_sq, rms, xn_ready, xT_ps, hT_act, hT_dve = (
            sem(n) for n in ("sumsq", "mean_sq", "rms", "xn_ready", "xT_ps", "hT_act", "hT_dve"))
        x_ready = sem("x_ready")
        bq_ready, in_ps, in_evac, mixed = (sem(n) for n in ("bq_ready", "in_ps", "in_evac", "mixed"))
        vtA_ps, vtA_ready, sc_ps, nm_ready, p_ready = (sem(n) for n in ("vtA_ps", "vtA_ready", "sc_ps", "nm_ready", "p_ready"))
        pT_ps, pT_ready, pv_ps, ao_ready, ao_ssq, ao_ms, ao_rms, ao_normed, aoT_ps, yTa_ready = (
            sem(n) for n in ("pT_ps", "pT_ready", "pv_ps", "ao_ready", "ao_ssq", "ao_ms", "ao_rms", "ao_normed", "aoT_ps", "yTa_ready"))
        lora_in, lora_ps, gates_ready, g_ready = (sem(n) for n in ("lora_in", "lora_ps", "gates_ready", "g_ready"))
        sqk_ready, kss_ps, kss_max, knorm, csum_ready, decay_ready = (
            sem(n) for n in ("sqk_ready", "kss_ps", "kss_max", "knorm", "csum_ready", "decay_ready"))
        rk_ready, bonus_ps, bonus_ready, bkt_ready, tok_ps, tok_ready = (
            sem(n) for n in ("rk_ready", "bonus_ps", "bonus_ready", "bkt_ready", "tok_ps", "tok_ready"))
        prod_ps, prod_ready, mt_ready, m_ps, xm_ready, px_ready, xp_ps, xpt_ps = (
            sem(n) for n in ("prod_ps", "prod_ready", "mt_ready", "m_ps", "xm_ready", "px_ready", "xp_ps", "xpt_ps"))
        rhs_ps, rhs_ready, sa_ps, sa_ready, y_ps, y_ready, st_ps, st_ready = (
            sem(n) for n in ("rhs_ps", "rhs_ready", "sa_ps", "sa_ready", "y_ps", "y_ready", "st_ps", "st_ready"))
        yc_ready, ysq_ready, yv_ready, ystd, yn_ready, yT_ps, yTr_ready, op_ps = (
            sem(n) for n in ("yc_ready", "ysq_ready", "yv_ready", "ystd", "yn_ready", "yT_ps", "yTr_ready", "op_ps"))
        q_ps, q_ready, psc_ps, psc_ready = (sem(n) for n in ("q_ps", "q_ready", "psc_ps", "psc_ready"))
        bd_ready, bexp_ready, slot_ready, slot_ps, slot_T = (sem(n) for n in ("bd_ready", "bexp_ready", "slot_ready", "slot_ps", "slot_T"))
        hTh_ready, hTl_ready = sem("hTh_ready"), sem("hTl_ready")
        hot_made, g_ps, g_evac = sem("hot_made"), sem("g_ps"), sem("g_evac")
        u_hi, u_lo, v_hi, v_lo = (sem(n) for n in ("u_hi", "u_lo", "v_hi", "v_lo"))
        a_ps, ga_ready, w_made, w_hi, w_ready, v_used, peer_ps = (
            sem(n) for n in ("a_ps", "ga_ready", "w_made", "w_hi", "w_ready", "v_used", "peer_ps"))
        gate_ps, ple_ps, sgm_ready, ple_sum = (sem(n) for n in ("gate_ps", "ple_ps", "sgm_ready", "ple_sum"))
        out_ready, out_done = sem("out_ready"), sem("out_done")
        dve_step, act_step, pool_step = sem("dve_step"), sem("act_step"), sem("pool_step")

        block = ctx.enter_context(nc.Block())

        def full(layer, n):
            return ring[:, n % RING, :]

        @block.sync
        def _(sp):
            sp.dma_start(xres[:], x).then_inc(in_x, 16)
            sp.dma_start(cst[:], consts).then_inc(in_c, 16)
            sp.dma_start(vec[:], vecs).then_inc(in_v, 16)

            def load(layer, n, src):
                sp.dma_start(full(layer, n), src).then_inc(filled[n % RING], 16)

            for L in range(DEPTH):
                for n in list(range(S_PEER)):
                    if L or n >= RING:
                        before = n - RING if n >= RING else S_ALL + n - RING
                        used = before if n >= RING else (S_PEER + (before - S_GATE) if before <= S_PLE else S_PEER + (before - RING - S_GATE))
                        sp.wait_ge(slab_used, N_PROJ_SLABS * (L if n >= RING else L - 1) + used + 1)
                    load(L, n, w_slabs[L, n])
                    if L == 0 and n == RING - 1:
                        sp.dma_start(pT[:], p_t).then_inc(in_p, 16)
                for e in range(RING):
                    sp.wait_ge(slab_used, N_PROJ_SLABS * L + S_PEER - RING + e + 1)
                    load(L, S_PEER + e, peer_slabs[L, e])
                with sp.Fori(0, NSUB // RING - 1) as i:
                    for j in range(RING):
                        sp.wait_ge(v_lo, NSUB * L + 4 * i + j + 1)
                        sp.dma_start(ring[:, j, :], peer_slabs[L, 4 * i + (RING + j)]).then_inc(filled[j], 16)
                for n in range(S_GATE, S_PLE + 1):
                    if n < S_PLE:
                        sp.wait_ge(v_lo, NSUB * L + n - RING - S_PEER + 1)
                    else:
                        sp.wait_ge(slab_used, N_PROJ_SLABS * L + S_PEER + 1)
                    load(L, n, w_slabs[L, S_PEER + n - S_GATE])
            sp.wait_ge(ple_sum, DEPTH)
            sp.dma_start(gfin[:], g_final).then_inc(in_g, 16)
            sp.wait_ge(out_ready, TB)
            sp.dma_start(out, obuf[:]).then_inc(out_done, 16)
            sp.wait_ge(out_done, 16)

        @block.gpsimd
        def _(pool):
            pool.memset(zeros[:], 0.0).then_inc(zeros_made, 1)
            pool.wait_ge(in_c, 16)
            for L in range(DEPTH):
                for lv in range(LEVELS):
                    pool.wait_ge(prod_ready, 16 * (L + 1))
                    if lv >= 2:
                        pool.wait_ge(m_ps, 4 * LEVELS * L + 4 * (lv - 1))
                        pool.wait_ge(xm_ready, 4 * LEVELS * L + 4 * (lv - 1))
                    mask = cst[:, K_LMASK + lv * P:K_LMASK + (lv + 1) * P].unsqueeze(1).broadcast_to([P, 16, P])
                    pool.tensor_tensor(Mt[:, lv % 2], prods[:, :, 0:P], mask, ALU.mult).then_inc(mt_ready, 1)

        @block.scalar
        def _(act):
            steps = [0]

            def link(ins):
                steps[0] += 1
                ins.then_inc(act_step, 1)
                act.wait_ge(act_step, steps[0])

            def norm(r, xs_ready, gain):
                act.wait_ge(x_ready, xs_ready) if xs_ready else act.wait_ge(in_x, 16)
                for tb in range(TB):
                    act.activation(xn[:, tb], xres[:, tb], ACT.Square, accum_out=ssq[:, tb:tb + 1]).then_inc(sumsq, 1)
                act.wait_ge(mean_sq, r + 1)
                act.activation(rstd, ssq, ACT.Sqrt).then_inc(rms, 1)
                if gain is None:
                    return
                for k in (0, 1, 4, 5):
                    act.wait_ge(xT_ps, 4 * r + k // 2 + 1)
                    act.activation(hT[:, k], PS[:, k // 2, (k % 2) * SEQ:(k % 2 + 1) * SEQ], ACT.Identity, scale=gain[:, k:k + 1]).then_inc(hT_act, 1)

            act.wait_ge(in_v, 16)
            for L in range(DEPTH):
                V = vec[:, L]
                norm(3 * L, 3 * L, V[:, C_GMIX:C_GMIX + KT])
                for m in range(IN_TILES):
                    act.wait_ge(in_ps, IN_TILES * L + m + 1)
                    src = PS[:, 4 + m % 4, 0:SEQ]
                    if m == 0 and L:
                        act.wait_ge(ple_sum, L)
                    if m < RW_TILES:
                        act.activation(fpad[:, m, 1:SEQ + 1], src, ACT.Identity, bias=V[:, C_BIN + m:C_BIN + m + 1]).then_inc(in_evac, 1)
                    elif m < T_K:
                        if m == T_Q:
                            act.wait_ge(bq_ready, L + 1)
                        act.activation(aT[:, m - T_Q], src, ACT.Identity, bias=bq8[:, m - T_Q:m - T_Q + 1], scale=HD ** -0.5).then_inc(in_evac, 1)
                    else:
                        act.activation(aT[:, m - T_Q], src, ACT.Identity, bias=V[:, C_BIN + m:C_BIN + m + 1]).then_inc(in_evac, 1)
                act.wait_ge(vtA_ps, L + 1)
                act.copy(vtA[:], PS[:, 0, 0:TB * P]).then_inc(vtA_ready, 1)
                for tb in range(TB):
                    act.wait_ge(nm_ready, TB * L + tb + 1)
                    lg = lg1 if tb else lg0
                    for h in range(NH):
                        c = tb * NH + h
                        act.activation(lg[:, h], lg[:, h], ACT.Exp, bias=anm[:, c:c + 1], accum_out=arow[:, c:c + 1])
                    act.activation(asink[:, tb * NH:(tb + 1) * NH], asink[:, tb * NH:(tb + 1) * NH], ACT.Exp).then_inc(p_ready, 1)
                for n in range(6):
                    act.wait_ge(pT_ps, 6 * L + n + 1)
                    if n < 2:
                        act.copy(PT0[:, 4 * n:4 * n + 4], PS[:, 1 + n].rearrange("p (a b) -> p a b", a=4)).then_inc(pT_ready, 1)
                    else:
                        act.copy(PT1[:, 2 * (n - 2):2 * (n - 1)], PS[:, 2 + n].rearrange("p (a c b) -> p a c b", a=2, c=2)).then_inc(pT_ready, 1)
                act.wait_ge(ao_ready, TB * (L + 1))
                for tb in range(TB):
                    act.activation(PS[:, 6 + tb], ao[:, tb], ACT.Square, accum_out=assq[:, tb:tb + 1]).then_inc(ao_ssq, 1)
                act.wait_ge(ao_ms, L + 1)
                act.activation(arstd, assq, ACT.Sqrt).then_inc(ao_rms, 1)
                act.wait_ge(mixed, L + 1)
                act.activation(xw_t[0:64], fm[0:64, T_LORA], ACT.Tanh).then_inc(lora_in, 1)
                act.activation(xg_s[:, :, :], fm[:, T_GATE:T_GATE + 2], ACT.Sigmoid).then_inc(lora_in, 1)
                act.wait_ge(lora_ps, 3 * L + 1)
                act.wait_ge(yTa_ready, L + 1)
                for t in range(4):
                    ins = act.activation(sw[:, t], PS[:, t // 2, (t % 2) * SEQ:(t % 2 + 1) * SEQ], ACT.Sigmoid, bias=V[:, C_W0 + t:C_W0 + t + 1])
                ins.then_inc(gates_ready, 1)
                act.wait_ge(lora_ps, 3 * L + 2)
                for t in range(4):
                    ins = act.activation(avec[:, t], PS[:, 2 + t // 2, (t % 2) * SEQ:(t % 2 + 1) * SEQ], ACT.Sigmoid, bias=V[:, C_A0 + t:C_A0 + t + 1])
                ins.then_inc(gates_ready, 1)
                act.wait_ge(lora_ps, 3 * L + 3)
                act.copy(gT[:], PS[:, 4:6].rearrange("p a (b c) -> p (a b) c", b=2)).then_inc(g_ready, 1)
                act.wait_ge(kss_max, L + 1)
                act.activation(rnorm[:], rnorm[:], ACT.Sqrt).then_inc(knorm, 1)
                act.wait_ge(csum_ready, 2 * L + 1)
                act.activation(wcum[:], csum[:], ACT.Exp, scale=-EXP_MINUS_HALF).then_inc(decay_ready, 1)
                act.activation(winv[:], csum[:], ACT.Exp, scale=EXP_MINUS_HALF).then_inc(decay_ready, 1)
                act.wait_ge(csum_ready, 2 * L + 2)
                act.activation(wprev[:], cprev[:], ACT.Exp, scale=-EXP_MINUS_HALF).then_inc(decay_ready, 1)
                for n, dst in enumerate((vtok, btok, ktok)):
                    act.wait_ge(tok_ps, 3 * L + n + 1)
                    act.copy(dst[:], PS[:, 2 * n:2 * n + 2]).then_inc(tok_ready, 1)
                for lv in range(1, LEVELS):
                    for g in range(4):
                        act.wait_ge(m_ps, 4 * (LEVELS * L + lv) + g + 1)
                        act.copy(PX[:, 4 * g:4 * g + 4], PS[:, g].rearrange("p (a b) -> p a b", a=4)).then_inc(px_ready, 1)
                for c in range(NCHUNK):
                    o = 64 * (c % 2)
                    act.wait_ge(sa_ps, NCHUNK * L + c + 1)
                    act.copy(sa[o:o + 64], PS[o:o + 64, 1]).then_inc(sa_ready, 1)
                    act.wait_ge(y_ps, NCHUNK * L + c + 1)
                    act.copy(ytok[o:o + 64, c // 2], PS[o:o + 64, 2]).then_inc(y_ready, 1)
                act.wait_ge(yc_ready, L + 1)
                act.activation(ysq[:], yc[:], ACT.Square).then_inc(ysq_ready, 1)
                act.wait_ge(yv_ready, L + 1)
                act.activation(gvar, gvar, ACT.Sqrt).then_inc(ystd, 1)
                norm(3 * L + 1, 3 * L + 1, V[:, C_GFFN:C_GFFN + KT])
                act.wait_ge(hT_dve, 4 * (3 * L + 2))
                act.wait_ge(hT_act, 4 * (3 * L + 2))
                act.copy(hTh[:], hT[:]).then_inc(hTh_ready, 1)
                for m in range(HC):
                    act.wait_ge(q_ps, HC * L + m + 1)
                    act.copy(qT[:, m], PS[:, 4 + m % 4, 0:SEQ]).then_inc(q_ready, 1)
                for n in range(8):
                    act.wait_ge(psc_ps, 8 * L + n + 1)
                    act.copy(sc[:, n // 4, 4 * (n % 4):4 * (n % 4) + 4], PS[:, n].rearrange("p (a b) -> p a b", a=4)).then_inc(psc_ready, 1)
                for tb in range(TB):
                    act.wait_ge(bd_ready, TB * L + tb + 1)
                    act.activation(slot[:, 2, tb], slot[:, 2, tb], ACT.Exp).then_inc(bexp_ready, 1)
                act.wait_ge(slot_ps, L + 1)
                act.copy(sT[:, 0:2], PS[:, 0].rearrange("p (a b) -> p a b", a=2))
                act.copy(sT[:, 2], PS[:, 1, 0:SEQ]).then_inc(slot_T, 1)
                for half in range(HALVES):
                    g0 = NGROUPS * (HALVES * L + half)

                    def evacuate(group, bank):
                        act.wait_ge(g_ps, GROUP * (g0 + 1) + GROUP * group)
                        act.copy(G[:, :, bass.ds(GROUP * group, GROUP)],
                                 PS[:, bank].rearrange("p (t i) -> p i t", t=GROUP)).then_inc(g_evac, 1)

                    if half:
                        act.wait_ge(w_made, NSUB * L + I2H)
                    with act.Fori(0, NGROUPS // 2) as i:
                        for b in range(2):
                            evacuate(2 * i + b, 4 + b)
                    e0 = NSUB * L + I2H * half
                    f0 = (S_PEER + I2H * half) // RING

                    def split_u(e, j):
                        act.wait_ge(filled[j % RING], 16 * (fills(L, S_PEER + j % RING) + I2H * half // RING) + (e - j % RING) * (16 // RING))
                        act.copy(UH[:, j % 2], ring[:, j % RING, 0:D]).then_inc(u_hi, 1)

                    def split_v(j):
                        act.copy(VH[:, j % 2], ring[:, j % RING, D:2 * D]).then_inc(v_hi, 1)

                    def step(e, j, more_u=True, more_v=True):
                        act.wait_ge(a_ps, e0 + 1 + e)
                        act.activation(ga[:, j % 2], PS[:, 6 + j % 2, 0:SEQ], ACT.Gelu).then_inc(ga_ready, 1)
                        if more_u:
                            split_u(e + 2, j + 2)
                        if more_v:
                            act.wait_ge(v_used, e0 + e) if L or half or not isinstance(e, int) or e else None
                            split_v(j + 1)

                    if e0:
                        act.wait_ge(v_used, e0)
                    act.wait_ge(g_evac, g0 + NGROUPS)
                    split_u(0, 0)
                    split_u(1, 1)
                    split_v(0)
                    step(0, 0)
                    step(1, 1)
                    step(2, 2)
                    step(3, 3)
                    with act.Fori(1, I2H // RING - 1) as i:
                        for j in range(RING):
                            step(RING * i + j, j)
                    for j in range(RING):
                        step(I2H - RING + j, j, j < 2, j < 3)
                norm(3 * L + 2, 3 * L + 2, V[:, C_GPLE:C_GPLE + KT])
                act.wait_ge(gate_ps, L + 1)
                for n in range(4):
                    act.activation(sgm[:, n // 2, (n % 2) * 512:(n % 2 + 1) * 512], PS[:, n], ACT.Sigmoid).then_inc(sgm_ready, 1)
            norm(3 * DEPTH, 3 * DEPTH, None)

        @block.vector
        def _(dve):
            steps = [0]

            def link(ins):
                steps[0] += 1
                ins.then_inc(dve_step, 1)
                dve.wait_ge(dve_step, steps[0])

            def mean_square(r):
                dve.wait_ge(sumsq, TB * (r + 1))
                dve.tensor_scalar(ssq, ssq, 1.0 / D, EPS, ALU.mult, ALU.add).then_inc(mean_sq, 1)
                dve.wait_ge(rms, r + 1)
                link(dve.reciprocal(rstd, rstd))

            def norm(r, gain):
                mean_square(r)
                for tb in range(TB):
                    dve.tensor_scalar(xn[:, tb], xres[:, tb], rstd[:, tb:tb + 1], None, ALU.mult).then_inc(xn_ready, 1)
                for k in (2, 3, 6, 7):
                    dve.wait_ge(xT_ps, 4 * r + k // 2 + 1)
                    dve.tensor_scalar(hT[:, k], PS[:, k // 2, (k % 2) * SEQ:(k % 2 + 1) * SEQ], gain[:, k:k + 1], None, ALU.mult).then_inc(hT_dve, 1)

            def bc(col, n):
                return col.unsqueeze(2).broadcast_to([P, col.shape[1], n])

            dve.wait_ge(in_x, 16)
            dve.wait_ge(in_v, 16)
            dve.wait_ge(in_c, 16)
            for L in range(DEPTH):
                V = vec[:, L]
                norm(3 * L, V[:, C_GMIX:C_GMIX + KT])
                dve.tensor_scalar(bq8, V[:, C_BIN + T_Q:C_BIN + T_K], HD ** -0.5, None, ALU.mult).then_inc(bq_ready, 1)
                dve.memset(fpad[:, :, 0:1], 0.0).then_inc(dve_step, 1)
                steps[0] += 1
                dve.wait_ge(dve_step, steps[0])
                for m in range(RW_TILES):
                    dve.wait_ge(in_evac, IN_TILES * L + m + 1)
                    link(dve.tensor_tensor(fm[:, m], fpad[:, m, 0:SEQ], fpad[:, m, 1:SEQ + 1], ALU.subtract))
                    ins = dve.scalar_tensor_tensor(fm[:, m], fm[:, m], V[:, C_MU + m:C_MU + m + 1], fpad[:, m, 1:SEQ + 1], ALU.mult, ALU.add)
                ins.then_inc(mixed, 1)
                sinks = V[:, C_SINK:C_SINK + NH]
                for tb in range(TB):
                    dve.wait_ge(sc_ps, TB * L + tb + 1)
                    nk = P * (tb + 1)
                    lg = lg1 if tb else lg0
                    dist = cst[:, K_DIST1:K_DIST1 + nk] if tb else cst[:, K_DIST0:K_DIST0 + nk]
                    for h in range(NH):
                        bank = 4 + h // 2 if tb else 1 + h // 4
                        at = (h % 2) * 2 * P if tb else (h % 4) * P
                        ins = dve.scalar_tensor_tensor(lg[:, h], dist, -SLOPES[h], PS[:, bank, at:at + nk], ALU.mult, ALU.add)
                    link(ins)
                    c = slice(tb * NH, (tb + 1) * NH)
                    link(dve.tensor_reduce(amax[:, c], lg[:], AX.X, ALU.max))
                    link(dve.tensor_tensor(amax[:, c], amax[:, c], sinks, ALU.max))
                    dve.tensor_scalar(anm[:, c], amax[:, c], -1.0, None, ALU.mult)
                    dve.tensor_tensor(asink[:, c], sinks, amax[:, c], ALU.subtract).then_inc(nm_ready, 1)
                for tb in range(TB):
                    c = slice(tb * NH, (tb + 1) * NH)
                    dve.wait_ge(p_ready, TB * L + tb + 1)
                    link(dve.tensor_tensor(aden[:, c], arow[:, c], asink[:, c], ALU.add))
                    link(dve.reciprocal(aden[:, c], aden[:, c]))
                    dve.wait_ge(pv_ps, TB * L + tb + 1)
                    dve.tensor_tensor(ao[:, tb].rearrange("p (h d) -> p h d", h=NH),
                                      PS[:, 0 if tb else 3].rearrange("p (h d) -> p h d", h=NH),
                                      bc(aden[:, c], HD), ALU.mult).then_inc(ao_ready, 1)
                dve.wait_ge(ao_ssq, TB * (L + 1))
                dve.tensor_scalar(assq, assq, 1.0 / 512, EPS, ALU.mult, ALU.add).then_inc(ao_ms, 1)
                dve.wait_ge(ao_rms, L + 1)
                link(dve.reciprocal(arstd, arstd))
                for tb in range(TB):
                    ins = dve.tensor_scalar(ao[:, tb], ao[:, tb], arstd[:, tb:tb + 1], None, ALU.mult)
                ins.then_inc(ao_normed, 1)
                for k in range(4):
                    dve.wait_ge(aoT_ps, 2 * L + k // 2 + 1)
                    ins = dve.tensor_scalar(hT[:, k], PS[:, 4 + k // 2, (k % 2) * SEQ:(k % 2 + 1) * SEQ], V[:, C_AN + k:C_AN + k + 1], None, ALU.mult)
                ins.then_inc(yTa_ready, 1)
                for t in range(4):
                    ins = dve.tensor_scalar(kk[:, t], fm[:, 4 + t], V[:, C_KK + t:C_KK + t + 1], None, ALU.mult)
                link(ins)
                dve.tensor_tensor(sqk[:], kk[:], kk[:], ALU.mult).then_inc(sqk_ready, 1)
                dve.wait_ge(gates_ready, 2 * L + 1)
                for t in range(4):
                    ins = dve.tensor_tensor_scan(csum[:, t], cst[:, K_RESET:K_RESET + SEQ], sw[:, t], 0.0, ALU.mult, ALU.add)
                ins.then_inc(csum_ready, 1)
                dve.wait_ge(csum_ready, 2 * L + 1)
                dve.tensor_tensor(cprev[:], csum[:], sw[:], ALU.subtract).then_inc(csum_ready, 1)
                dve.wait_ge(kss_ps, L + 1)
                dve.tensor_scalar(rnorm[:], PS[:, 6:8].rearrange("p a (b c) -> p (a b) c", b=2), 1e-24, None, ALU.max).then_inc(kss_max, 1)
                dve.wait_ge(gates_ready, 2 * L + 2)
                for t in range(4):
                    ins = dve.tensor_scalar(kmod[:, t], avec[:, t], 1.0, V[:, C_KA + t:C_KA + t + 1], ALU.subtract, ALU.mult)
                link(ins)
                link(dve.scalar_tensor_tensor(kmod[:], kmod[:], 1.0, fm[:, 4:8], ALU.add, ALU.mult))
                for t in range(4):
                    ins = dve.scalar_tensor_tensor(rkprod[:, t], fm[:, t], V[:, C_RK + t:C_RK + t + 1], kmod[:, t], ALU.mult, ALU.mult)
                ins.then_inc(rk_ready, 1)
                dve.wait_ge(knorm, L + 1)
                link(dve.reciprocal(rnorm[:], rnorm[:]))
                link(dve.tensor_tensor(kk[:], kk[:], rnorm[:], ALU.mult))
                link(dve.tensor_tensor(bvec[:], kk[:], avec[:], ALU.mult))
                dve.wait_ge(decay_ready, 3 * (L + 1))
                v8 = lambda t: t[:].rearrange("p a (b c) -> p (a b) c", b=TB)
                dve.tensor_tensor(bt[:], bvec[:], winv[:], ALU.mult)
                dve.tensor_tensor(kt[:], kmod[:], winv[:], ALU.mult).then_inc(bkt_ready, 1)
                arv = ar[:].rearrange("p a b c d -> p (a b) c d")
                dve.scalar_tensor_tensor(arv[:, :, 0], v8(kk), -1.0, v8(wprev), ALU.mult, ALU.mult)
                dve.tensor_tensor(arv[:, :, 1], fm[:, 0:4].rearrange("p a (b c) -> p (a b) c", b=TB), v8(wcum), ALU.mult).then_inc(bkt_ready, 1)
                dve.wait_ge(bonus_ps, L + 1)
                dve.tensor_tensor(bonus_v[:], PS[:, 6:8].rearrange("p a (b c) -> p (a b) c", b=2), fm[:, 8:12], ALU.mult).then_inc(bonus_ready, 1)
                pm = cst[:, K_PMASK:K_PMASK + 256].unsqueeze(1).broadcast_to([P, 2, 256])
                for n in range(16):
                    dve.wait_ge(prod_ps, 16 * L + n + 1)
                    dve.tensor_tensor(prods[:, n].rearrange("p (a b) -> p a b", a=2),
                                      PS[:, 6 + n % 2].rearrange("p (a b) -> p a b", a=2), pm, ALU.mult).then_inc(prod_ready, 1)
                for lv in range(LEVELS):
                    for g in range(4):
                        gs = slice(4 * g, 4 * g + 4)
                        four = lambda a: a.rearrange("p (a b) -> p a b", a=4)
                        if lv == 0:
                            dve.wait_ge(m_ps, 4 * LEVELS * L + g + 1)
                            dve.wait_ge(mt_ready, LEVELS * L + 1)
                            eye = ident.unsqueeze(1).broadcast_to([P, 4, P])
                            dve.tensor_tensor(XT[:, gs], Mt[:, 0, gs], eye, ALU.add)
                            dve.tensor_tensor(X[:, gs], four(PS[:, g]), eye, ALU.add).then_inc(xm_ready, 1)
                            continue
                        dve.wait_ge(xpt_ps, 4 * ((LEVELS - 1) * L + lv - 1) + g + 1)
                        dve.wait_ge(xm_ready, 4 * (LEVELS * L + lv - 1) + g + 1)
                        if lv < LEVELS - 1:
                            dve.tensor_tensor(XT[:, gs], XT[:, gs], four(PS[:, g]), ALU.add)
                            dve.tensor_tensor(X[:, gs], X[:, gs], four(PS[:, 4 + g]), ALU.add).then_inc(xm_ready, 1)
                        else:
                            dve.tensor_tensor(XT[:, gs], XT[:, gs], four(PS[:, g]), ALU.add).then_inc(xm_ready, 1)
                dve.memset(rhs[:], 0.0)
                dve.memset(sa[:], 0.0)
                link(dve.memset(ST[:], 0.0))
                for c in range(NCHUNK):
                    o = 64 * (c % 2)
                    dve.wait_ge(rhs_ps, NCHUNK * L + c + 1)
                    dve.tensor_copy(rhs[o:o + 64], PS[o:o + 64, 0]).then_inc(rhs_ready, 1)
                    if c == NCHUNK - 1:
                        continue
                    dve.wait_ge(st_ps, (NCHUNK - 1) * L + c + 1)
                    for b in range(2):
                        hr = slice(64 * b, 64 * b + 64)
                        src = PS[hr, 3, 0:4 * HD].rearrange("p (a b) -> p a b", a=4)
                        wend = wcum[hr, :, 64 * c + 63:64 * c + 64].broadcast_to([64, 4, HD])
                        state = ST[hr, c % 2, :, hr]
                        if c:
                            link(dve.tensor_tensor(state, ST[hr, (c - 1) % 2, :, hr], src, ALU.add))
                            ins = dve.tensor_tensor(state, state, wend, ALU.mult)
                        else:
                            ins = dve.tensor_tensor(state, src, wend, ALU.mult)
                    ins.then_inc(st_ready, 1)
                dve.wait_ge(y_ready, NCHUNK * (L + 1))
                y16 = ytok[:].rearrange("p a (h d) -> p (a h) d", h=NH)
                yc16 = yc[:].rearrange("p a (h d) -> p (a h) d", h=NH)
                link(dve.tensor_reduce(gmean, y16, AX.X, ALU.add))
                link(dve.tensor_scalar(gmean, gmean, -1.0 / HD, None, ALU.mult))
                dve.tensor_tensor(yc16, y16, bc(gmean, HD), ALU.add).then_inc(yc_ready, 1)
                dve.wait_ge(ysq_ready, L + 1)
                link(dve.tensor_reduce(gvar, ysq[:].rearrange("p a (h d) -> p (a h) d", h=NH), AX.X, ALU.add))
                dve.tensor_scalar(gvar, gvar, 1.0 / HD, LNX_EPS, ALU.mult, ALU.add).then_inc(yv_ready, 1)
                dve.wait_ge(ystd, L + 1)
                link(dve.reciprocal(gvar, gvar))
                dve.tensor_tensor(yc16, yc16, bc(gvar, HD), ALU.mult).then_inc(yn_ready, 1)
                dve.wait_ge(yT_ps, L + 1)
                for t in range(4):
                    ins = dve.tensor_scalar(ytmp[:, t], PS[:, 4 + t // 2, (t % 2) * SEQ:(t % 2 + 1) * SEQ],
                                            V[:, C_LNW + t:C_LNW + t + 1], V[:, C_LNB + t:C_LNB + t + 1], ALU.mult, ALU.add)
                link(ins)
                link(dve.tensor_tensor(ytmp[:], ytmp[:], bonus_v[:], ALU.add))
                dve.wait_ge(g_ready, L + 1)
                dve.tensor_tensor(hT[:, 4:8], ytmp[:], gT[:], ALU.mult).then_inc(yTr_ready, 1)
                dve.wait_ge(op_ps, L + 1)
                for n in range(4):
                    s = slice((n % 2) * 512, (n % 2 + 1) * 512)
                    ins = dve.tensor_tensor(xres[:, n // 2, s], xres[:, n // 2, s], PS[:, n], ALU.add)
                ins.then_inc(x_ready, 1)
                dve.wait_ge(x_ready, 3 * L + 1)
                norm(3 * L + 1, V[:, C_GFFN:C_GFFN + KT])
                dve.wait_ge(hTh_ready, L + 1)
                dve.tensor_tensor(hTl[:], hT[:], hTh[:].bitcast(F32), ALU.subtract).then_inc(hTl_ready, 1)
                def top16(rows, n, values, vals, idx, scratch=None):
                    for r in range(rows):
                        ins = dve.max(vals[:, r, 0:8], values(r))
                    link(ins)
                    for r in range(rows):
                        dve.max_index(idx[:, r, 0:8], vals[:, r, 0:8], values(r))
                        ins = dve.match_replace(values(r), vals[:, r, 0:8], values(r), -3.0e38)
                    link(ins)
                    for r in range(rows):
                        ins = dve.max(vals[:, r, 8:16], values(r))
                    link(ins)
                    for r in range(rows):
                        ins = dve.max_index(idx[:, r, 8:16], vals[:, r, 8:16], values(r))
                    link(ins)

                for tb in range(TB):
                    dve.wait_ge(psc_ready, 8 * L + 4 * (tb + 1))
                    top16(HC, NSUB, lambda r: sc[:, tb, r], topv, topi)
                    link(dve.tensor_copy(topf[:], topi[:]))
                    tv = topv[:].rearrange("p (h c) k -> p h c k", c=2)
                    tf = topf[:].rearrange("p (h c) k -> p h c k", c=2)
                    link(dve.tensor_tensor(cand[:].rearrange("p h (a b) -> p h a b", a=TOPK),
                                           tv[:, :, 0].unsqueeze(3).broadcast_to([P, PH, TOPK, TOPK]),
                                           tv[:, :, 1].unsqueeze(2).broadcast_to([P, PH, TOPK, TOPK]), ALU.add))
                    top16(PH, TOPK * TOPK, lambda r: cand[:, r], bestv, bestc)
                    bflat = bestc[:].rearrange("p a b -> p (a b)")
                    dve.tensor_scalar(bestd[:, 0], bflat, 4, None, ALU.logical_shift_right)
                    link(dve.tensor_scalar(bestd[:, 1], bflat, 15, None, ALU.bitwise_and))
                    link(dve.tensor_copy(bestf[:].rearrange("p c a b -> p c (a b)"), bestd[:]))
                    for c in range(2):
                        link(dve.tensor_tensor(onehot[:], bestf[:, c].unsqueeze(3).broadcast_to([P, PH, TOPK, TOPK]),
                                               iota16.unsqueeze(1).unsqueeze(1).broadcast_to([P, PH, TOPK, TOPK]), ALU.is_equal))
                        link(dve.tensor_tensor(picked[:], onehot[:], tf[:, :, c].unsqueeze(2).broadcast_to([P, PH, TOPK, TOPK]), ALU.mult))
                        link(dve.tensor_reduce(slot[:, c, tb].rearrange("p (a b) -> p a b", a=PH), picked[:], AX.X, ALU.add))
                    s3 = slot[:, 2, tb].rearrange("p (a b) -> p a b", a=PH)
                    dve.tensor_tensor(s3, bestv[:], bestv[:, :, 0:1].broadcast_to([P, PH, TOPK]), ALU.subtract).then_inc(bd_ready, 1)
                    dve.wait_ge(bexp_ready, TB * L + tb + 1)
                    link(dve.tensor_reduce(gsum, s3, AX.X, ALU.add))
                    link(dve.reciprocal(gsum, gsum))
                    dve.tensor_tensor(s3, s3, bc(gsum, TOPK), ALU.mult).then_inc(slot_ready, 1)
                for half in range(HALVES):
                    t0 = SEQ * (HALVES * L + half)
                    dve.wait_ge(slot_T, L + 1)

                    def one_hots(t, j, wait=True):
                        if wait:
                            dve.wait_ge(g_ps, t0 - GROUP + 1 + t)
                        dve.tensor_scalar(hot1[:, j], iota, sT[:, 0, bass.ds(t, 1)], sT[:, 2, bass.ds(t, 1)], ALU.is_equal, ALU.mult)
                        dve.tensor_scalar(hot2[:, j], iota[:, I2H * half:I2H * (half + 1)], sT[:, 1, bass.ds(t, 1)], None, ALU.is_equal).then_inc(hot_made, 1)

                    for j in range(GROUP):
                        one_hots(j, j, bool(t0))
                    with dve.Fori(1, NGROUPS) as i:
                        for j in range(GROUP):
                            one_hots(GROUP * i + j, j)
                    e0 = NSUB * L + I2H * half

                    def split_u(e, j):
                        dve.wait_ge(u_hi, e0 + 1 + e)
                        dve.tensor_tensor(UL[:, j % 2], ring[:, j % RING, 0:D], UH[:, j % 2].bitcast(F32), ALU.subtract).then_inc(u_lo, 1)

                    def split_v(e, j):
                        dve.wait_ge(v_hi, e0 + 1 + e)
                        dve.tensor_tensor(VL[:, j % 2], ring[:, j % RING, D:2 * D], VH[:, j % 2].bitcast(F32), ALU.subtract).then_inc(v_lo, 1)

                    def step(e, j, more_u=True, more_v=True):
                        dve.wait_ge(ga_ready, e0 + 1 + e)
                        dve.wait_ge(v_used, e0 - 1 + e) if e0 or not isinstance(e, int) or e > 1 else None
                        dve.tensor_tensor(Wt[:, j % 2:j % 2 + 1], ga[:, j % 2:j % 2 + 1], G[:, bass.ds(e, 1)], ALU.mult).then_inc(w_made, 1)
                        dve.wait_ge(w_made, e0 + 1 + e)
                        dve.tensor_copy(WH[:, j % 2], Wt[:, j % 2]).then_inc(w_hi, 1)
                        dve.wait_ge(w_hi, e0 + 1 + e)
                        dve.tensor_tensor(WL[:, j % 2], Wt[:, j % 2], WH[:, j % 2].bitcast(F32), ALU.subtract).then_inc(w_ready, 1)
                        if more_u:
                            split_u(e + 2, j + 2)
                        if more_v:
                            split_v(e + 1, j + 1)

                    split_u(0, 0)
                    split_u(1, 1)
                    split_v(0, 0)
                    dve.wait_ge(g_evac, NGROUPS * (HALVES * L + half + 1))
                    for j in range(RING):
                        step(j, j)
                    with dve.Fori(1, I2H // RING - 1) as i:
                        for j in range(RING):
                            step(RING * i + j, j)
                    for j in range(RING):
                        step(I2H - RING + j, j, j < 2, j < 3)
                dve.wait_ge(peer_ps, L + 1)
                for n in range(4):
                    s = slice((n % 2) * 512, (n % 2 + 1) * 512)
                    ins = dve.tensor_tensor(xres[:, n // 2, s], xres[:, n // 2, s], PS[:, n], ALU.add)
                ins.then_inc(x_ready, 1)
                dve.wait_ge(x_ready, 3 * L + 2)
                norm(3 * L + 2, V[:, C_GPLE:C_GPLE + KT])
                dve.wait_ge(ple_ps, L + 1)
                dve.wait_ge(sgm_ready, 4 * (L + 1))
                for n in range(4):
                    s = slice((n % 2) * 512, (n % 2 + 1) * 512)
                    ins = dve.tensor_tensor(ptmp[:, n // 2, s], sgm[:, n // 2, s], PS[:, 4 + n], ALU.mult)
                link(ins)
                dve.tensor_tensor(xres[:], xres[:], ptmp[:], ALU.add).then_inc(x_ready, 1)
                dve.wait_ge(x_ready, 3 * (L + 1))
                dve.engine_nop().then_inc(ple_sum, 1)
            mean_square(3 * DEPTH)
            dve.wait_ge(in_g, 16)
            for tb in range(TB):
                dve.scalar_tensor_tensor(obuf[:, tb], xres[:, tb], rstd[:, tb:tb + 1], gfin[:], ALU.mult, ALU.mult).then_inc(out_ready, 1)

        @block.tensor
        def _(pe):
            mm = pe.matmul

            def norm(r):
                pe.wait_ge(xn_ready, TB * (r + 1))
                for k in range(KT):
                    for tb in range(TB):
                        ins = pe.transpose(PS[:, k // 2, (k % 2) * SEQ + tb * P:(k % 2) * SEQ + (tb + 1) * P], xn[:, tb, k * P:(k + 1) * P], ident)
                    if k % 2:
                        ins.then_inc(xT_ps, 1)
                pe.wait_ge(hT_act, 4 * (r + 1))
                pe.wait_ge(hT_dve, 4 * (r + 1))

            def slab(L, n):
                pe.wait_ge(filled[n % RING], 16 * fills(L, n))
                return ring[:, n % RING, :]

            def token_rows(L, n0, act_T, ktiles, bank0, wait=None):
                for k in range(ktiles):
                    if k % 2 == 0:
                        w = slab(L, n0 + k // 2)
                    for n in range(4):
                        ins = mm(PS[:, bank0 + n], act_T[:, k, (n // 2) * P:(n // 2 + 1) * P],
                                 w[:, (k % 2) * D + (n % 2) * 512:(k % 2) * D + (n % 2 + 1) * 512], start=k == 0, stop=k == ktiles - 1)
                    if k % 2 and k < ktiles - 1:
                        ins.then_inc(slab_used, 1)
                return ins

            pe.wait_ge(in_c, 16)
            pe.wait_ge(zeros_made, 1)
            for L in range(DEPTH):
                V = vec[:, L]
                norm(3 * L)
                for m in range(IN_TILES):
                    if m % 2 == 0:
                        w = slab(L, S_IN + m // 2)
                    if m >= 4:
                        pe.wait_ge(in_evac, IN_TILES * L + m - 3)
                    for k in range(KT):
                        ins = mm(PS[:, 4 + m % 4, 0:SEQ], w[:, (m % 2) * D + k * P:(m % 2) * D + (k + 1) * P], hT[:, k], start=k == 0, stop=k == KT - 1)
                    ins.then_inc(in_ps, 1)
                    if m % 2 or m == IN_TILES - 1:
                        pe.wait_ge(in_ps, IN_TILES * L + m + 1)
                        pe.nop().then_inc(slab_used, 1)
                pe.wait_ge(in_evac, IN_TILES * (L + 1))
                for tb in range(TB):
                    ins = pe.transpose(PS[:, 0, tb * P:(tb + 1) * P], aT[:, T_V - T_Q, tb * P:(tb + 1) * P], ident)
                ins.then_inc(vtA_ps, 1)
                for tb in range(TB):
                    nk = P * (tb + 1)
                    for h in range(NH):
                        r = slice(64 * (h // 4), 64 * (h // 4) + 64)
                        bank = 4 + h // 2 if tb else 1 + h // 4
                        at = (h % 2) * 2 * P if tb else (h % 4) * P
                        ins = mm(PS[:, bank, at:at + nk], aT[r, h % 4, tb * P:(tb + 1) * P], aT[r, T_K - T_Q, 0:nk], start=True, stop=True)
                    ins.then_inc(sc_ps, 1)
                for tb in range(TB):
                    pe.wait_ge(p_ready, TB * L + tb + 1)
                    for h in range(NH):
                        for s in range(tb + 1):
                            i = h * (tb + 1) + s
                            bank = (4 if tb else 1) + i // 4
                            ins = pe.transpose(PS[:, bank, (i % 4) * P:(i % 4 + 1) * P], (lg1 if tb else lg0)[:, h, s * P:(s + 1) * P], ident)
                            if i % 4 == 3:
                                ins.then_inc(pT_ps, 1)
                for tb in range(TB):
                    pe.wait_ge(pT_ready, 6 * L + (6 if tb else 2))
                    pe.wait_ge(vtA_ready, L + 1)
                    for h in range(NH):
                        for s in range(tb + 1):
                            ins = mm(PS[:, 0 if tb else 3, h * HD:(h + 1) * HD], PT1[:, h, s] if tb else PT0[:, h],
                                     vtA[:, s, HD * (h // 4):HD * (h // 4 + 1)], start=s == 0, stop=s == tb)
                    ins.then_inc(pv_ps, 1)
                pe.wait_ge(ao_normed, L + 1)
                for k in range(4):
                    for tb in range(TB):
                        ins = pe.transpose(PS[:, 4 + k // 2, (k % 2) * SEQ + tb * P:(k % 2) * SEQ + (tb + 1) * P], ao[:, tb, k * P:(k + 1) * P], ident)
                    if k % 2:
                        ins.then_inc(aoT_ps, 1)
                w = slab(L, S_LORA)
                pe.wait_ge(yTa_ready, L + 1)
                pe.wait_ge(lora_in, 2 * (L + 1))
                for t in range(4):
                    ins = mm(PS[:, t // 2, (t % 2) * SEQ:(t % 2 + 1) * SEQ], w[0:64, t * P:(t + 1) * P], xw_t[0:64], start=True, stop=True)
                ins.then_inc(lora_ps, 1)
                for t in range(4):
                    ins = mm(PS[:, 2 + t // 2, (t % 2) * SEQ:(t % 2 + 1) * SEQ], w[64:128, t * P:(t + 1) * P], fm[64:128, T_LORA], start=True, stop=True)
                ins.then_inc(lora_ps, 1)
                for t in range(4):
                    dst = PS[:, 4 + t // 2, (t % 2) * SEQ:(t % 2 + 1) * SEQ]
                    mm(dst, w[:, 512 + t * P:512 + (t + 1) * P], xg_s[:, 0], start=True, stop=False)
                    ins = mm(dst, w[0:32, 1024 + t * P:1024 + (t + 1) * P], xg_s[0:32, 1], start=False, stop=True)
                ins.then_inc(lora_ps, 1)
                pe.wait_ge(lora_ps, 3 * (L + 1))
                pe.nop().then_inc(slab_used, 1)
                pe.wait_ge(sqk_ready, L + 1)
                for n in range(2):
                    ins = mm(PS[:, 6 + n], ones2, sqk[:, 2 * n:2 * n + 2].rearrange("p a b -> p (a b)"), start=True, stop=True)
                ins.then_inc(kss_ps, 1)
                pe.wait_ge(kss_max, L + 1)
                pe.wait_ge(rk_ready, L + 1)
                for n in range(2):
                    ins = mm(PS[:, 6 + n], ones2, rkprod[:, 2 * n:2 * n + 2].rearrange("p a b -> p (a b)"), start=True, stop=True)
                ins.then_inc(bonus_ps, 1)
                pe.wait_ge(gates_ready, 2 * (L + 1))
                pe.wait_ge(g_ready, L + 1)
                for n, src in enumerate((fm[:, 8:12], bt, kt)):
                    if n == 1:
                        pe.wait_ge(bkt_ready, 2 * L + 1)
                    for tb in range(TB):
                        for t in range(4):
                            ins = pe.transpose(PS[:, 2 * n + tb, t * P:(t + 1) * P], src[:, t, tb * P:(tb + 1) * P], ident)
                    ins.then_inc(tok_ps, 1)
                pe.wait_ge(bkt_ready, 2 * (L + 1))
                pe.wait_ge(bonus_ready, L + 1)
                for n in range(16):
                    tb, h = n // NH, n % NH
                    r = slice(64 * (h % 2), 64 * (h % 2) + 64)
                    if n >= 2:
                        pe.wait_ge(prod_ready, 16 * L + n - 1)
                    rhs2 = ar[r, h // 2, tb].rearrange("p a b -> p (a b)")
                    mm(PS[:, 6 + n % 2, 0:256], bt[r, h // 2, tb * P:(tb + 1) * P], rhs2, start=True, stop=True)
                    mm(PS[:, 6 + n % 2, 256:512], kt[r, h // 2, tb * P:(tb + 1) * P], rhs2, start=True, stop=True).then_inc(prod_ps, 1)
                pe.wait_ge(tok_ready, 3 * (L + 1))
                pe.wait_ge(prod_ready, 16 * (L + 1))
                for lv in range(LEVELS):
                    pe.wait_ge(mt_ready, LEVELS * L + lv + 1)
                    for g in range(4):
                        if lv:
                            pe.wait_ge(xm_ready, 4 * (LEVELS * L + lv - 1) + g + 1)
                        for n in range(4 * g, 4 * g + 4):
                            ins = mm(PS[:, g, (n % 4) * P:(n % 4 + 1) * P], Mt[:, lv % 2, n], X[:, n] if lv else ident, start=True, stop=True)
                        ins.then_inc(m_ps, 1)
                    if lv == 0:
                        continue
                    for g in range(4):
                        pe.wait_ge(px_ready, 4 * ((LEVELS - 1) * L + lv - 1) + g + 1)
                        for n in range(4 * g, 4 * g + 4):
                            if lv < LEVELS - 1:
                                mm(PS[:, 4 + g, (n % 4) * P:(n % 4 + 1) * P], XT[:, n], PX[:, n], start=True, stop=True)
                        for n in range(4 * g, 4 * g + 4):
                            ins = mm(PS[:, g, (n % 4) * P:(n % 4 + 1) * P], PX[:, n], XT[:, n], start=True, stop=True)
                        ins.then_inc(xpt_ps, 1)
                pe.wait_ge(xm_ready, 4 * LEVELS * (L + 1))
                for c in range(NCHUNK):
                    tb, o = c // 2, 64 * (c % 2)
                    rows, cols = slice(o, o + 64), slice(o, o + 64)
                    if c:
                        pe.wait_ge(st_ready, (NCHUNK - 1) * L + c)
                    for t in range(4):
                        if c:
                            mm(PS[rows, 0, t * P:(t + 1) * P], ar[:, t, tb, 0, cols], ST[:, (c - 1) % 2, t], start=True, stop=False)
                        for h in (2 * t, 2 * t + 1):
                            ins = mm(PS[rows, 0, h * HD:(h + 1) * HD], prods[:, tb * NH + h, 256 + o:256 + o + 64], vtok[:, tb, h * HD:(h + 1) * HD],
                                     start=c == 0, stop=c == 0 or h % 2 == 1)
                    ins.then_inc(rhs_ps, 1)
                    pe.wait_ge(rhs_ready, NCHUNK * L + c + 1)
                    for h in range(NH):
                        ins = mm(PS[rows, 1, h * HD:(h + 1) * HD], XT[:, tb * NH + h, cols], rhs[:, h * HD:(h + 1) * HD], start=True, stop=True)
                    ins.then_inc(sa_ps, 1)
                    pe.wait_ge(sa_ready, NCHUNK * L + c + 1)
                    if c < NCHUNK - 1:
                        for h in range(NH):
                            hr = slice(64 * (h % 2), 64 * (h % 2) + 64)
                            dst = PS[hr, 3, (h // 2) * HD:(h // 2 + 1) * HD]
                            mm(dst, btok[rows, tb, h * HD:(h + 1) * HD], sa[rows, h * HD:(h + 1) * HD], start=True, stop=False)
                            ins = mm(dst, ktok[rows, tb, h * HD:(h + 1) * HD], vtok[rows, tb, h * HD:(h + 1) * HD], start=False, stop=True)
                        ins.then_inc(st_ps, 1)
                    if c:
                        pe.wait_ge(y_ready, NCHUNK * L + c)
                    for t in range(4):
                        if c:
                            mm(PS[rows, 2, t * P:(t + 1) * P], ar[:, t, tb, 1, cols], ST[:, (c - 1) % 2, t], start=True, stop=False)
                        for h in (2 * t, 2 * t + 1):
                            dst = PS[rows, 2, h * HD:(h + 1) * HD]
                            mm(dst, prods[:, tb * NH + h, 128 + o:128 + o + 64], sa[:, h * HD:(h + 1) * HD], start=c == 0, stop=False)
                            ins = mm(dst, prods[:, tb * NH + h, 384 + o:384 + o + 64], vtok[:, tb, h * HD:(h + 1) * HD], start=False, stop=c == 0 or h % 2 == 1)
                    ins.then_inc(y_ps, 1)
                pe.wait_ge(yn_ready, L + 1)
                for t in range(4):
                    for tb in range(TB):
                        ins = pe.transpose(PS[:, 4 + t // 2, (t % 2) * SEQ + tb * P:(t % 2) * SEQ + (tb + 1) * P], yc[:, tb, t * P:(t + 1) * P], ident)
                ins.then_inc(yT_ps, 1)
                pe.wait_ge(yTr_ready, L + 1)
                token_rows(L, S_OUT, hT, KT, 0).then_inc(op_ps, 1)
                pe.wait_ge(op_ps, L + 1)
                pe.nop().then_inc(slab_used, 1)
                norm(3 * L + 1)
                for m in range(HC):
                    if m % 2 == 0:
                        w = slab(L, S_WQ + m // 2)
                    if m >= 4:
                        pe.wait_ge(q_ready, HC * L + m - 3)
                    for k in range(KT):
                        ins = mm(PS[:, 4 + m % 4, 0:SEQ], w[:, (m % 2) * D + k * P:(m % 2) * D + (k + 1) * P], hT[:, k], start=k == 0, stop=k == KT - 1)
                    ins.then_inc(q_ps, 1)
                    if m % 2:
                        pe.wait_ge(q_ps, HC * L + m + 1)
                        pe.nop().then_inc(slab_used, 1)
                pe.wait_ge(q_ready, HC * (L + 1))
                for n in range(8):
                    for j in range(4):
                        hc = 4 * (n % 4) + j
                        keys = V[:, C_KEYS + (hc % 2) * NSUB:C_KEYS + (hc % 2 + 1) * NSUB]
                        ins = mm(PS[:, n, j * P:(j + 1) * P], qT[:, hc, (n // 4) * P:(n // 4 + 1) * P], keys, start=True, stop=True)
                    ins.then_inc(psc_ps, 1)
                pe.wait_ge(psc_ready, 8 * (L + 1))
                pe.wait_ge(slot_ready, TB * (L + 1))
                for c in range(3):
                    for tb in range(TB):
                        at = (c % 2) * SEQ + tb * P
                        ins = pe.transpose(PS[:, c // 2, at:at + P], slot[:, c, tb], ident)
                ins.then_inc(slot_ps, 1)
                for half in range(HALVES):
                    t0, g0 = SEQ * (HALVES * L + half), NGROUPS * (HALVES * L + half)

                    def spread(group, bank, wait=True):
                        if wait:
                            pe.wait_ge(g_evac, g0 - 1 + group)
                        for j in range(GROUP):
                            pe.wait_ge(hot_made, t0 + j + 1 + GROUP * group)
                            mm(PS[:, bank, j * I2H:(j + 1) * I2H], hot1[:, j], hot2[:, j], start=True, stop=True).then_inc(g_ps, 1)

                    spread(0, 4, bool(g0))
                    spread(1, 5, bool(g0))
                    with pe.Fori(1, NGROUPS // 2) as i:
                        spread(2 * i, 4)
                        spread(2 * i + 1, 5)
                    if half == 0:
                        pe.wait_ge(slot_T, L + 1)
                        pe.wait_ge(hTl_ready, L + 1)
                        for n in range(4):
                            mm(PS[:, n], zeros[:, 0:P], zeros[:], start=True, stop=False, skip_group_check=True)
                    e0 = NSUB * L + I2H * half

                    def hidden(e, j):
                        pe.wait_ge(u_lo, e0 + 1 + e)
                        pe.wait_ge(ga_ready, e0 - 1 + e) if e0 or not isinstance(e, int) or e > 1 else None
                        n = 0
                        for k in range(KT):
                            ks = slice(k * P, (k + 1) * P)
                            for u, h in ((UH, hTh), (UH, hTl), (UL, hTh)):
                                ins = mm(PS[:, 6 + j % 2, 0:SEQ], u[:, j % 2, ks], h[:, k], start=n == 0, stop=n == 3 * KT - 1)
                                n += 1
                        ins.then_inc(a_ps, 1)

                    def spend(e, j):
                        pe.wait_ge(v_lo, e0 + 1 + e)
                        pe.wait_ge(w_ready, e0 + 1 + e)
                        for tb in range(TB):
                            for w, v in ((WH, VH), (WH, VL), (WL, VH)):
                                for s in range(2):
                                    ins = mm(PS[:, 2 * tb + s], w[:, j % 2, tb * P:(tb + 1) * P], v[:, j % 2, s * 512:(s + 1) * 512],
                                             start=False, stop=False, skip_group_check=True)
                        ins.then_inc(v_used, 1)

                    hidden(0, 0)
                    for j in range(RING):
                        hidden(j + 1, j + 1)
                        spend(j, j)
                    with pe.Fori(1, I2H // RING - 1) as i:
                        for j in range(RING):
                            hidden(RING * i + j + 1, j + 1)
                            spend(RING * i + j, j)
                    for j in range(RING):
                        if j < RING - 1:
                            hidden(I2H - RING + j + 1, j + 1)
                        spend(I2H - RING + j, j)
                for n in range(4):
                    ins = mm(PS[:, n], zeros[:, 0:P], zeros[:], start=False, stop=True, skip_group_check=True)
                ins.then_inc(peer_ps, 1)
                norm(3 * L + 2)
                token_rows(L, S_GATE, hT, KT, 0).then_inc(gate_ps, 1)
                pe.wait_ge(gate_ps, L + 1)
                pe.nop().then_inc(slab_used, 1)
                if L == 0:
                    pe.wait_ge(in_p, 16)
                token_rows(L, S_PLE, pT[:, L], 2, 4).then_inc(ple_ps, 1)
                pe.wait_ge(ple_ps, L + 1)
                pe.nop().then_inc(slab_used, 1)


def shape_constants():
    c = np.zeros((P, NCONST), np.float32)
    i = np.arange(P)
    s, t = i[:, None], i[None, :]
    same = s // CHUNK == t // CHUNK
    c[:, K_ID:K_ID + P] = s == t
    c[:, K_ONES:K_ONES + P] = s // HD == t // HD
    c[:, K_PMASK:K_PMASK + P] = same & (s < t)
    c[:, K_PMASK + P:K_PMASK + 2 * P] = same & (s <= t)
    for lv in range(LEVELS):
        bs, bt = s >> lv, t >> lv
        c[:, K_LMASK + lv * P:K_LMASK + (lv + 1) * P] = (bt % 2 == 1) & (bs == bt - 1)
    c[:, K_RESET:K_RESET + SEQ] = np.arange(SEQ)[None, :] % CHUNK != 0
    for k0, q0, nk in ((K_DIST0, 0, P), (K_DIST1, P, 2 * P)):
        q, key = q0 + i[:, None], np.arange(nk)[None, :]
        back = q // CHUNK - key // CHUNK
        c[:, k0:k0 + nk] = np.where((back >= 0) & (back <= 1), np.abs(q - key), 1e33)
    c[:, K_IOTA:K_IOTA + NSUB] = i[None, :]
    c[:, K_IOTA16:K_IOTA16 + TOPK] = np.arange(TOPK)[None, :]
    return c


def lay_out(a):
    f = np.float32
    A, RW = 768, 1824
    w_in, b_in = np.asarray(a["w_in"]), np.asarray(a["b_in"])
    q_order = np.concatenate([np.concatenate([np.arange(HD) + HD * t, np.arange(HD) + HD * (t + 4)]) for t in range(4)])

    def in_tiles(m):
        pad = np.zeros(m.shape[:-1] + (RW_TILES * P - RW,), f)
        return np.concatenate([m[..., A:A + RW], pad, m[..., q_order], m[..., 512:A]], -1)

    def column_slabs(w):
        n = w.shape[1] // P
        s = w.reshape(KT, P, n, P).transpose(2, 1, 0, 3).reshape(n, P, D)
        if n % 2:
            s = np.concatenate([s, np.zeros((1, P, D), f)])
        return s.reshape(-1, 2, P, D).transpose(0, 2, 1, 3).reshape(-1, P, SLABW)

    def row_slabs(w):
        return w.reshape(-1, 2, P, D).transpose(0, 2, 1, 3).reshape(-1, P, SLABW)

    def cols(v):
        return v.reshape(-1, P).T

    slabs, vecs, peer = [], [], []
    for L in range(DEPTH):
        g = lambda n: np.asarray(a[n])[L]
        lora = np.zeros((P, SLABW), f)
        lora[0:64, 0:512], lora[64:128, 0:512] = g("rwkv_w_up"), g("rwkv_a_up")
        lora[:, 512:1024], lora[0:32, 1024:1536] = g("rwkv_g_up")[0:P], g("rwkv_g_up")[P:]
        slabs.append(np.concatenate([column_slabs(in_tiles(w_in[L])), lora[None], row_slabs(g("w_out")), column_slabs(g("peer_wq")),
                                     row_slabs(g("ple_gate")), row_slabs(g("ple_proj"))]))
        mu = np.concatenate([g("rwkv_mu"), np.zeros(RW_TILES * P - RW, f)])
        v = [cols(g("norm_mix")), cols(g("norm_ffn")), cols(g("norm_ple")), cols(in_tiles(b_in[L])), cols(mu)]
        v += [cols(g("rwkv_" + n).reshape(-1)) for n in ("w0", "a0", "k_k", "k_a", "r_k", "lnx_w", "lnx_b")]
        v += [cols(g("attn_out_norm")), np.broadcast_to(g("attn_sinks")[None], (P, NH))]
        v += [g("peer_keys")[c].T for c in range(2)]
        vecs.append(np.concatenate(v, 1))
        u = g("peer_u").reshape(NSUB, NSUB, KT, P).transpose(1, 3, 2, 0).reshape(NSUB, P, D)
        t = g("peer_v").reshape(NSUB, NSUB, D).transpose(1, 0, 2)
        peer.append(np.concatenate([u, t], 2))
    p = np.asarray(a["p"])[:, 0]
    return {
        "x": np.asarray(a["x"])[0].reshape(TB, P, D).transpose(1, 0, 2),
        "w_slabs": np.stack(slabs),
        "peer_slabs": np.stack(peer),
        "vecs": np.stack(vecs, 1),
        "consts": shape_constants(),
        "p_t": p.transpose(0, 2, 1).reshape(DEPTH, 2, P, SEQ).transpose(2, 0, 1, 3),
        "g_final": np.broadcast_to(np.asarray(a["norm_final"])[None], (P, D)),
    }


def kernel(**inputs):
    from concourse import bacc
    from concourse.bass_utils import run_bass_kernel_spmd

    nc = bacc.Bacc("TRN2", target_bir_lowering=False, num_devices=1)
    arrays, args = {}, []
    for name, v in lay_out(inputs).items():
        v = np.ascontiguousarray(v)
        arrays[f"in_{name}"] = v
        args.append(nc.dram_tensor(f"in_{name}", v.shape, mybir.dt.from_np(v.dtype), kind="ExternalInput").ap())
    out = nc.dram_tensor("out", (P, TB, D), F32, kind="ExternalOutput").ap()
    hybrid_encoder(nc, *args, out)
    r = run_bass_kernel_spmd(nc, [arrays], core_ids=[0])
    return r.results[0]["out"].transpose(1, 0, 2).reshape(1, SEQ, D)
```

```python
from contextlib import ExitStack

import numpy as np

import concourse.bass as bass
from concourse import mybir

F32 = mybir.dt.float32
F32R = mybir.dt.float32r
U32 = mybir.dt.uint32
ALU = mybir.AluOpType
ACT = mybir.ActivationFunctionType
AX = mybir.AxisListType

P = 128
DEPTH, SEQ, D = 2, 256, 1024
TB = SEQ // P
KT = D // P
CHUNK, HD, NH, NKV = 64, 64, 8, 2
NCHUNK = SEQ // CHUNK
EPS, LNX_EPS = 1e-6, 64e-5
EXP_MINUS_HALF = float(np.exp(-0.5))
SLOPES = [float(2.0 ** (-8.0 * (h + 1) / NH)) for h in range(NH)]

RW_TILES, IN_TILES = 15, 21
T_LORA, T_GATE, T_Q, T_K, T_V = 12, 13, 15, 19, 20

PH, TOPK, NSUB = 8, 16, 128
HC = 2 * PH
SLOTS = PH * TOPK
NQ = 4
QT = NSUB // NQ
HELD = 2 * QT
GROUP = 8
NGROUPS = SEQ // GROUP
A_FIRST, A_SECOND, A_TOP = 16, 28, 32

RING, SLABW = 4, 2048
S_IN, S_LORA, S_OUT, S_WQ, S_PEER, S_GATE, S_PLE, S_ALL = 0, 11, 12, 16, 24, 152, 156, 160
S_UV, S_VV = S_PEER + HELD // 2, S_PEER + HELD // 2 + HELD
U_ALL, V_ALL, U_PRE, V_PRE = 156, 155, 23, 22

C_GMIX, C_GFFN, C_GPLE, C_BIN, C_MU = 0, 8, 16, 24, 45
C_W0, C_A0, C_KK, C_KA, C_RK, C_LNW, C_LNB, C_AN, C_SINK, C_KEYS = 60, 64, 68, 72, 76, 80, 84, 88, 92, 100
NVEC = C_KEYS + 2 * NSUB
K_ID, K_ONES, K_PMASK, K_LMASK, K_RESET, K_DIST0, K_DIST1, K_IOTA, K_IOTA16 = 0, 128, 256, 512, 1280, 1536, 1664, 1920, 2048
NCONST = 2064
LEVELS = 6


def fills(layer, n):
    per_layer = S_ALL // RING - (1 if n % RING else 0)
    return layer * per_layer + n // RING + 1


class Tile:

    def __init__(self, layer, slab, part, count):
        self.layer, self.slab, self.part, self.count = layer, slab, part, count


def projection_tile(layer, stage, k):
    slab, u, v = {"in": (S_IN, 0, 0), "out": (S_OUT, 11, 10), "wq": (S_WQ, 15, 14), "ple": (S_GATE, U_PRE + NSUB, V_PRE + NSUB)}[stage]
    return Tile(layer, slab + k // 2, k % 2, layer * (V_ALL if k % 2 else U_ALL) + (v if k % 2 else u) + k // 2)


def hybrid_encoder(nc, x, w_slabs, peer_slabs, vecs, consts, p_t, g_final, out):
    with ExitStack() as ctx:
        def sem(name):
            return ctx.enter_context(nc.semaphore(name))

        first = (nc.sbuf_base + 31) // 32 * 8

        def place(name, at, shape, dt=F32):
            return nc.alloc_sbuf_tensor_at(name, [P] + shape, dt, offset=4 * (first + at))

        xres = place("xres", 0, [TB, D])
        hTh = place("hTh", 2048, [KT, SEQ], F32R)
        hTl = place("hTl", 4096, [KT, SEQ], F32R)
        ring = place("ring", 6144, [RING, SLABW])
        cst = place("cst", 14336, [NCONST])
        vec = place("vec", 16400, [DEPTH, NVEC])
        pTh = place("pTh", 17120, [DEPTH, 2, SEQ], F32R)
        pTl = place("pTl", 18144, [DEPTH, 2, SEQ], F32R)
        stat = place("stat", 19168, [256])
        M = 19424
        UH = place("UH", M, [2, D], F32R)
        UL = place("UL", M + 2048, [2, D], F32R)
        VH = place("VH", M + 4096, [2, D], F32R)
        VL = place("VL", M + 6144, [2, D], F32R)
        R = M + 8192
        zeros = place("zeros", R + 25088, [P])
        praw = place("praw", R + 24064, [DEPTH, 2, SEQ])
        xn = place("xn", R, [TB, D])
        gfin = place("gfin", R + 6144, [D])
        obuf = place("obuf", R + 8192, [TB, D])
        fpad = place("fpad", R + 2048, [RW_TILES, SEQ + 1])
        fm = place("fm", R + 5904, [RW_TILES, SEQ])
        prods = place("prods", R + 2048, [TB * NH, 512])
        sw = place("sw", M, [4, SEQ])
        csum = place("csum", M + 1024, [4, SEQ])
        cprev = place("cprev", M + 2048, [4, SEQ])
        winv = place("winv", M + 3072, [4, SEQ])
        wprev = place("wprev", M + 4096, [4, SEQ])
        kk = place("kk", M + 5120, [4, SEQ])
        sqk = place("sqk", M + 6144, [4, SEQ])
        kmod = place("kmod", M + 6144, [4, SEQ])
        rnorm = place("rnorm", M + 7168, [4, SEQ])
        bvec = place("bvec", M + 8192, [4, SEQ])
        rkprod = place("rkprod", M + 9216, [4, SEQ])
        Mt = place("Mt", M, [2, TB * NH, P])
        X = place("X", M + 4096, [TB * NH, P])
        XT = place("XT", M + 6144, [TB * NH, P])
        PX = place("PX", M + 8192, [TB * NH, P])
        ytok = place("ytok", R, [TB, 512])
        rhs = place("rhs", R + 1024, [512])
        sa = place("sa", R + 1536, [512])
        yc = place("yc", R + 2048, [TB, 512])
        ysq = place("ysq", R + 3072, [TB, 512])
        ytmp = place("ytmp", R + 4096, [4, SEQ])
        lg0 = place("lg0", M, [NH, P])
        lg1 = place("lg1", M + 1024, [NH, 2 * P])
        PT0 = place("PT0", M + 3072, [NH, P])
        PT1 = place("PT1", M + 4096, [NH, 2, P])
        wcum = place("wcum", R + 10240, [4, SEQ])
        ar = place("ar", R + 11264, [4, TB, 2, P])
        bt = place("bt", R + 13312, [4, SEQ])
        kt = place("kt", R + 14336, [4, SEQ])
        vtok = place("vtok", R + 15360, [TB, 512])
        btok = place("btok", R + 16384, [TB, 512])
        ktok = place("ktok", R + 17408, [TB, 512])
        avec = place("avec", R + 17408, [4, SEQ])
        bonus_v = place("bonus_v", R + 18432, [4, SEQ])
        gT = place("gT", R + 19456, [4, SEQ])
        aT = place("aT", R + 20480, [6, SEQ])
        ST = place("ST", R + 20480, [2, 4, P])
        vtA = place("vtA", R + 22016, [TB, P])
        ao = place("ao", R + 22272, [TB, 512])
        xw_t = place("xw_t", R + 23296, [SEQ])
        xg_s = place("xg_s", R + 23552, [2, SEQ])
        GA = place("GA", R, [HELD, SEQ])
        WH = place("WH", R + 16384, [2, SEQ], F32R)
        WL = place("WL", R + 16896, [2, SEQ], F32R)
        hot1 = place("hot1", R + 17408, [2, GROUP, NSUB])
        hot2 = place("hot2", R + 19456, [2, GROUP, QT])
        sT = place("sT", R + 19968, [3, SEQ + GROUP])
        qT = place("qT", R + 2048, [HC, SEQ])
        sc = place("sc", R + 12288, [TB, HC, NSUB])
        topv = place("topv", R + 16384, [HC, TOPK])
        topi = place("topi", R + 16640, [HC, TOPK], U32)
        topf = place("topf", R + 16896, [HC, TOPK])
        bestv = place("bestv", R + 17152, [PH, TOPK])
        bestc = place("bestc", R + 17280, [PH, TOPK], U32)
        bestd = place("bestd", R + 17408, [2, PH * TOPK], U32)
        bestf = place("bestf", R + 17664, [2, PH, TOPK])
        onehot = place("onehot", R + 17920, [PH, TOPK, TOPK])
        slot = place("slot", R + 20768, [3, TB, SLOTS])
        cand = place("cand", R + 21536, [PH, TOPK * TOPK])
        picked = place("picked", R + 21536, [PH, TOPK, TOPK])
        sgm = place("sgm", R + 2048, [TB, D])
        ptmp = place("ptmp", R + 4096, [TB, D])

        PS = ctx.enter_context(nc.psum_tensor("PS", [P, 8, 512], F32))

        ident = cst[:, K_ID:K_ID + P]
        ones2 = cst[:, K_ONES:K_ONES + P]
        iota = cst[:, K_IOTA:K_IOTA + NSUB]
        iota16 = cst[:, K_IOTA16:K_IOTA16 + TOPK]
        ssq, rstd = stat[:, 0:2], stat[:, 2:4]
        amax, anm, arow, asink, aden = (stat[:, 8 + 16 * i:24 + 16 * i] for i in range(5))
        gmean, gvar = stat[:, 96:112], stat[:, 112:128]
        assq, arstd = stat[:, 128:130], stat[:, 130:132]
        gsum = stat[:, 136:144]
        bq8 = stat[:, 144:148]
        junk = PS

        in_x, in_c, in_v, in_p, in_g, p_hi, p_lo = (sem(n) for n in ("in_x", "in_c", "in_v", "in_p", "in_g", "p_hi", "p_lo"))
        filled = [sem(f"filled{i}") for i in range(RING)]
        part_hi, part_lo, part_used = ((sem("u" + n), sem("v" + n)) for n in ("_hi", "_lo", "_used"))
        zeros_made = sem("zeros_made")
        sumsq, mean_sq, rms, xn_ready, xT_ps, hT_hi, hT_lo = (
            sem(n) for n in ("sumsq", "mean_sq", "rms", "xn_ready", "xT_ps", "hT_hi", "hT_lo"))
        x_ready = sem("x_ready")
        bq_ready, in_evac, mixed = (sem(n) for n in ("bq_ready", "in_evac", "mixed"))
        vtA_ps, vtA_ready, sc_ps, nm_ready, p_ready = (sem(n) for n in ("vtA_ps", "vtA_ready", "sc_ps", "nm_ready", "p_ready"))
        pT_ps, pT_ready, pv_ps, ao_ready, ao_ssq, ao_ms, ao_rms, ao_normed, aoT_ps, yTa_hi, yTa_ready = (
            sem(n) for n in ("pT_ps", "pT_ready", "pv_ps", "ao_ready", "ao_ssq", "ao_ms", "ao_rms", "ao_normed", "aoT_ps", "yTa_hi", "yTa_ready"))
        lora_in, lora_ps, gates_ready, g_ready = (sem(n) for n in ("lora_in", "lora_ps", "gates_ready", "g_ready"))
        sqk_ready, kss_ps, kss_max, knorm, csum_ready, decay_ready = (
            sem(n) for n in ("sqk_ready", "kss_ps", "kss_max", "knorm", "csum_ready", "decay_ready"))
        rk_ready, bonus_ps, bonus_ready, bkt_ready, tok_ps, tok_ready = (
            sem(n) for n in ("rk_ready", "bonus_ps", "bonus_ready", "bkt_ready", "tok_ps", "tok_ready"))
        prod_ps, prod_ready, mt_ready, m_ps, xm_ready, px_ready, xp_ps, xpt_ps = (
            sem(n) for n in ("prod_ps", "prod_ready", "mt_ready", "m_ps", "xm_ready", "px_ready", "xp_ps", "xpt_ps"))
        rhs_ps, rhs_ready, sa_ps, sa_ready, y_ps, y_ready, st_ps, st_ready = (
            sem(n) for n in ("rhs_ps", "rhs_ready", "sa_ps", "sa_ready", "y_ps", "y_ready", "st_ps", "st_ready"))
        yc_ready, ysq_ready, yv_ready, ystd, yn_ready, yT_ps, yg_ready, yTr_hi, yTr_ready = (
            sem(n) for n in ("yc_ready", "ysq_ready", "yv_ready", "ystd", "yn_ready", "yT_ps", "yg_ready", "yTr_hi", "yTr_ready"))
        q_ready, psc_ps, psc_ready = (sem(n) for n in ("q_ready", "psc_ps", "psc_ready"))
        bd_ready, bexp_ready, slot_ready, slot_ps, slot_T = (sem(n) for n in ("bd_ready", "bexp_ready", "slot_ready", "slot_ps", "slot_T"))
        hot2_made, hots_made, spread_ps, gated = (sem(n) for n in ("hot2_made", "hots_made", "spread_ps", "gated"))
        ga_ready, w_hi, w_lo, peer_ps = (sem(n) for n in ("ga_ready", "w_hi", "w_lo", "peer_ps"))
        sgm_ready, ple_sum = (sem(n) for n in ("sgm_ready", "ple_sum"))
        out_ready, out_done = sem("out_ready"), sem("out_done")
        dve_step, act_step, pool_step = sem("dve_step"), sem("act_step"), sem("pool_step")

        block = ctx.enter_context(nc.Block())

        def raw(slab, part):
            return ring[:, slab % RING, part * D:(part + 1) * D]

        high, low = (UH, VH), (UL, VL)

        u0 = [U_ALL * L + U_PRE for L in range(DEPTH)]
        v0 = [V_ALL * L + V_PRE for L in range(DEPTH)]

        @block.sync
        def _(sp):
            sp.dma_start(xres[:], x).then_inc(in_x, 16)
            sp.dma_start(cst[:], consts).then_inc(in_c, 16)
            sp.dma_start(vec[:], vecs).then_inc(in_v, 16)

            def load(layer, n, src):
                sp.dma_start(ring[:, n % RING, :], src).then_inc(filled[n % RING], 16)

            def wait_split(part, count):
                sp.wait_ge(part_lo[part], count)

            def wait_free(L, n):
                before, Lb = (n - RING, L) if n >= RING else (S_GATE + n if n else S_PLE, L - 1)
                if Lb < 0:
                    return
                if before == S_LORA:
                    sp.wait_ge(lora_ps, 3 * (Lb + 1))
                elif before == S_LORA - 1:
                    wait_split(0, projection_tile(Lb, "in", IN_TILES - 1).count + 1)
                elif before < S_PEER:
                    stage, k = ("in", before) if before < S_LORA else ("out", before - S_OUT) if before < S_WQ else ("wq", before - S_WQ)
                    wait_split(1, projection_tile(Lb, stage, 2 * k + 1).count + 1)
                elif before >= S_GATE:
                    wait_split(1, projection_tile(Lb, "ple", 2 * (before - S_GATE) + 1).count + 1)
                else:
                    wait_split(1, v0[L] + NSUB - 2 * (S_GATE - 1 - before))

            for L in range(DEPTH):
                for n in range(S_PEER + RING):
                    wait_free(L, n)
                    load(L, n, w_slabs[L, n] if n < S_PEER else peer_slabs[L, n - S_PEER])
                    if L == 0 and n == RING - 1:
                        sp.dma_start(praw[:], p_t).then_inc(in_p, 16)
                with sp.Fori(0, (S_UV - S_PEER) // RING) as i:
                    for j in range(RING):
                        wait_split(0, u0[L] + 2 * (RING * i + j) + 2)
                        load(L, j, peer_slabs[L, RING * i + (j + RING)])
                with sp.Fori(0, (S_VV - S_UV) // RING) as i:
                    for j in range(RING):
                        wait_split(1, v0[L] + RING * i + (j + 1))
                        load(L, j, peer_slabs[L, RING * i + (j + S_UV - S_PEER + RING)])
                with sp.Fori(0, (S_GATE - S_VV) // RING - 1) as i:
                    for j in range(RING):
                        wait_split(1, v0[L] + HELD + 2 * (RING * i + j) + 2)
                        load(L, j, peer_slabs[L, RING * i + (j + S_VV - S_PEER + RING)])
                for n in range(S_GATE, S_PLE + 1):
                    wait_free(L, n)
                    load(L, n, w_slabs[L, S_PEER + n - S_GATE])
            sp.wait_ge(ple_sum, DEPTH)
            sp.dma_start(gfin[:], g_final).then_inc(in_g, 16)
            sp.wait_ge(out_ready, TB)
            sp.dma_start(out, obuf[:]).then_inc(out_done, 16)
            sp.wait_ge(out_done, 16)

        @block.gpsimd
        def _(pool):
            pool.memset(zeros[:], 0.0).then_inc(zeros_made, 1)
            pool.wait_ge(in_c, 16)
            for L in range(DEPTH):
                for lv in range(LEVELS):
                    pool.wait_ge(prod_ready, 16 * (L + 1))
                    if lv >= 2:
                        pool.wait_ge(m_ps, 4 * LEVELS * L + 4 * (lv - 1))
                        pool.wait_ge(xm_ready, 4 * LEVELS * L + 4 * (lv - 1))
                    mask = cst[:, K_LMASK + lv * P:K_LMASK + (lv + 1) * P].unsqueeze(1).broadcast_to([P, 16, P])
                    pool.tensor_tensor(Mt[:, lv % 2], prods[:, :, 0:P], mask, ALU.mult).then_inc(mt_ready, 1)
                def split_u(e, half, place, j):
                    pool.wait_ge(part_hi[0], u0[L] + 1 + e)
                    b = (u0[L] + j) % 2
                    pool.tensor_tensor(UL[:, b], ring[:, place, half * D:(half + 1) * D], UH[:, b].bitcast(F32), ALU.subtract).then_inc(part_lo[0], 1)

                with pool.Fori(0, HELD // 8) as i:
                    for j in range(8):
                        split_u(8 * i + j, j % 2, j // 2 % RING, j)
                with pool.Fori(0, (NSUB - HELD) // RING) as i:
                    for j in range(RING):
                        split_u(RING * i + (j + HELD), 0, j, j)

        @block.scalar
        def _(act):
            steps = [0]

            def link(ins):
                steps[0] += 1
                ins.then_inc(act_step, 1)
                act.wait_ge(act_step, steps[0])

            def split(tile):
                if tile.count >= 2:
                    act.wait_ge(part_used[tile.part], tile.count - 1)
                act.wait_ge(filled[tile.slab % RING], 16 * fills(tile.layer, tile.slab))
                act.copy(high[tile.part][:, tile.count % 2], raw(tile.slab, tile.part)).then_inc(part_hi[tile.part], 1)

            def norm(r, xs_ready, gain):
                act.wait_ge(x_ready, xs_ready) if xs_ready else act.wait_ge(in_x, 16)
                for tb in range(TB):
                    act.activation(xn[:, tb], xres[:, tb], ACT.Square, accum_out=ssq[:, tb:tb + 1]).then_inc(sumsq, 1)
                act.wait_ge(mean_sq, r + 1)
                act.activation(rstd, ssq, ACT.Sqrt).then_inc(rms, 1)
                if gain is None:
                    return
                for k in range(KT):
                    act.wait_ge(xT_ps, 4 * r + k // 2 + 1)
                    act.activation(hTh[:, k], PS[:, k // 2, (k % 2) * SEQ:(k % 2 + 1) * SEQ], ACT.Identity, scale=gain[:, k:k + 1]).then_inc(hT_hi, 1)

            act.wait_ge(in_v, 16)
            for L in range(DEPTH):
                V = vec[:, L]
                if L:
                    act.wait_ge(ple_sum, L)
                for k in range(4):
                    split(projection_tile(L, "in", k))
                norm(3 * L, 3 * L, V[:, C_GMIX:C_GMIX + KT])
                if L == 0:
                    act.wait_ge(in_p, 16)
                    act.copy(pTh[:], praw[:]).then_inc(p_hi, 1)
                for m in range(IN_TILES):
                    tile = projection_tile(L, "in", m)
                    act.wait_ge(part_used[tile.part], tile.count + 1)
                    src = PS[:, 4 + m % 4, 0:SEQ]
                    if m < RW_TILES:
                        act.activation(fpad[:, m, 1:SEQ + 1], src, ACT.Identity, bias=V[:, C_BIN + m:C_BIN + m + 1]).then_inc(in_evac, 1)
                    elif m < T_K:
                        if m == T_Q:
                            act.wait_ge(bq_ready, L + 1)
                        act.activation(aT[:, m - T_Q], src, ACT.Identity, bias=bq8[:, m - T_Q:m - T_Q + 1], scale=HD ** -0.5).then_inc(in_evac, 1)
                    else:
                        act.activation(aT[:, m - T_Q], src, ACT.Identity, bias=V[:, C_BIN + m:C_BIN + m + 1]).then_inc(in_evac, 1)
                    if m + 4 < IN_TILES:
                        split(projection_tile(L, "in", m + 4))
                act.wait_ge(vtA_ps, L + 1)
                act.copy(vtA[:], PS[:, 0, 0:TB * P]).then_inc(vtA_ready, 1)
                for tb in range(TB):
                    act.wait_ge(nm_ready, TB * L + tb + 1)
                    lg = lg1 if tb else lg0
                    for h in range(NH):
                        c = tb * NH + h
                        act.activation(lg[:, h], lg[:, h], ACT.Exp, bias=anm[:, c:c + 1], accum_out=arow[:, c:c + 1])
                    act.activation(asink[:, tb * NH:(tb + 1) * NH], asink[:, tb * NH:(tb + 1) * NH], ACT.Exp).then_inc(p_ready, 1)
                for n in range(6):
                    act.wait_ge(pT_ps, 6 * L + n + 1)
                    if n < 2:
                        act.copy(PT0[:, 4 * n:4 * n + 4], PS[:, 1 + n].rearrange("p (a b) -> p a b", a=4)).then_inc(pT_ready, 1)
                    else:
                        act.copy(PT1[:, 2 * (n - 2):2 * (n - 1)], PS[:, 2 + n].rearrange("p (a c b) -> p a c b", a=2, c=2)).then_inc(pT_ready, 1)
                act.wait_ge(ao_ready, TB * (L + 1))
                for tb in range(TB):
                    act.activation(PS[:, 6 + tb], ao[:, tb], ACT.Square, accum_out=assq[:, tb:tb + 1]).then_inc(ao_ssq, 1)
                act.wait_ge(ao_ms, L + 1)
                act.activation(arstd, assq, ACT.Sqrt).then_inc(ao_rms, 1)
                for k in range(4):
                    act.wait_ge(aoT_ps, 2 * L + k // 2 + 1)
                    act.activation(hTh[:, k], PS[:, 4 + k // 2, (k % 2) * SEQ:(k % 2 + 1) * SEQ], ACT.Identity, scale=V[:, C_AN + k:C_AN + k + 1]).then_inc(yTa_hi, 1)
                act.wait_ge(mixed, L + 1)
                act.activation(xw_t[0:64], fm[0:64, T_LORA], ACT.Tanh).then_inc(lora_in, 1)
                act.activation(xg_s[:, :, :], fm[:, T_GATE:T_GATE + 2], ACT.Sigmoid).then_inc(lora_in, 1)
                act.wait_ge(lora_ps, 3 * L + 1)
                act.wait_ge(yTa_ready, L + 1)
                for t in range(4):
                    ins = act.activation(sw[:, t], PS[:, t // 2, (t % 2) * SEQ:(t % 2 + 1) * SEQ], ACT.Sigmoid, bias=V[:, C_W0 + t:C_W0 + t + 1])
                ins.then_inc(gates_ready, 1)
                act.wait_ge(lora_ps, 3 * L + 2)
                for t in range(4):
                    ins = act.activation(avec[:, t], PS[:, 2 + t // 2, (t % 2) * SEQ:(t % 2 + 1) * SEQ], ACT.Sigmoid, bias=V[:, C_A0 + t:C_A0 + t + 1])
                ins.then_inc(gates_ready, 1)
                act.wait_ge(lora_ps, 3 * L + 3)
                act.copy(gT[:], PS[:, 4:6].rearrange("p a (b c) -> p (a b) c", b=2)).then_inc(g_ready, 1)
                act.wait_ge(kss_max, L + 1)
                act.activation(rnorm[:], rnorm[:], ACT.Sqrt).then_inc(knorm, 1)
                act.wait_ge(csum_ready, 2 * L + 1)
                act.activation(wcum[:], csum[:], ACT.Exp, scale=-EXP_MINUS_HALF).then_inc(decay_ready, 1)
                act.activation(winv[:], csum[:], ACT.Exp, scale=EXP_MINUS_HALF).then_inc(decay_ready, 1)
                act.wait_ge(csum_ready, 2 * L + 2)
                act.activation(wprev[:], cprev[:], ACT.Exp, scale=-EXP_MINUS_HALF).then_inc(decay_ready, 1)
                for n, dst in enumerate((vtok, btok, ktok)):
                    act.wait_ge(tok_ps, 3 * L + n + 1)
                    act.copy(dst[:], PS[:, 2 * n:2 * n + 2]).then_inc(tok_ready, 1)
                for lv in range(1, LEVELS):
                    for g in range(4):
                        act.wait_ge(m_ps, 4 * (LEVELS * L + lv) + g + 1)
                        act.copy(PX[:, 4 * g:4 * g + 4], PS[:, g].rearrange("p (a b) -> p a b", a=4)).then_inc(px_ready, 1)
                for c in range(NCHUNK):
                    o = 64 * (c % 2)
                    act.wait_ge(sa_ps, NCHUNK * L + c + 1)
                    act.copy(sa[o:o + 64], PS[o:o + 64, 1]).then_inc(sa_ready, 1)
                    act.wait_ge(y_ps, NCHUNK * L + c + 1)
                    act.copy(ytok[o:o + 64, c // 2], PS[o:o + 64, 2]).then_inc(y_ready, 1)
                act.wait_ge(yc_ready, L + 1)
                act.activation(ysq[:], yc[:], ACT.Square).then_inc(ysq_ready, 1)
                act.wait_ge(yv_ready, L + 1)
                act.activation(gvar, gvar, ACT.Sqrt).then_inc(ystd, 1)
                for k in range(4):
                    split(projection_tile(L, "out", k))
                act.wait_ge(yg_ready, L + 1)
                act.copy(hTh[:, 4:8], ytmp[:]).then_inc(yTr_hi, 1)
                for k in range(4, KT):
                    split(projection_tile(L, "out", k))
                for k in range(4):
                    split(projection_tile(L, "wq", k))
                norm(3 * L + 1, 3 * L + 1, V[:, C_GFFN:C_GFFN + KT])
                for m in range(HC):
                    tile = projection_tile(L, "wq", m)
                    act.wait_ge(part_used[tile.part], tile.count + 1)
                    act.copy(qT[:, m], PS[:, 4 + m % 4, 0:SEQ]).then_inc(q_ready, 1)
                    if m + 4 < HC:
                        split(projection_tile(L, "wq", m + 4))
                for n in range(8):
                    act.wait_ge(psc_ps, 8 * L + n + 1)
                    act.copy(sc[:, n // 4, 4 * (n % 4):4 * (n % 4) + 4], PS[:, n].rearrange("p (a b) -> p a b", a=4)).then_inc(psc_ready, 1)

                def split_tile(part, count, parity, place, half, fill):
                    act.wait_ge(part_used[part], count - 1)
                    act.wait_ge(filled[place], fill)
                    act.copy(high[part][:, parity], ring[:, place, half * D:(half + 1) * D]).then_inc(part_hi[part], 1)

                def gelu(place, j):
                    act.activation(GA[:, bass.ds(place, 1)], PS[:, 6 + j % 2:7 + j % 2, 0:SEQ], ACT.Gelu).then_inc(ga_ready, 1)

                def split_u(e0_8, j):
                    place = j // 2 % RING
                    split_tile(0, u0[L] + j + e0_8, (u0[L] + j) % 2, place, j % 2, 16 * fills(L, S_PEER + j // 2) + (16 // 8) * e0_8)

                def split_w(s, j):
                    act.wait_ge(part_used[1], v0[L] - 1 + s)
                    act.copy(WH[:, j % 2:j % 2 + 1], GA[:, bass.ds(s, 1)]).then_inc(w_hi, 1)

                split_u(0, 0)
                split_u(0, 1)
                def exponentials(tb):
                    act.wait_ge(bd_ready, TB * L + tb + 1)
                    act.activation(slot[:, 2, tb], slot[:, 2, tb], ACT.Exp).then_inc(bexp_ready, 1)

                with act.Fori(0, A_FIRST // 8) as i:
                    for j in range(8):
                        split_u(8 * i, j + 2)
                        gelu(8 * i + j, j)
                exponentials(0)
                with act.Fori(A_FIRST // 8, A_SECOND // 8) as i:
                    for j in range(8):
                        split_u(8 * i, j + 2)
                        gelu(8 * i + j, j)
                for e in range(A_SECOND // 8 * 8, A_TOP):
                    if e == A_SECOND:
                        exponentials(1)
                    split_u((e + 2) // 8 * 8, (e + 2) % 8)
                    gelu(e, e)
                act.wait_ge(slot_ps, L + 1)
                act.copy(sT[:, 0:2, 0:SEQ], PS[:, 4].rearrange("p (a b) -> p a b", a=2))
                act.copy(sT[:, 0:2, SEQ:], PS[:, 4].rearrange("p (a b) -> p a b", a=2)[:, :, 0:GROUP])
                act.copy(sT[:, 2, 0:SEQ], PS[:, 5, 0:SEQ])
                act.copy(sT[:, 2, SEQ:], PS[:, 5, 0:GROUP]).then_inc(slot_T, 1)
                with act.Fori(A_TOP // 8, HELD // 8 - 1) as i:
                    for j in range(8):
                        split_u(8 * i, j + 2)
                        gelu(8 * i + j, j)
                for j in range(6):
                    split_u(HELD - 8, j + 2)
                    gelu(HELD - 8 + j, j)

                def split_uv(i, j, part):
                    if part:
                        act.wait_ge(part_lo[0], u0[L] + HELD + 1 + RING * i + j)
                    base = (u0[L] + HELD if part == 0 else v0[L]) + j
                    split_tile(part, RING * i + base, base % 2, j % RING, part, 16 * fills(L, S_UV + j) + 16 * i)

                def split_vv(i, j):
                    base = v0[L] + HELD + j
                    split_tile(1, 8 * i + base, base % 2, j // 2 % RING, j % 2, 16 * fills(L, S_VV + j // 2) + 16 * i)

                for j in range(2):
                    split_uv(0, j, 0)
                    gelu(HELD - 2 + j, j)
                split_uv(0, 0, 1)
                act.wait_ge(gated, NGROUPS * (NQ * L + 1))
                split_w(0, 0)

                def split_w_late(place, j):
                    act.wait_ge(part_used[1], v0[L] + HELD - 1 + place)
                    act.copy(WH[:, j % 2:j % 2 + 1], GA[:, bass.ds(place, 1)]).then_inc(w_hi, 1)

                def step(i, j):
                    s = RING * i + j
                    act.wait_ge(w_lo, NSUB * L + 1 + s)
                    split_uv(i, j + 1, 1)
                    split_uv(i, j + 2, 0)
                    gelu(s, j)
                    act.wait_ge(gated, NGROUPS * NQ * L + NGROUPS + 1 + s)
                    split_w(s + 1, j + 1)

                with act.Fori(0, HELD // RING - 1) as i:
                    for j in range(RING):
                        step(i, j)
                for s in range(HELD - RING, HELD):
                    if s < HELD - 1:
                        split_uv(s // RING, s % RING + 1, 1)
                    else:
                        split_vv(0, 0)
                    if s < HELD - 2:
                        split_uv(s // RING, s % RING + 2, 0)
                    else:
                        act.wait_ge(part_used[0], u0[L] + HELD + s + 1)
                    act.wait_ge(w_lo, NSUB * L + 1 + s)
                    gelu(s, s)
                    act.wait_ge(gated, NGROUPS * NQ * L + NGROUPS + 1 + s)
                    if s < HELD - 1:
                        split_w(s + 1, s + 1)
                    else:
                        split_w_late(0, 0)
                for lo, hi in ((0, QT // 8), (QT // 8, HELD // 8 - 1)):
                    with act.Fori(lo, hi) as i:
                        for j in range(8):
                            split_vv(i, j + 1)
                            if lo == 0:
                                act.wait_ge(gated, NGROUPS * (NQ * L + 3) + 1 + 8 * i + j)
                            split_w_late(8 * i + (j + 1), j + 1)
                for j in range(7):
                    split_vv(HELD // 8 - 1, j + 1)
                    split_w_late(HELD - 8 + (j + 1), j + 1)
                for k in range(2):
                    split(projection_tile(L, "ple", 2 * k))
                    split(projection_tile(L, "ple", 2 * k + 1))
                norm(3 * L + 2, 3 * L + 2, V[:, C_GPLE:C_GPLE + KT])
                for k in range(4, 10):
                    split(projection_tile(L, "ple", k))
                act.wait_ge(part_used[1], projection_tile(L, "ple", KT - 1).count + 1)
                for n in range(4):
                    act.activation(sgm[:, n // 2, (n % 2) * 512:(n % 2 + 1) * 512], PS[:, n], ACT.Sigmoid).then_inc(sgm_ready, 1)
            norm(3 * DEPTH, 3 * DEPTH, None)

        @block.vector
        def _(dve):
            steps = [0]

            def link(ins):
                steps[0] += 1
                ins.then_inc(dve_step, 1)
                dve.wait_ge(dve_step, steps[0])

            def mean_square(r):
                dve.wait_ge(sumsq, TB * (r + 1))
                dve.tensor_scalar(ssq, ssq, 1.0 / D, EPS, ALU.mult, ALU.add).then_inc(mean_sq, 1)
                dve.wait_ge(rms, r + 1)
                link(dve.reciprocal(rstd, rstd))

            def split(tile):
                dve.wait_ge(part_hi[tile.part], tile.count + 1)
                dve.tensor_tensor(low[tile.part][:, tile.count % 2], raw(tile.slab, tile.part),
                                  high[tile.part][:, tile.count % 2].bitcast(F32), ALU.subtract).then_inc(part_lo[tile.part], 1)

            def norm(r, gain):
                mean_square(r)
                for tb in range(TB):
                    dve.tensor_scalar(xn[:, tb], xres[:, tb], rstd[:, tb:tb + 1], None, ALU.mult).then_inc(xn_ready, 1)
                for k in range(KT):
                    dve.wait_ge(hT_hi, KT * r + k // 2 * 2 + 2)
                    dve.scalar_tensor_tensor(hTl[:, k], PS[:, k // 2, (k % 2) * SEQ:(k % 2 + 1) * SEQ], gain[:, k:k + 1],
                                             hTh[:, k].bitcast(F32), ALU.mult, ALU.subtract).then_inc(hT_lo, 1)

            def bc(col, n):
                return col.unsqueeze(2).broadcast_to([P, col.shape[1], n])

            dve.wait_ge(in_x, 16)
            dve.wait_ge(in_v, 16)
            dve.wait_ge(in_c, 16)
            for L in range(DEPTH):
                V = vec[:, L]
                for k in range(4):
                    split(projection_tile(L, "in", k))
                norm(3 * L, V[:, C_GMIX:C_GMIX + KT])
                if L == 0:
                    dve.wait_ge(p_hi, 1)
                    dve.tensor_tensor(pTl[:], praw[:], pTh[:].bitcast(F32), ALU.subtract).then_inc(p_lo, 1)
                dve.tensor_scalar(bq8, V[:, C_BIN + T_Q:C_BIN + T_K], HD ** -0.5, None, ALU.mult).then_inc(bq_ready, 1)
                dve.memset(fpad[:, :, 0:1], 0.0).then_inc(dve_step, 1)
                steps[0] += 1
                dve.wait_ge(dve_step, steps[0])
                for m in range(RW_TILES):
                    split(projection_tile(L, "in", m + 4))
                    dve.wait_ge(in_evac, IN_TILES * L + m + 1)
                    link(dve.tensor_tensor(fm[:, m], fpad[:, m, 0:SEQ], fpad[:, m, 1:SEQ + 1], ALU.subtract))
                    ins = dve.scalar_tensor_tensor(fm[:, m], fm[:, m], V[:, C_MU + m:C_MU + m + 1], fpad[:, m, 1:SEQ + 1], ALU.mult, ALU.add)
                ins.then_inc(mixed, 1)
                for m in range(RW_TILES + 4, IN_TILES):
                    split(projection_tile(L, "in", m))
                sinks = V[:, C_SINK:C_SINK + NH]
                for tb in range(TB):
                    dve.wait_ge(sc_ps, TB * L + tb + 1)
                    nk = P * (tb + 1)
                    lg = lg1 if tb else lg0
                    dist = cst[:, K_DIST1:K_DIST1 + nk] if tb else cst[:, K_DIST0:K_DIST0 + nk]
                    for h in range(NH):
                        bank = 4 + h // 2 if tb else 1 + h // 4
                        at = (h % 2) * 2 * P if tb else (h % 4) * P
                        ins = dve.scalar_tensor_tensor(lg[:, h], dist, -SLOPES[h], PS[:, bank, at:at + nk], ALU.mult, ALU.add)
                    link(ins)
                    c = slice(tb * NH, (tb + 1) * NH)
                    link(dve.tensor_reduce(amax[:, c], lg[:], AX.X, ALU.max))
                    link(dve.tensor_tensor(amax[:, c], amax[:, c], sinks, ALU.max))
                    dve.tensor_scalar(anm[:, c], amax[:, c], -1.0, None, ALU.mult)
                    dve.tensor_tensor(asink[:, c], sinks, amax[:, c], ALU.subtract).then_inc(nm_ready, 1)
                for tb in range(TB):
                    c = slice(tb * NH, (tb + 1) * NH)
                    dve.wait_ge(p_ready, TB * L + tb + 1)
                    link(dve.tensor_tensor(aden[:, c], arow[:, c], asink[:, c], ALU.add))
                    link(dve.reciprocal(aden[:, c], aden[:, c]))
                    dve.wait_ge(pv_ps, TB * L + tb + 1)
                    dve.tensor_tensor(ao[:, tb].rearrange("p (h d) -> p h d", h=NH),
                                      PS[:, 0 if tb else 3].rearrange("p (h d) -> p h d", h=NH),
                                      bc(aden[:, c], HD), ALU.mult).then_inc(ao_ready, 1)
                dve.wait_ge(ao_ssq, TB * (L + 1))
                dve.tensor_scalar(assq, assq, 1.0 / 512, EPS, ALU.mult, ALU.add).then_inc(ao_ms, 1)
                dve.wait_ge(ao_rms, L + 1)
                link(dve.reciprocal(arstd, arstd))
                for tb in range(TB):
                    ins = dve.tensor_scalar(ao[:, tb], ao[:, tb], arstd[:, tb:tb + 1], None, ALU.mult)
                ins.then_inc(ao_normed, 1)
                for k in range(4):
                    dve.wait_ge(yTa_hi, 4 * L + k // 2 * 2 + 2)
                    ins = dve.scalar_tensor_tensor(hTl[:, k], PS[:, 4 + k // 2, (k % 2) * SEQ:(k % 2 + 1) * SEQ], V[:, C_AN + k:C_AN + k + 1],
                                                   hTh[:, k].bitcast(F32), ALU.mult, ALU.subtract)
                ins.then_inc(yTa_ready, 1)
                for t in range(4):
                    ins = dve.tensor_scalar(kk[:, t], fm[:, 4 + t], V[:, C_KK + t:C_KK + t + 1], None, ALU.mult)
                link(ins)
                dve.tensor_tensor(sqk[:], kk[:], kk[:], ALU.mult).then_inc(sqk_ready, 1)
                dve.wait_ge(gates_ready, 2 * L + 1)
                for t in range(4):
                    ins = dve.tensor_tensor_scan(csum[:, t], cst[:, K_RESET:K_RESET + SEQ], sw[:, t], 0.0, ALU.mult, ALU.add)
                ins.then_inc(csum_ready, 1)
                dve.wait_ge(csum_ready, 2 * L + 1)
                dve.tensor_tensor(cprev[:], csum[:], sw[:], ALU.subtract).then_inc(csum_ready, 1)
                dve.wait_ge(kss_ps, L + 1)
                dve.tensor_scalar(rnorm[:], PS[:, 6:8].rearrange("p a (b c) -> p (a b) c", b=2), 1e-24, None, ALU.max).then_inc(kss_max, 1)
                dve.wait_ge(gates_ready, 2 * L + 2)
                for t in range(4):
                    ins = dve.tensor_scalar(kmod[:, t], avec[:, t], 1.0, V[:, C_KA + t:C_KA + t + 1], ALU.subtract, ALU.mult)
                link(ins)
                link(dve.scalar_tensor_tensor(kmod[:], kmod[:], 1.0, fm[:, 4:8], ALU.add, ALU.mult))
                for t in range(4):
                    ins = dve.scalar_tensor_tensor(rkprod[:, t], fm[:, t], V[:, C_RK + t:C_RK + t + 1], kmod[:, t], ALU.mult, ALU.mult)
                ins.then_inc(rk_ready, 1)
                dve.wait_ge(knorm, L + 1)
                link(dve.reciprocal(rnorm[:], rnorm[:]))
                link(dve.tensor_tensor(kk[:], kk[:], rnorm[:], ALU.mult))
                link(dve.tensor_tensor(bvec[:], kk[:], avec[:], ALU.mult))
                dve.wait_ge(decay_ready, 3 * (L + 1))
                v8 = lambda t: t[:].rearrange("p a (b c) -> p (a b) c", b=TB)
                dve.tensor_tensor(bt[:], bvec[:], winv[:], ALU.mult)
                dve.tensor_tensor(kt[:], kmod[:], winv[:], ALU.mult).then_inc(bkt_ready, 1)
                arv = ar[:].rearrange("p a b c d -> p (a b) c d")
                dve.scalar_tensor_tensor(arv[:, :, 0], v8(kk), -1.0, v8(wprev), ALU.mult, ALU.mult)
                dve.tensor_tensor(arv[:, :, 1], fm[:, 0:4].rearrange("p a (b c) -> p (a b) c", b=TB), v8(wcum), ALU.mult).then_inc(bkt_ready, 1)
                dve.wait_ge(bonus_ps, L + 1)
                dve.tensor_tensor(bonus_v[:], PS[:, 6:8].rearrange("p a (b c) -> p (a b) c", b=2), fm[:, 8:12], ALU.mult).then_inc(bonus_ready, 1)
                pm = cst[:, K_PMASK:K_PMASK + 256].unsqueeze(1).broadcast_to([P, 2, 256])
                for n in range(16):
                    dve.wait_ge(prod_ps, 16 * L + n + 1)
                    dve.tensor_tensor(prods[:, n].rearrange("p (a b) -> p a b", a=2),
                                      PS[:, 6 + n % 2].rearrange("p (a b) -> p a b", a=2), pm, ALU.mult).then_inc(prod_ready, 1)
                for lv in range(LEVELS):
                    for g in range(4):
                        gs = slice(4 * g, 4 * g + 4)
                        four = lambda a: a.rearrange("p (a b) -> p a b", a=4)
                        if lv == 0:
                            dve.wait_ge(m_ps, 4 * LEVELS * L + g + 1)
                            dve.wait_ge(mt_ready, LEVELS * L + 1)
                            eye = ident.unsqueeze(1).broadcast_to([P, 4, P])
                            dve.tensor_tensor(XT[:, gs], Mt[:, 0, gs], eye, ALU.add)
                            dve.tensor_tensor(X[:, gs], four(PS[:, g]), eye, ALU.add).then_inc(xm_ready, 1)
                            continue
                        dve.wait_ge(xpt_ps, 4 * ((LEVELS - 1) * L + lv - 1) + g + 1)
                        dve.wait_ge(xm_ready, 4 * (LEVELS * L + lv - 1) + g + 1)
                        if lv < LEVELS - 1:
                            dve.tensor_tensor(XT[:, gs], XT[:, gs], four(PS[:, g]), ALU.add)
                            dve.tensor_tensor(X[:, gs], X[:, gs], four(PS[:, 4 + g]), ALU.add).then_inc(xm_ready, 1)
                        else:
                            dve.tensor_tensor(XT[:, gs], XT[:, gs], four(PS[:, g]), ALU.add).then_inc(xm_ready, 1)
                dve.memset(rhs[:], 0.0)
                dve.memset(sa[:], 0.0)
                link(dve.memset(ST[:], 0.0))
                for c in range(NCHUNK):
                    o = 64 * (c % 2)
                    dve.wait_ge(rhs_ps, NCHUNK * L + c + 1)
                    dve.tensor_copy(rhs[o:o + 64], PS[o:o + 64, 0]).then_inc(rhs_ready, 1)
                    if c == NCHUNK - 1:
                        continue
                    dve.wait_ge(st_ps, (NCHUNK - 1) * L + c + 1)
                    for b in range(2):
                        hr = slice(64 * b, 64 * b + 64)
                        src = PS[hr, 3, 0:4 * HD].rearrange("p (a b) -> p a b", a=4)
                        wend = wcum[hr, :, 64 * c + 63:64 * c + 64].broadcast_to([64, 4, HD])
                        state = ST[hr, c % 2, :, hr]
                        if c:
                            link(dve.tensor_tensor(state, ST[hr, (c - 1) % 2, :, hr], src, ALU.add))
                            ins = dve.tensor_tensor(state, state, wend, ALU.mult)
                        else:
                            ins = dve.tensor_tensor(state, src, wend, ALU.mult)
                    ins.then_inc(st_ready, 1)
                dve.wait_ge(y_ready, NCHUNK * (L + 1))
                y16 = ytok[:].rearrange("p a (h d) -> p (a h) d", h=NH)
                yc16 = yc[:].rearrange("p a (h d) -> p (a h) d", h=NH)
                link(dve.tensor_reduce(gmean, y16, AX.X, ALU.add))
                link(dve.tensor_scalar(gmean, gmean, -1.0 / HD, None, ALU.mult))
                dve.tensor_tensor(yc16, y16, bc(gmean, HD), ALU.add).then_inc(yc_ready, 1)
                dve.wait_ge(ysq_ready, L + 1)
                link(dve.tensor_reduce(gvar, ysq[:].rearrange("p a (h d) -> p (a h) d", h=NH), AX.X, ALU.add))
                dve.tensor_scalar(gvar, gvar, 1.0 / HD, LNX_EPS, ALU.mult, ALU.add).then_inc(yv_ready, 1)
                dve.wait_ge(ystd, L + 1)
                link(dve.reciprocal(gvar, gvar))
                dve.tensor_tensor(yc16, yc16, bc(gvar, HD), ALU.mult).then_inc(yn_ready, 1)
                for k in range(4):
                    split(projection_tile(L, "out", k))
                dve.wait_ge(yT_ps, L + 1)
                for t in range(4):
                    ins = dve.tensor_scalar(ytmp[:, t], PS[:, 4 + t // 2, (t % 2) * SEQ:(t % 2 + 1) * SEQ],
                                            V[:, C_LNW + t:C_LNW + t + 1], V[:, C_LNB + t:C_LNB + t + 1], ALU.mult, ALU.add)
                link(ins)
                link(dve.tensor_tensor(ytmp[:], ytmp[:], bonus_v[:], ALU.add))
                dve.wait_ge(g_ready, L + 1)
                dve.tensor_tensor(ytmp[:], ytmp[:], gT[:], ALU.mult).then_inc(yg_ready, 1)
                dve.wait_ge(yTr_hi, L + 1)
                dve.tensor_tensor(hTl[:, 4:8], ytmp[:], hTh[:, 4:8].bitcast(F32), ALU.subtract).then_inc(yTr_ready, 1)
                for k in range(4, KT):
                    split(projection_tile(L, "out", k))
                dve.wait_ge(part_used[1], projection_tile(L, "out", KT - 1).count + 1)
                for n in range(4):
                    s = slice((n % 2) * 512, (n % 2 + 1) * 512)
                    ins = dve.tensor_tensor(xres[:, n // 2, s], xres[:, n // 2, s], PS[:, n], ALU.add)
                ins.then_inc(x_ready, 1)
                dve.wait_ge(x_ready, 3 * L + 1)
                for k in range(4):
                    split(projection_tile(L, "wq", k))
                norm(3 * L + 1, V[:, C_GFFN:C_GFFN + KT])
                for k in range(4, HC):
                    split(projection_tile(L, "wq", k))
                def split_tile(part, count, parity, place, half):
                    dve.wait_ge(part_hi[part], count + 1)
                    dve.tensor_tensor(low[part][:, parity], ring[:, place, half * D:(half + 1) * D],
                                      high[part][:, parity].bitcast(F32), ALU.subtract).then_inc(part_lo[part], 1)

                def top16(rows, n, values, vals, idx, scratch=None):
                    for r in range(rows):
                        ins = dve.max(vals[:, r, 0:8], values(r))
                    link(ins)
                    for r in range(rows):
                        dve.max_index(idx[:, r, 0:8], vals[:, r, 0:8], values(r))
                        ins = dve.match_replace(values(r), vals[:, r, 0:8], values(r), -3.0e38)
                    link(ins)
                    for r in range(rows):
                        ins = dve.max(vals[:, r, 8:16], values(r))
                    link(ins)
                    for r in range(rows):
                        ins = dve.max_index(idx[:, r, 8:16], vals[:, r, 8:16], values(r))
                    link(ins)

                for tb in range(TB):
                    dve.wait_ge(psc_ready, 8 * L + 4 * (tb + 1))
                    top16(HC, NSUB, lambda r: sc[:, tb, r], topv, topi)
                    link(dve.tensor_copy(topf[:], topi[:]))
                    tv = topv[:].rearrange("p (h c) k -> p h c k", c=2)
                    tf = topf[:].rearrange("p (h c) k -> p h c k", c=2)
                    link(dve.tensor_tensor(cand[:].rearrange("p h (a b) -> p h a b", a=TOPK),
                                           tv[:, :, 0].unsqueeze(3).broadcast_to([P, PH, TOPK, TOPK]),
                                           tv[:, :, 1].unsqueeze(2).broadcast_to([P, PH, TOPK, TOPK]), ALU.add))
                    top16(PH, TOPK * TOPK, lambda r: cand[:, r], bestv, bestc)
                    bflat = bestc[:].rearrange("p a b -> p (a b)")
                    dve.tensor_scalar(bestd[:, 0], bflat, 4, None, ALU.logical_shift_right)
                    link(dve.tensor_scalar(bestd[:, 1], bflat, 15, None, ALU.bitwise_and))
                    link(dve.tensor_copy(bestf[:].rearrange("p c a b -> p c (a b)"), bestd[:]))
                    for c in range(2):
                        link(dve.tensor_tensor(onehot[:], bestf[:, c].unsqueeze(3).broadcast_to([P, PH, TOPK, TOPK]),
                                               iota16.unsqueeze(1).unsqueeze(1).broadcast_to([P, PH, TOPK, TOPK]), ALU.is_equal))
                        link(dve.tensor_tensor(picked[:], onehot[:], tf[:, :, c].unsqueeze(2).broadcast_to([P, PH, TOPK, TOPK]), ALU.mult))
                        link(dve.tensor_reduce(slot[:, c, tb].rearrange("p (a b) -> p a b", a=PH), picked[:], AX.X, ALU.add))
                    s3 = slot[:, 2, tb].rearrange("p (a b) -> p a b", a=PH)
                    dve.tensor_tensor(s3, bestv[:], bestv[:, :, 0:1].broadcast_to([P, PH, TOPK]), ALU.subtract).then_inc(bd_ready, 1)
                    dve.wait_ge(bexp_ready, TB * L + tb + 1)
                    link(dve.tensor_reduce(gsum, s3, AX.X, ALU.add))
                    link(dve.reciprocal(gsum, gsum))
                    dve.tensor_tensor(s3, s3, bc(gsum, TOPK), ALU.mult).then_inc(slot_ready, 1)
                dve.wait_ge(slot_T, L + 1)
                g0 = NGROUPS * NQ * L

                def one_hots(g, group, b, chunk):
                    if L or not isinstance(g, int) or g > 1:
                        dve.wait_ge(spread_ps, g0 - 1 + g)

                    def column(c, n):
                        return sT[:, c, bass.ds(GROUP * group, GROUP)].unsqueeze(2).broadcast_to([P, GROUP, n])

                    dve.tensor_tensor(hot2[:, b], iota[:, QT * chunk:QT * (chunk + 1)].unsqueeze(1).broadcast_to([P, GROUP, QT]),
                                      column(1, QT), ALU.is_equal).then_inc(hot2_made, 1)
                    dve.tensor_tensor(hot1[:, b], iota.unsqueeze(1).broadcast_to([P, GROUP, NSUB]), column(0, NSUB), ALU.is_equal)
                    dve.wait_ge(hot2_made, g0 + 1 + g)
                    dve.tensor_tensor(hot2[:, b], hot2[:, b], column(2, QT), ALU.mult).then_inc(hots_made, 1)

                def apply_gates(g, group, b, chunk):
                    dve.wait_ge(spread_ps, g0 + 1 + g)
                    acts = GA[:, chunk % 2 * QT:chunk % 2 * QT + QT, bass.ds(GROUP * group, GROUP)]
                    dve.tensor_tensor(acts, acts, PS[:, 4 + b, 0:GROUP * QT].rearrange("p (t i) -> p i t", t=GROUP), ALU.mult).then_inc(gated, 1)

                def split_w(s, place, j):
                    dve.wait_ge(w_hi, NSUB * L + 1 + s)
                    dve.tensor_tensor(WL[:, j % 2:j % 2 + 1], GA[:, bass.ds(place, 1)], WH[:, j % 2:j % 2 + 1].bitcast(F32), ALU.subtract).then_inc(w_lo, 1)

                def split_v(s, j):
                    split_tile(1, v0[L] + s, (v0[L] + j) % 2, j % RING, 1)

                def split_vv(n, j):
                    split_tile(1, v0[L] + HELD + n, (v0[L] + j) % 2, j // 2 % RING, j % 2)

                one_hots(0, 0, 0, 0)
                dve.wait_ge(ga_ready, NSUB * L + QT)

                def first_chunk(g, b, last=False):
                    one_hots(g + 1, g + 1, (b + 1) % 2, int(last))
                    apply_gates(g, g, b, 0)

                for b in range(2):
                    first_chunk(b, b)
                with dve.Fori(1, NGROUPS // 2 - 1) as i:
                    for b in range(2):
                        first_chunk(2 * i + b, b)
                for b in range(2):
                    first_chunk(NGROUPS - 2 + b, b, b == 1)
                split_v(0, 0)
                split_w(0, 0, 0)

                def step(s, j, group, chunk, last=False):
                    split_v(s + 1, j + 1)
                    one_hots(s + (NGROUPS + 1), group + 1, (j + 1) % 2, chunk + last)
                    apply_gates(s + NGROUPS, group, j % 2, chunk)
                    split_w(s + 1, s + 1, j + 1)

                for chunk in (1, 2):
                    s0 = QT * (chunk - 1)
                    dve.wait_ge(ga_ready, NSUB * L + QT * (chunk + 1))
                    with dve.Fori(0, QT // RING - 1) as i:
                        for j in range(RING):
                            step(RING * i + (j + s0), j, RING * i + j, chunk)
                    if chunk == 1:
                        for j in range(QT - RING, QT):
                            step(j, j, j, 1, j == QT - 1)
                for s in range(HELD - RING, HELD):
                    if s < HELD - 1:
                        step(s, s % RING, s % QT, 2)
                    else:
                        split_vv(0, 0)
                        one_hots(s + NGROUPS + 1, s % QT + 1, 0, 3)
                        apply_gates(s + NGROUPS, s % QT, 1, 2)
                        split_w(s + 1, 0, 0)
                dve.wait_ge(ga_ready, NSUB * (L + 1))

                def last_chunk(n, j, last=False):
                    split_vv(n + 1, j + 1)
                    if not last:
                        one_hots(n + (HELD + NGROUPS + 1), n + 1, (j + 1) % 2, 3)
                    apply_gates(n + (HELD + NGROUPS), n, j % 2, 3)
                    split_w(n + (HELD + 1), n + 1, j + 1)

                with dve.Fori(0, QT // 8 - 1) as i:
                    for j in range(8):
                        last_chunk(8 * i + j, j)
                for j in range(8):
                    last_chunk(QT - 8 + j, j, j == 7)
                with dve.Fori(QT // 8, HELD // 8 - 1) as i:
                    for j in range(8):
                        split_vv(8 * i + (j + 1), j + 1)
                        split_w(8 * i + (j + HELD + 1), 8 * i + (j + 1), j + 1)
                for j in range(7):
                    split_vv(HELD - 8 + j + 1, j + 1)
                    split_w(NSUB - 8 + j + 1, HELD - 8 + j + 1, j + 1)
                for k in range(4):
                    split(projection_tile(L, "ple", k))
                dve.wait_ge(peer_ps, L + 1)
                for n in range(4):
                    s = slice((n % 2) * 512, (n % 2 + 1) * 512)
                    ins = dve.tensor_tensor(xres[:, n // 2, s], xres[:, n // 2, s], PS[:, n], ALU.add)
                ins.then_inc(x_ready, 1)
                dve.wait_ge(x_ready, 3 * L + 2)
                norm(3 * L + 2, V[:, C_GPLE:C_GPLE + KT])
                for k in range(4, 10):
                    split(projection_tile(L, "ple", k))
                dve.wait_ge(part_used[1], projection_tile(L, "ple", KT + 1).count + 1)
                dve.wait_ge(sgm_ready, 4 * (L + 1))
                for n in range(4):
                    s = slice((n % 2) * 512, (n % 2 + 1) * 512)
                    ins = dve.tensor_tensor(ptmp[:, n // 2, s], sgm[:, n // 2, s], PS[:, 4 + n], ALU.mult)
                link(ins)
                dve.tensor_tensor(xres[:], xres[:], ptmp[:], ALU.add).then_inc(x_ready, 1)
                dve.wait_ge(x_ready, 3 * (L + 1))
                dve.engine_nop().then_inc(ple_sum, 1)
            mean_square(3 * DEPTH)
            dve.wait_ge(in_g, 16)
            for tb in range(TB):
                dve.scalar_tensor_tensor(obuf[:, tb], xres[:, tb], rstd[:, tb:tb + 1], gfin[:], ALU.mult, ALU.mult).then_inc(out_ready, 1)

        @block.tensor
        def _(pe):
            mm = pe.matmul

            def norm(r):
                pe.wait_ge(xn_ready, TB * (r + 1))
                for k in range(KT):
                    for tb in range(TB):
                        ins = pe.transpose(PS[:, k // 2, (k % 2) * SEQ + tb * P:(k % 2) * SEQ + (tb + 1) * P], xn[:, tb, k * P:(k + 1) * P], ident)
                    if k % 2:
                        ins.then_inc(xT_ps, 1)
                pe.wait_ge(hT_lo, KT * (r + 1))

            def channel_rows(tile, dst):
                pe.wait_ge(part_lo[tile.part], tile.count + 1)
                b, n = tile.count % 2, 0
                for k in range(KT):
                    ks = slice(k * P, (k + 1) * P)
                    for w, h in ((high, hTh), (high, hTl), (low, hTh)):
                        ins = mm(dst, w[tile.part][:, b, ks], h[:, k], start=n == 0, stop=n == 3 * KT - 1)
                        n += 1
                ins.then_inc(part_used[tile.part], 1)

            def token_rows(L, stage, k0, hi, lo, ktiles, bank0):
                for k in range(ktiles):
                    tile = projection_tile(L, stage, k0 + k)
                    pe.wait_ge(part_lo[tile.part], tile.count + 1)
                    b = tile.count % 2
                    for tb in range(TB):
                        for c, (h, w) in enumerate(((hi, high), (hi, low), (lo, high))):
                            for s in range(2):
                                ins = mm(PS[:, bank0 + 2 * tb + s], h[:, k, tb * P:(tb + 1) * P], w[tile.part][:, b, s * 512:(s + 1) * 512],
                                         start=k == 0 and c == 0, stop=k == ktiles - 1 and c == 2)
                    ins.then_inc(part_used[tile.part], 1)

            pe.wait_ge(in_c, 16)
            pe.wait_ge(zeros_made, 1)
            for L in range(DEPTH):
                V = vec[:, L]
                norm(3 * L)
                for m in range(IN_TILES):
                    if m >= 4:
                        pe.wait_ge(in_evac, IN_TILES * L + m - 3)
                    channel_rows(projection_tile(L, "in", m), PS[:, 4 + m % 4, 0:SEQ])
                pe.wait_ge(in_evac, IN_TILES * (L + 1))
                for tb in range(TB):
                    ins = pe.transpose(PS[:, 0, tb * P:(tb + 1) * P], aT[:, T_V - T_Q, tb * P:(tb + 1) * P], ident)
                ins.then_inc(vtA_ps, 1)
                for tb in range(TB):
                    nk = P * (tb + 1)
                    for h in range(NH):
                        r = slice(64 * (h // 4), 64 * (h // 4) + 64)
                        bank = 4 + h // 2 if tb else 1 + h // 4
                        at = (h % 2) * 2 * P if tb else (h % 4) * P
                        ins = mm(PS[:, bank, at:at + nk], aT[r, h % 4, tb * P:(tb + 1) * P], aT[r, T_K - T_Q, 0:nk], start=True, stop=True)
                    ins.then_inc(sc_ps, 1)
                for tb in range(TB):
                    pe.wait_ge(p_ready, TB * L + tb + 1)
                    for h in range(NH):
                        for s in range(tb + 1):
                            i = h * (tb + 1) + s
                            bank = (4 if tb else 1) + i // 4
                            ins = pe.transpose(PS[:, bank, (i % 4) * P:(i % 4 + 1) * P], (lg1 if tb else lg0)[:, h, s * P:(s + 1) * P], ident)
                            if i % 4 == 3:
                                ins.then_inc(pT_ps, 1)
                for tb in range(TB):
                    pe.wait_ge(pT_ready, 6 * L + (6 if tb else 2))
                    pe.wait_ge(vtA_ready, L + 1)
                    for h in range(NH):
                        for s in range(tb + 1):
                            ins = mm(PS[:, 0 if tb else 3, h * HD:(h + 1) * HD], PT1[:, h, s] if tb else PT0[:, h],
                                     vtA[:, s, HD * (h // 4):HD * (h // 4 + 1)], start=s == 0, stop=s == tb)
                    ins.then_inc(pv_ps, 1)
                pe.wait_ge(ao_normed, L + 1)
                for k in range(4):
                    for tb in range(TB):
                        ins = pe.transpose(PS[:, 4 + k // 2, (k % 2) * SEQ + tb * P:(k % 2) * SEQ + (tb + 1) * P], ao[:, tb, k * P:(k + 1) * P], ident)
                    if k % 2:
                        ins.then_inc(aoT_ps, 1)
                pe.wait_ge(filled[S_LORA % RING], 16 * fills(L, S_LORA))
                w = ring[:, S_LORA % RING, :]
                pe.wait_ge(yTa_ready, L + 1)
                pe.wait_ge(lora_in, 2 * (L + 1))
                for t in range(4):
                    ins = mm(PS[:, t // 2, (t % 2) * SEQ:(t % 2 + 1) * SEQ], w[0:64, t * P:(t + 1) * P], xw_t[0:64], start=True, stop=True)
                ins.then_inc(lora_ps, 1)
                for t in range(4):
                    ins = mm(PS[:, 2 + t // 2, (t % 2) * SEQ:(t % 2 + 1) * SEQ], w[64:128, t * P:(t + 1) * P], fm[64:128, T_LORA], start=True, stop=True)
                ins.then_inc(lora_ps, 1)
                for t in range(4):
                    dst = PS[:, 4 + t // 2, (t % 2) * SEQ:(t % 2 + 1) * SEQ]
                    mm(dst, w[:, 512 + t * P:512 + (t + 1) * P], xg_s[:, 0], start=True, stop=False)
                    ins = mm(dst, w[0:32, 1024 + t * P:1024 + (t + 1) * P], xg_s[0:32, 1], start=False, stop=True)
                ins.then_inc(lora_ps, 1)
                pe.wait_ge(sqk_ready, L + 1)
                for n in range(2):
                    ins = mm(PS[:, 6 + n], ones2, sqk[:, 2 * n:2 * n + 2].rearrange("p a b -> p (a b)"), start=True, stop=True)
                ins.then_inc(kss_ps, 1)
                pe.wait_ge(kss_max, L + 1)
                pe.wait_ge(rk_ready, L + 1)
                for n in range(2):
                    ins = mm(PS[:, 6 + n], ones2, rkprod[:, 2 * n:2 * n + 2].rearrange("p a b -> p (a b)"), start=True, stop=True)
                ins.then_inc(bonus_ps, 1)
                pe.wait_ge(gates_ready, 2 * (L + 1))
                pe.wait_ge(g_ready, L + 1)
                for n, src in enumerate((fm[:, 8:12], bt, kt)):
                    if n == 1:
                        pe.wait_ge(bkt_ready, 2 * L + 1)
                    for tb in range(TB):
                        for t in range(4):
                            ins = pe.transpose(PS[:, 2 * n + tb, t * P:(t + 1) * P], src[:, t, tb * P:(tb + 1) * P], ident)
                    ins.then_inc(tok_ps, 1)
                pe.wait_ge(bkt_ready, 2 * (L + 1))
                pe.wait_ge(bonus_ready, L + 1)
                for n in range(16):
                    tb, h = n // NH, n % NH
                    r = slice(64 * (h % 2), 64 * (h % 2) + 64)
                    if n >= 2:
                        pe.wait_ge(prod_ready, 16 * L + n - 1)
                    rhs2 = ar[r, h // 2, tb].rearrange("p a b -> p (a b)")
                    mm(PS[:, 6 + n % 2, 0:256], bt[r, h // 2, tb * P:(tb + 1) * P], rhs2, start=True, stop=True)
                    mm(PS[:, 6 + n % 2, 256:512], kt[r, h // 2, tb * P:(tb + 1) * P], rhs2, start=True, stop=True).then_inc(prod_ps, 1)
                pe.wait_ge(tok_ready, 3 * (L + 1))
                pe.wait_ge(prod_ready, 16 * (L + 1))
                for lv in range(LEVELS):
                    pe.wait_ge(mt_ready, LEVELS * L + lv + 1)
                    for g in range(4):
                        if lv:
                            pe.wait_ge(xm_ready, 4 * (LEVELS * L + lv - 1) + g + 1)
                        for n in range(4 * g, 4 * g + 4):
                            ins = mm(PS[:, g, (n % 4) * P:(n % 4 + 1) * P], Mt[:, lv % 2, n], X[:, n] if lv else ident, start=True, stop=True)
                        ins.then_inc(m_ps, 1)
                    if lv == 0:
                        continue
                    for g in range(4):
                        pe.wait_ge(px_ready, 4 * ((LEVELS - 1) * L + lv - 1) + g + 1)
                        for n in range(4 * g, 4 * g + 4):
                            if lv < LEVELS - 1:
                                mm(PS[:, 4 + g, (n % 4) * P:(n % 4 + 1) * P], XT[:, n], PX[:, n], start=True, stop=True)
                        for n in range(4 * g, 4 * g + 4):
                            ins = mm(PS[:, g, (n % 4) * P:(n % 4 + 1) * P], PX[:, n], XT[:, n], start=True, stop=True)
                        ins.then_inc(xpt_ps, 1)
                pe.wait_ge(xm_ready, 4 * LEVELS * (L + 1))
                for c in range(NCHUNK):
                    tb, o = c // 2, 64 * (c % 2)
                    rows, cols = slice(o, o + 64), slice(o, o + 64)
                    if c:
                        pe.wait_ge(st_ready, (NCHUNK - 1) * L + c)
                    for t in range(4):
                        if c:
                            mm(PS[rows, 0, t * P:(t + 1) * P], ar[:, t, tb, 0, cols], ST[:, (c - 1) % 2, t], start=True, stop=False)
                        for h in (2 * t, 2 * t + 1):
                            ins = mm(PS[rows, 0, h * HD:(h + 1) * HD], prods[:, tb * NH + h, 256 + o:256 + o + 64], vtok[:, tb, h * HD:(h + 1) * HD],
                                     start=c == 0, stop=c == 0 or h % 2 == 1)
                    ins.then_inc(rhs_ps, 1)
                    pe.wait_ge(rhs_ready, NCHUNK * L + c + 1)
                    for h in range(NH):
                        ins = mm(PS[rows, 1, h * HD:(h + 1) * HD], XT[:, tb * NH + h, cols], rhs[:, h * HD:(h + 1) * HD], start=True, stop=True)
                    ins.then_inc(sa_ps, 1)
                    pe.wait_ge(sa_ready, NCHUNK * L + c + 1)
                    if c < NCHUNK - 1:
                        for h in range(NH):
                            hr = slice(64 * (h % 2), 64 * (h % 2) + 64)
                            dst = PS[hr, 3, (h // 2) * HD:(h // 2 + 1) * HD]
                            mm(dst, btok[rows, tb, h * HD:(h + 1) * HD], sa[rows, h * HD:(h + 1) * HD], start=True, stop=False)
                            ins = mm(dst, ktok[rows, tb, h * HD:(h + 1) * HD], vtok[rows, tb, h * HD:(h + 1) * HD], start=False, stop=True)
                        ins.then_inc(st_ps, 1)
                    if c:
                        pe.wait_ge(y_ready, NCHUNK * L + c)
                    for t in range(4):
                        if c:
                            mm(PS[rows, 2, t * P:(t + 1) * P], ar[:, t, tb, 1, cols], ST[:, (c - 1) % 2, t], start=True, stop=False)
                        for h in (2 * t, 2 * t + 1):
                            dst = PS[rows, 2, h * HD:(h + 1) * HD]
                            mm(dst, prods[:, tb * NH + h, 128 + o:128 + o + 64], sa[:, h * HD:(h + 1) * HD], start=c == 0, stop=False)
                            ins = mm(dst, prods[:, tb * NH + h, 384 + o:384 + o + 64], vtok[:, tb, h * HD:(h + 1) * HD], start=False, stop=c == 0 or h % 2 == 1)
                    ins.then_inc(y_ps, 1)
                pe.wait_ge(yn_ready, L + 1)
                for t in range(4):
                    for tb in range(TB):
                        ins = pe.transpose(PS[:, 4 + t // 2, (t % 2) * SEQ + tb * P:(t % 2) * SEQ + (tb + 1) * P], yc[:, tb, t * P:(t + 1) * P], ident)
                ins.then_inc(yT_ps, 1)
                pe.wait_ge(yTr_ready, L + 1)
                token_rows(L, "out", 0, hTh, hTl, KT, 0)
                norm(3 * L + 1)
                for m in range(HC):
                    if m >= 4:
                        pe.wait_ge(q_ready, HC * L + m - 3)
                    channel_rows(projection_tile(L, "wq", m), PS[:, 4 + m % 4, 0:SEQ])
                pe.wait_ge(q_ready, HC * (L + 1))
                for n in range(8):
                    for j in range(4):
                        hc = 4 * (n % 4) + j
                        keys = V[:, C_KEYS + (hc % 2) * NSUB:C_KEYS + (hc % 2 + 1) * NSUB]
                        ins = mm(PS[:, n, j * P:(j + 1) * P], qT[:, hc, (n // 4) * P:(n // 4 + 1) * P], keys, start=True, stop=True)
                    ins.then_inc(psc_ps, 1)
                pe.wait_ge(psc_ready, 8 * (L + 1))
                for n in range(4):
                    mm(PS[:, n], zeros[:], cst[:, 0:512], start=True, stop=False, skip_group_check=True)
                g0 = NGROUPS * NQ * L

                def hidden(e, j):
                    pe.wait_ge(part_lo[0], u0[L] + 1 + e)
                    if L or not isinstance(e, int) or e > 1:
                        pe.wait_ge(ga_ready, NSUB * L - 1 + e)
                    b, n = (u0[L] + j) % 2, 0
                    for k in range(KT):
                        ks = slice(k * P, (k + 1) * P)
                        for u, h in ((UH, hTh), (UH, hTl), (UL, hTh)):
                            ins = mm(PS[:, 6 + j % 2, 0:SEQ], u[:, b, ks], h[:, k], start=n == 0, stop=n == 3 * KT - 1)
                            n += 1
                    ins.then_inc(part_used[0], 1)

                def spread(g, b):
                    pe.wait_ge(hots_made, g0 + 1 + g)
                    if L or not isinstance(g, int) or g > 1:
                        pe.wait_ge(gated, g0 - 1 + g)
                    for t in range(GROUP):
                        ins = mm(PS[:, 4 + b, t * QT:(t + 1) * QT], hot1[:, b, t], hot2[:, b, t], start=True, stop=True)
                    ins.then_inc(spread_ps, 1)

                def spend(e, j):
                    pe.wait_ge(part_lo[1], v0[L] + 1 + e)
                    pe.wait_ge(w_lo, NSUB * L + 1 + e)
                    b = (v0[L] + j) % 2
                    for tb in range(TB):
                        for w, v in ((WH, VH), (WH, VL), (WL, VH)):
                            for s in range(2):
                                ins = mm(PS[:, 2 * tb + s], w[:, j % 2, tb * P:(tb + 1) * P], v[:, b, s * 512:(s + 1) * 512],
                                         start=False, stop=False, skip_group_check=True)
                    ins.then_inc(part_used[1], 1)

                for e in range(4):
                    hidden(e, e)
                with pe.Fori(1, A_TOP // 4) as i:
                    for j in range(4):
                        hidden(4 * i + j, j)
                pe.wait_ge(slot_ready, TB * (L + 1))
                for c in range(3):
                    for tb in range(TB):
                        at = (c % 2) * SEQ + tb * P
                        ins = pe.transpose(PS[:, 4 + c // 2, at:at + P], slot[:, c, tb], ident)
                ins.then_inc(slot_ps, 1)
                for r in range(2):
                    hidden(A_TOP + r, r)
                    spread(r, r)
                with pe.Fori(1, (HELD - A_TOP) // 2) as i:
                    for j in range(2):
                        hidden(2 * i + (j + A_TOP), j)
                        spread(2 * i + j, j)
                with pe.Fori(0, HELD // 4) as i:
                    for j in range(4):
                        spread(4 * i + (j + NGROUPS), j % 2)
                        hidden(4 * i + (j + HELD), j)
                        spend(4 * i + j, j)
                with pe.Fori(HELD // 4, (HELD + QT) // 4) as i:
                    for j in range(4):
                        spread(4 * i + (j + NGROUPS), j % 2)
                        spend(4 * i + j, j)
                with pe.Fori((HELD + QT) // 4, NSUB // 4) as i:
                    for j in range(4):
                        spend(4 * i + j, j)
                for n in range(4):
                    ins = mm(PS[:, n], zeros[:], cst[:, 0:512], start=False, stop=True, skip_group_check=True)
                ins.then_inc(peer_ps, 1)
                norm(3 * L + 2)
                token_rows(L, "ple", 0, hTh, hTl, KT, 0)
                if L == 0:
                    pe.wait_ge(p_lo, 1)
                token_rows(L, "ple", KT, pTh[:, L], pTl[:, L], 2, 4)


def shape_constants():
    c = np.zeros((P, NCONST), np.float32)
    i = np.arange(P)
    s, t = i[:, None], i[None, :]
    same = s // CHUNK == t // CHUNK
    c[:, K_ID:K_ID + P] = s == t
    c[:, K_ONES:K_ONES + P] = s // HD == t // HD
    c[:, K_PMASK:K_PMASK + P] = same & (s < t)
    c[:, K_PMASK + P:K_PMASK + 2 * P] = same & (s <= t)
    for lv in range(LEVELS):
        bs, bt = s >> lv, t >> lv
        c[:, K_LMASK + lv * P:K_LMASK + (lv + 1) * P] = (bt % 2 == 1) & (bs == bt - 1)
    c[:, K_RESET:K_RESET + SEQ] = np.arange(SEQ)[None, :] % CHUNK != 0
    for k0, q0, nk in ((K_DIST0, 0, P), (K_DIST1, P, 2 * P)):
        q, key = q0 + i[:, None], np.arange(nk)[None, :]
        back = q // CHUNK - key // CHUNK
        c[:, k0:k0 + nk] = np.where((back >= 0) & (back <= 1), np.abs(q - key), 1e33)
    c[:, K_IOTA:K_IOTA + NSUB] = i[None, :]
    c[:, K_IOTA16:K_IOTA16 + TOPK] = np.arange(TOPK)[None, :]
    return c


def lay_out(a):
    f = np.float32
    A, RW = 768, 1824
    w_in, b_in = np.asarray(a["w_in"]), np.asarray(a["b_in"])
    q_order = np.concatenate([np.concatenate([np.arange(HD) + HD * t, np.arange(HD) + HD * (t + 4)]) for t in range(4)])

    def in_tiles(m):
        pad = np.zeros(m.shape[:-1] + (RW_TILES * P - RW,), f)
        return np.concatenate([m[..., A:A + RW], pad, m[..., q_order], m[..., 512:A]], -1)

    def column_slabs(w):
        n = w.shape[1] // P
        s = w.reshape(KT, P, n, P).transpose(2, 1, 0, 3).reshape(n, P, D)
        if n % 2:
            s = np.concatenate([s, np.zeros((1, P, D), f)])
        return s.reshape(-1, 2, P, D).transpose(0, 2, 1, 3).reshape(-1, P, SLABW)

    def row_slabs(w):
        return w.reshape(-1, 2, P, D).transpose(0, 2, 1, 3).reshape(-1, P, SLABW)

    def cols(v):
        return v.reshape(-1, P).T

    slabs, vecs, peer = [], [], []
    for L in range(DEPTH):
        g = lambda n: np.asarray(a[n])[L]
        lora = np.zeros((P, SLABW), f)
        lora[0:64, 0:512], lora[64:128, 0:512] = g("rwkv_w_up"), g("rwkv_a_up")
        lora[:, 512:1024], lora[0:32, 1024:1536] = g("rwkv_g_up")[0:P], g("rwkv_g_up")[P:]
        slabs.append(np.concatenate([column_slabs(in_tiles(w_in[L])), lora[None], row_slabs(g("w_out")), column_slabs(g("peer_wq")),
                                     row_slabs(g("ple_gate")), row_slabs(g("ple_proj"))]))
        mu = np.concatenate([g("rwkv_mu"), np.zeros(RW_TILES * P - RW, f)])
        v = [cols(g("norm_mix")), cols(g("norm_ffn")), cols(g("norm_ple")), cols(in_tiles(b_in[L])), cols(mu)]
        v += [cols(g("rwkv_" + n).reshape(-1)) for n in ("w0", "a0", "k_k", "k_a", "r_k", "lnx_w", "lnx_b")]
        v += [cols(g("attn_out_norm")), np.broadcast_to(g("attn_sinks")[None], (P, NH))]
        v += [g("peer_keys")[c].T for c in range(2)]
        vecs.append(np.concatenate(v, 1))
        u = g("peer_u").reshape(NSUB, NSUB, KT, P).transpose(1, 3, 2, 0).reshape(NSUB, P, D)
        t = g("peer_v").reshape(NSUB, NSUB, D).transpose(1, 0, 2)
        pairs = lambda m: m.reshape(-1, 2, P, D).transpose(0, 2, 1, 3).reshape(-1, P, SLABW)
        peer.append(np.concatenate([pairs(u[:HELD]), np.concatenate([u[HELD:], t[:HELD]], 2), pairs(t[HELD:])]))
    p = np.asarray(a["p"])[:, 0]
    return {
        "x": np.asarray(a["x"])[0].reshape(TB, P, D).transpose(1, 0, 2),
        "w_slabs": np.stack(slabs),
        "peer_slabs": np.stack(peer),
        "vecs": np.stack(vecs, 1),
        "consts": shape_constants(),
        "p_t": p.transpose(0, 2, 1).reshape(DEPTH, 2, P, SEQ).transpose(2, 0, 1, 3),
        "g_final": np.broadcast_to(np.asarray(a["norm_final"])[None], (P, D)),
    }


def kernel(**inputs):
    from concourse import bacc
    from concourse.bass_utils import run_bass_kernel_spmd

    nc = bacc.Bacc("TRN2", target_bir_lowering=False, num_devices=1)
    arrays, args = {}, []
    for name, v in lay_out(inputs).items():
        v = np.ascontiguousarray(v)
        arrays[f"in_{name}"] = v
        args.append(nc.dram_tensor(f"in_{name}", v.shape, mybir.dt.from_np(v.dtype), kind="ExternalInput").ap())
    out = nc.dram_tensor("out", (P, TB, D), F32, kind="ExternalOutput").ap()
    hybrid_encoder(nc, *args, out)
    r = run_bass_kernel_spmd(nc, [arrays], core_ids=[0])
    return r.results[0]["out"].transpose(1, 0, 2).reshape(1, SEQ, D)
```

```python
from contextlib import ExitStack

import numpy as np

import concourse.bass as bass
from concourse import mybir

F32 = mybir.dt.float32
F32R = mybir.dt.float32r
BF16 = mybir.dt.bfloat16
U32 = mybir.dt.uint32
ALU = mybir.AluOpType
ACT = mybir.ActivationFunctionType
AX = mybir.AxisListType

P = 128
DEPTH, SEQ, D = 2, 256, 1024
TB = SEQ // P
KT = D // P
CHUNK, HD, NH = 64, 64, 8
NCHUNK = SEQ // CHUNK
EPS, LNX_EPS = 1e-6, 64e-5
EXP_MINUS_HALF = float(np.exp(-0.5))
SLOPES = [float(2.0 ** (-8.0 * (h + 1) / NH)) for h in range(NH)]

RW_TILES, IN_TILES = 15, 21
QKV_TILES, T_K, T_V = 6, 4, 5
T_LORA, T_GATE = 12, 13

PH, TOPK, NSUB = 8, 16, 128
HC = 2 * PH
SLOTS = PH * TOPK
NQ = 4
QT = NSUB // NQ
HELD = 2 * QT
GROUP = 8
NGROUPS = SEQ // GROUP
A_FIRST, A_SECOND, A_TOP, A_LOOP = 16, 35, 38, 40

RING, SLABW = 4, 2048
S_IN, S_LORA, S_OUT, S_WQ, S_PEER, S_PLE, S_LAST, S_ALL = 0, 11, 12, 16, 24, 152, 156, 160
S_UV, S_VV = S_PEER + HELD // 2, S_PEER + HELD // 2 + HELD
DEEP = 4
N_PRE, N_ALL = 45, 311
POOL_ALL, DVE_V, DVE_ALL = NSUB + QT, NSUB - QT, N_ALL - NSUB - QT
C_UV, C_VV = HELD, 3 * HELD

C_GMIX, C_GFFN, C_GPLE, C_BIN, C_MU = 0, 8, 16, 24, 45
C_W0, C_A0, C_KK, C_KA, C_RK, C_LNW, C_LNB, C_AN, C_SINK, C_KEYS = 60, 64, 68, 72, 76, 80, 84, 88, 92, 100
NVEC = C_KEYS + 2 * NSUB
K_ID, K_ONES, K_PMASK, K_LMASK, K_RESET, K_DIST0, K_DIST1, K_IOTA, K_IOTA16 = 0, 128, 256, 512, 1280, 1536, 1664, 1920, 2048
NCONST = 2064
LEVELS = 6
PT_BANKS, AOT_BANKS = (3, 0, 1, 2, 3, 0), (3, 0)


def fills(layer, n):
    per_layer = S_ALL // RING - (1 if n % RING else 0)
    return layer * per_layer + n // RING + 1


class Tile:

    def __init__(self, layer, slab, half, count, low):
        self.layer, self.slab, self.half, self.count, self.low = layer, slab, half, count, low


def projection_tile(layer, stage, k):
    slab, first = {"in": (S_IN, 0), "out": (S_OUT, IN_TILES), "wq": (S_WQ, IN_TILES + KT), "ple": (S_PLE, N_PRE)}[stage]
    peer = stage == "ple"
    return Tile(layer, slab + k // 2, k % 2, layer * N_ALL + first + k + 2 * NSUB * peer, layer * DVE_ALL + first + k + DVE_V * peer)


def hybrid_encoder(nc, x, w_slabs, peer_slabs, vecs, consts, p_t, g_final, out):
    with ExitStack() as ctx:
        def sem(name):
            return ctx.enter_context(nc.semaphore(name))

        first = (nc.sbuf_base + 31) // 32 * 8

        def place(name, at, shape, dt=F32):
            return nc.alloc_sbuf_tensor_at(name, [P] + shape, dt, offset=4 * (first + at))

        xres = place("xres", 0, [TB, D])
        hTh = place("hTh", 2048, [KT, SEQ], F32R)
        hTl = place("hTl", 4096, [KT, SEQ], F32R)
        ring = place("ring", 6144, [RING, SLABW])
        cst = place("cst", 14336, [NCONST])
        vec = place("vec", 16400, [DEPTH, NVEC])
        pTh = place("pTh", 17120, [DEPTH, 2, SEQ], F32R)
        pTl = place("pTl", 18144, [DEPTH, 2, SEQ], F32R)
        stat = place("stat", 19168, [256])
        M = 19424
        high = place("high", M, [DEEP, D], F32R)
        low = place("low", M + DEEP * D, [DEEP, D], F32R)
        R = M + 8192
        zeros = place("zeros", R + 25088, [P])
        iota_half = place("iota_half", R + 25216, [NSUB], BF16)
        praw = place("praw", R + 24064, [DEPTH, 2, SEQ])
        xn = place("xn", R, [TB, D])
        gfin = place("gfin", R + 6144, [D])
        obuf = place("obuf", R + 8192, [TB, D])
        fpad = place("fpad", R + 2048, [RW_TILES, SEQ + 1])
        fm = place("fm", R + 5904, [RW_TILES, SEQ])
        prods = place("prods", R + 2048, [TB * NH, 512])
        sw = place("sw", M, [4, SEQ])
        csum = place("csum", M + 1024, [4, SEQ])
        cprev = place("cprev", M + 2048, [4, SEQ])
        winv = place("winv", M + 3072, [4, SEQ])
        wprev = place("wprev", M + 4096, [4, SEQ])
        kk = place("kk", M + 5120, [4, SEQ])
        sqk = place("sqk", M + 6144, [4, SEQ])
        kmod = place("kmod", M + 6144, [4, SEQ])
        rnorm = place("rnorm", M + 7168, [4, SEQ])
        bvec = place("bvec", M + 8192, [4, SEQ])
        rkprod = place("rkprod", M + 9216, [4, SEQ])
        Mt = place("Mt", M, [2, TB * NH, P])
        X = place("X", M + 4096, [TB * NH, P])
        XT = place("XT", R + 21504, [TB * NH, P])
        PX = place("PX", M + 8192, [TB * NH, P])
        ytok = place("ytok", R, [TB, 512])
        rhs = place("rhs", R + 1024, [512])
        sa = place("sa", R + 1536, [512])
        yc = place("yc", R + 2048, [TB, 512])
        ysq = place("ysq", R + 3072, [TB, 512])
        ytmp = place("ytmp", R + 4096, [4, SEQ])
        lg0 = place("lg0", R + 10240, [NH, P])
        lg1 = place("lg1", R + 11264, [NH, 2 * P])
        PT0 = place("PT0", R + 13312, [NH, P])
        PT1 = place("PT1", R + 14336, [NH, 2, P])
        wcum = place("wcum", R + 10240, [4, SEQ])
        ar = place("ar", R + 11264, [4, TB, 2, P])
        bt = place("bt", R + 13312, [4, SEQ])
        kt = place("kt", R + 14336, [4, SEQ])
        vtok = place("vtok", R + 15360, [TB, 512])
        btok = place("btok", R + 16384, [TB, 512])
        ktok = place("ktok", R + 17408, [TB, 512])
        avec = place("avec", R + 17408, [4, SEQ])
        bonus_v = place("bonus_v", R + 18432, [4, SEQ])
        gT = place("gT", R + 19456, [4, SEQ])
        aT = place("aT", R + 20480, [6, SEQ])
        ST = place("ST", R + 20480, [2, 4, P])
        vtA = place("vtA", R + 22016, [TB, P])
        ao = place("ao", R + 22272, [TB, 512])
        xw_t = place("xw_t", R + 23296, [SEQ])
        xg_s = place("xg_s", R + 23552, [2, SEQ])
        GA = place("GA", R, [HELD, SEQ])
        WH = place("WH", R + 16384, [2, SEQ], F32R)
        WL = place("WL", R + 16896, [2, SEQ], F32R)
        hot1 = place("hot1", R + 17408, [2, GROUP, NSUB], BF16)
        hot2 = place("hot2", R + 18432, [2, GROUP, 3, QT], BF16)
        is_i2 = place("is_i2", R + 19200, [2, GROUP, QT], BF16)
        gate_parts = place("gate_parts", R + 21536, [SEQ + GROUP, 3], BF16)
        gate_rest = place("gate_rest", R + 21952, [SEQ + GROUP])
        sT = place("sT", R + 19968, [3, SEQ + GROUP])
        qT = place("qT", R + 2048, [HC, SEQ])
        sc = place("sc", R + 12288, [TB, HC, NSUB])
        topv = place("topv", R + 16384, [HC, TOPK])
        topi = place("topi", R + 16640, [HC, TOPK], U32)
        topf = place("topf", R + 16896, [HC, TOPK])
        bestv = place("bestv", R + 17152, [PH, TOPK])
        bestc = place("bestc", R + 17280, [PH, TOPK], U32)
        bestd = place("bestd", R + 17408, [2, PH * TOPK], U32)
        bestf = place("bestf", R + 17664, [2, PH, TOPK])
        onehot = place("onehot", R + 17920, [PH, TOPK, TOPK])
        slot = place("slot", R + 20768, [3, TB, SLOTS])
        cand = place("cand", R + 21536, [PH, TOPK * TOPK])
        picked = place("picked", R + 21536, [PH, TOPK, TOPK])
        sgm = place("sgm", R + 2048, [TB, D])
        ptmp = place("ptmp", R + 4096, [TB, D])

        PS = ctx.enter_context(nc.psum_tensor("PS", [P, 8, 512], F32))

        ident = cst[:, K_ID:K_ID + P]
        ones2 = cst[:, K_ONES:K_ONES + P]
        iota = cst[:, K_IOTA:K_IOTA + NSUB]
        iota16 = cst[:, K_IOTA16:K_IOTA16 + TOPK]
        ssq, rstd = stat[:, 0:2], stat[:, 2:4]
        amax, anm, arow, asink, aden = (stat[:, 8 + 16 * i:24 + 16 * i] for i in range(5))
        gmean, gvar = stat[:, 96:112], stat[:, 112:128]
        assq, arstd = stat[:, 128:130], stat[:, 130:132]
        gsum = stat[:, 136:144]
        bq8 = stat[:, 144:148]
        minus_half, ahead = stat[:, 148:149], stat[:, 149:150]

        in_x0, in_x1, in_c, in_c2, in_v, in_p, in_g, p_hi, p_lo = (sem(n) for n in ("in_x0", "in_x1", "in_c", "in_c2", "in_v", "in_p", "in_g", "p_hi", "p_lo"))
        filled = [sem(f"filled{i}") for i in range(RING)]
        part_hi, low_dve, low_pool, part_used = (sem(n) for n in ("part_hi", "low_dve", "low_pool", "part_used"))
        zeros_made = sem("zeros_made")
        sumsq, rms, xn_ready, xT_ps, hT_hi, hT_lo = (sem(n) for n in ("sumsq", "rms", "xn_ready", "xT_ps", "hT_hi", "hT_lo"))
        x_ready = sem("x_ready")
        bq_ready, in_evac, mixed = (sem(n) for n in ("bq_ready", "in_evac", "mixed"))
        vtA_ps, vtA_ready, sc_ps, lg_made, nm_ready, p_ready = (sem(n) for n in ("vtA_ps", "vtA_ready", "sc_ps", "lg_made", "nm_ready", "p_ready"))
        pT_ps, pT_ready, pv_ps, ao_ready, ao_ssq, ao_ms, ao_rms, ao_normed, aoT_ps, yTa_hi, yTa_ready = (
            sem(n) for n in ("pT_ps", "pT_ready", "pv_ps", "ao_ready", "ao_ssq", "ao_ms", "ao_rms", "ao_normed", "aoT_ps", "yTa_hi", "yTa_ready"))
        lora_in, lora_ps, gates_ready, g_ready = (sem(n) for n in ("lora_in", "lora_ps", "gates_ready", "g_ready"))
        sqk_ready, kss_ps, kss_max, knorm, csum_ready, decay_ready = (
            sem(n) for n in ("sqk_ready", "kss_ps", "kss_max", "knorm", "csum_ready", "decay_ready"))
        rk_ready, bonus_ps, bonus_ready, bkt_ready, tok_ps, tok_ready = (
            sem(n) for n in ("rk_ready", "bonus_ps", "bonus_ready", "bkt_ready", "tok_ps", "tok_ready"))
        prod_ps, prod_ready, mt_ready, m_ps, xm_ready, px_ready, xpt_ps, x_ps, x_made = (
            sem(n) for n in ("prod_ps", "prod_ready", "mt_ready", "m_ps", "xm_ready", "px_ready", "xpt_ps", "x_ps", "x_made"))
        rhs_ps, rhs_ready, sa_ps, sa_ready, y_ps, y_ready, st_ps, st_ready = (
            sem(n) for n in ("rhs_ps", "rhs_ready", "sa_ps", "sa_ready", "y_ps", "y_ready", "st_ps", "st_ready"))
        yc_ready, ysq_ready, yv_ready, ystd, yn_ready, yT_ps, yg_ready, yTr_hi, yTr_ready = (
            sem(n) for n in ("yc_ready", "ysq_ready", "yv_ready", "ystd", "yn_ready", "yT_ps", "yg_ready", "yTr_hi", "yTr_ready"))
        q_ready, psc_ps, psc_ready = (sem(n) for n in ("q_ready", "psc_ps", "psc_ready"))
        bd_ready, bexp_ready, slot_ready, slot_ps, slot_T = (sem(n) for n in ("bd_ready", "bexp_ready", "slot_ready", "slot_ps", "slot_T"))
        is_i2_made, hots_made, spread_ps, gated = (sem(n) for n in ("is_i2_made", "hots_made", "spread_ps", "gated"))
        ga_ready, w_hi, w_lo, peer_ps = (sem(n) for n in ("ga_ready", "w_hi", "w_lo", "peer_ps"))
        sgm_ready = sem("sgm_ready")
        out_ready, out_done = sem("out_ready"), sem("out_done")
        dve_step, act_step, pool_step = sem("dve_step"), sem("act_step"), sem("pool_step")

        block = ctx.enter_context(nc.Block())

        def raw(slab, part):
            return ring[:, slab % RING, part * D:(part + 1) * D]

        c0 = [N_ALL * L + N_PRE for L in range(DEPTH)]
        v0 = [DVE_ALL * L + N_PRE for L in range(DEPTH)]

        @block.sync
        def _(sp):
            for tb in range(TB):
                sp.dma_start(xres[:, tb], x[:, tb]).then_inc((in_x0, in_x1)[tb], 16)
            sp.dma_start(cst[:, 0:K_PMASK], consts[:, 0:K_PMASK]).then_inc(in_c, 16)

            def load(layer, n, src):
                sp.dma_start(ring[:, n % RING, :], src).then_inc(filled[n % RING], 16)

            def wait_free(L, n):
                before, Lb = (n - RING, L) if n >= RING else (S_PLE + n if n else S_LAST, L - 1)
                if Lb < 0:
                    return
                if before == S_LORA:
                    sp.wait_ge(lora_ps, 3 * (Lb + 1))
                elif before < S_LORA:
                    sp.wait_ge(low_dve, projection_tile(Lb, "in", min(2 * before + 1, IN_TILES - 1)).low + 1)
                elif before < S_WQ:
                    sp.wait_ge(low_dve, projection_tile(Lb, "out", 2 * (before - S_OUT) + 1).low + 1)
                elif before < S_PEER:
                    sp.wait_ge(low_dve, projection_tile(Lb, "wq", 2 * (before - S_WQ) + 1).low + 1)
                elif before >= S_PLE:
                    sp.wait_ge(low_dve, projection_tile(Lb, "ple", 2 * (before - S_PLE) + 1).low + 1)
                else:
                    sp.wait_ge(low_dve, v0[L] + DVE_V - 2 * (S_PLE - 1 - before))

            for L in range(DEPTH):
                for n in range(S_PEER + RING):
                    wait_free(L, n)
                    load(L, n, w_slabs[L, n] if n < S_PEER else peer_slabs[L, n - S_PEER])
                    if L == 0 and n == 0:
                        sp.dma_start(vec[:], vecs).then_inc(in_v, 16)
                    if L == 0 and n == 1:
                        sp.dma_start(cst[:, K_PMASK:], consts[:, K_PMASK:]).then_inc(in_c2, 16)
                    if L == 0 and n == RING - 1:
                        sp.dma_start(praw[:], p_t).then_inc(in_p, 16)
                with sp.Fori(0, (S_UV - S_PEER) // RING) as i:
                    for j in range(RING):
                        sp.wait_ge(low_pool, POOL_ALL * L + 2 * (RING * i + j) + 2)
                        load(L, j, peer_slabs[L, RING * i + (j + RING)])
                with sp.Fori(0, (S_VV - S_UV) // RING) as i:
                    for j in range(RING):
                        sp.wait_ge(low_dve, v0[L] + RING * i + (j + 1))
                        load(L, j, peer_slabs[L, RING * i + (j + S_UV - S_PEER + RING)])
                with sp.Fori(0, QT // 2 // RING) as i:
                    for j in range(RING):
                        sp.wait_ge(low_pool, POOL_ALL * L + NSUB + 2 * (RING * i + j) + 2)
                        load(L, j, peer_slabs[L, RING * i + (j + S_VV - S_PEER + RING)])
                with sp.Fori(QT // 2 // RING, (S_PLE - S_VV) // RING - 1) as i:
                    for j in range(RING):
                        sp.wait_ge(low_dve, v0[L] + (HELD - QT) + 2 * (RING * i + j) + 2)
                        load(L, j, peer_slabs[L, RING * i + (j + S_VV - S_PEER + RING)])
                for n in range(S_PLE, S_LAST + 1):
                    wait_free(L, n)
                    load(L, n, w_slabs[L, S_PEER + n - S_PLE])
            sp.wait_ge(low_dve, v0[DEPTH - 1] + DVE_V + 1)
            sp.dma_start(gfin[:], g_final).then_inc(in_g, 16)
            for tb in range(TB):
                sp.wait_ge(out_ready, tb + 1)
                sp.dma_start(out[:, tb], obuf[:, tb]).then_inc(out_done, 16)
            sp.wait_ge(out_done, 16 * TB)

        @block.gpsimd
        def _(pool):
            pool.memset(zeros[:], 0.0).then_inc(zeros_made, 1)
            pool.memset(minus_half, -0.5).then_inc(pool_step, 1)
            pool.wait_ge(pool_step, 1)
            steps = [1]

            def link(ins):
                steps[0] += 1
                ins.then_inc(pool_step, 1)
                pool.wait_ge(pool_step, steps[0])

            def norm(r):
                for tb in range(TB):
                    pool.wait_ge(sumsq, TB * r + tb + 1)
                    link(pool.tensor_scalar(rstd[:, tb:tb + 1], ssq[:, tb:tb + 1], EPS, None, ALU.add))
                    pool.tensor_tensor(rstd[:, tb:tb + 1], rstd[:, tb:tb + 1], minus_half, ALU.pow).then_inc(rms, 1)

            for L in range(DEPTH):
                norm(3 * L)
                pool.wait_ge(ao_ms, L + 1)
                pool.tensor_tensor(arstd, assq, minus_half.broadcast_to([P, TB]), ALU.pow).then_inc(ao_rms, 1)
                pool.wait_ge(in_c2, 16)
                for g in range(4):
                    pool.wait_ge(prod_ready, 16 * L + 4 * g + 4)
                    mask = cst[:, K_LMASK:K_LMASK + P].unsqueeze(1).broadcast_to([P, 4, P])
                    pool.tensor_tensor(Mt[:, 0, 4 * g:4 * g + 4], prods[:, 4 * g:4 * g + 4, 0:P], mask, ALU.mult).then_inc(mt_ready, 1)
                for lv in range(1, LEVELS):
                    pool.wait_ge(prod_ready, 16 * (L + 1))
                    if lv >= 2:
                        pool.wait_ge(m_ps, 4 * LEVELS * L + 4 * (lv - 1))
                        pool.wait_ge(xm_ready, 4 * LEVELS * L + 4 * (lv - 1))
                    mask = cst[:, K_LMASK + lv * P:K_LMASK + (lv + 1) * P].unsqueeze(1).broadcast_to([P, 16, P])
                    pool.tensor_tensor(Mt[:, lv % 2], prods[:, :, 0:P], mask, ALU.mult).then_inc(mt_ready, 1)
                norm(3 * L + 1)
                def split_tile(half, place, count, j):
                    pool.wait_ge(part_hi, count + 1)
                    b = (c0[L] + j) % DEEP
                    pool.tensor_tensor(low[:, b], ring[:, place, half * D:(half + 1) * D], high[:, b].bitcast(F32), ALU.subtract).then_inc(low_pool, 1)

                with pool.Fori(0, HELD // 8) as i:
                    for j in range(8):
                        split_tile(j % 2, j // 2 % RING, c0[L] + 8 * i + j, j)
                with pool.Fori(0, (NSUB - HELD) // RING) as i:
                    for j in range(RING):
                        split_tile(0, j, c0[L] + C_UV + 2 * j + 2 * RING * i, 2 * j)
                with pool.Fori(0, QT // 8) as i:
                    for j in range(8):
                        split_tile(j % 2, j // 2 % RING, c0[L] + C_VV + j + 8 * i, j)
                norm(3 * L + 2)
            norm(3 * DEPTH)

        @block.scalar
        def _(act):
            steps = [0]

            def link(ins):
                steps[0] += 1
                ins.then_inc(act_step, 1)
                act.wait_ge(act_step, steps[0])

            def split(tile):
                if tile.count >= DEEP:
                    act.wait_ge(part_used, tile.count - DEEP + 1)
                act.wait_ge(filled[tile.slab % RING], 16 * fills(tile.layer, tile.slab))
                act.copy(high[:, tile.count % DEEP], raw(tile.slab, tile.half)).then_inc(part_hi, 1)

            def norm(r, gain, meanwhile=None):
                for tb in range(TB):
                    if r:
                        act.wait_ge(x_ready, TB * (r - 1) + tb + 1)
                    else:
                        act.wait_ge((in_x0, in_x1)[tb], 16)
                    act.activation(xn[:, tb], xres[:, tb], ACT.Square, scale=D ** -0.5, accum_out=ssq[:, tb:tb + 1]).then_inc(sumsq, 1)
                if gain is None:
                    return
                if meanwhile:
                    meanwhile()
                for k in range(KT):
                    act.wait_ge(xT_ps, 4 * r + k // 2 + 1)
                    act.activation(hTh[:, k], PS[:, k // 2, (k % 2) * SEQ:(k % 2 + 1) * SEQ], ACT.Identity, scale=gain[:, k:k + 1]).then_inc(hT_hi, 1)

            for L in range(DEPTH):
                V = vec[:, L]
                def early():
                    if L:
                        split(projection_tile(L, "in", 3))
                    else:
                        for k in range(2):
                            split(projection_tile(L, "in", k))
                        act.wait_ge(in_v, 16)

                norm(3 * L, V[:, C_GMIX:C_GMIX + KT], early)
                if L == 0:
                    for k in range(2, 4):
                        split(projection_tile(L, "in", k))
                if L == 0:
                    act.wait_ge(in_p, 16)
                    act.copy(pTh[:], praw[:]).then_inc(p_hi, 1)
                def exps(tb):
                    act.wait_ge(nm_ready, TB * L + tb + 1)
                    lg = lg1 if tb else lg0
                    for h in range(NH):
                        c = tb * NH + h
                        act.activation(lg[:, h], lg[:, h], ACT.Exp, bias=anm[:, c:c + 1], accum_out=arow[:, c:c + 1])
                    act.activation(asink[:, tb * NH:(tb + 1) * NH], asink[:, tb * NH:(tb + 1) * NH], ACT.Exp).then_inc(p_ready, 1)

                def evacuate_pT(n):
                    act.wait_ge(pT_ps, 6 * L + n + 1)
                    src = PS[:, PT_BANKS[n]]
                    if n < 2:
                        act.copy(PT0[:, 4 * n:4 * n + 4], src.rearrange("p (a b) -> p a b", a=4)).then_inc(pT_ready, 1)
                    else:
                        act.copy(PT1[:, 2 * (n - 2):2 * (n - 1)], src.rearrange("p (a c b) -> p a c b", a=2, c=2)).then_inc(pT_ready, 1)

                for m in range(IN_TILES):
                    tile = projection_tile(L, "in", m)
                    act.wait_ge(part_used, tile.count + 1)
                    src = PS[:, 4 + m % 4, 0:SEQ]
                    if m == 0:
                        act.wait_ge(bq_ready, L + 1)
                    if m < T_K:
                        act.activation(aT[:, m], src, ACT.Identity, bias=bq8[:, m:m + 1], scale=HD ** -0.5).then_inc(in_evac, 1)
                    else:
                        dst = aT[:, m] if m < QKV_TILES else fpad[:, m - QKV_TILES, 1:SEQ + 1]
                        act.activation(dst, src, ACT.Identity, bias=V[:, C_BIN + m:C_BIN + m + 1]).then_inc(in_evac, 1)
                    if m + 4 < IN_TILES:
                        split(projection_tile(L, "in", m + 4))
                    if m == 8:
                        act.wait_ge(vtA_ps, L + 1)
                        act.copy(vtA[:], PS[:, 0, 0:TB * P]).then_inc(vtA_ready, 1)
                    elif m == 9:
                        exps(0)
                    elif m == 12:
                        exps(1)
                        evacuate_pT(0)
                        evacuate_pT(1)
                    elif m == 14:
                        for n in range(2, 6):
                            evacuate_pT(n)
                    elif m == 17:
                        act.wait_ge(ao_ready, TB * (L + 1))
                        for tb in range(TB):
                            act.activation(PS[:, 1 + tb], ao[:, tb], ACT.Square, accum_out=assq[:, tb:tb + 1]).then_inc(ao_ssq, 1)
                for k in range(4):
                    act.wait_ge(aoT_ps, 2 * L + k // 2 + 1)
                    act.activation(hTh[:, k], PS[:, AOT_BANKS[k // 2], (k % 2) * SEQ:(k % 2 + 1) * SEQ], ACT.Identity, scale=V[:, C_AN + k:C_AN + k + 1]).then_inc(yTa_hi, 1)
                act.wait_ge(mixed, L + 1)
                for t in range(4):
                    ins = act.activation(sqk[:, t], fm[:, 4 + t], ACT.Square, scale=V[:, C_KK + t:C_KK + t + 1])
                ins.then_inc(sqk_ready, 1)
                act.activation(xw_t[0:64], fm[0:64, T_LORA], ACT.Tanh).then_inc(lora_in, 1)
                act.activation(xg_s[:, :, :], fm[:, T_GATE:T_GATE + 2], ACT.Sigmoid).then_inc(lora_in, 1)
                act.wait_ge(lora_ps, 3 * L + 1)
                act.wait_ge(yTa_ready, L + 1)
                for t in range(4):
                    ins = act.activation(sw[:, t], PS[:, t // 2, (t % 2) * SEQ:(t % 2 + 1) * SEQ], ACT.Sigmoid, bias=V[:, C_W0 + t:C_W0 + t + 1])
                ins.then_inc(gates_ready, 1)
                act.wait_ge(lora_ps, 3 * L + 2)
                for t in range(4):
                    ins = act.activation(avec[:, t], PS[:, 2 + t // 2, (t % 2) * SEQ:(t % 2 + 1) * SEQ], ACT.Sigmoid, bias=V[:, C_A0 + t:C_A0 + t + 1])
                ins.then_inc(gates_ready, 1)
                act.wait_ge(lora_ps, 3 * L + 3)
                act.copy(gT[:], PS[:, 4:6].rearrange("p a (b c) -> p (a b) c", b=2)).then_inc(g_ready, 1)
                act.wait_ge(kss_max, L + 1)
                act.activation(rnorm[:], rnorm[:], ACT.Sqrt).then_inc(knorm, 1)
                act.wait_ge(csum_ready, 2 * L + 1)
                act.activation(wcum[:], csum[:], ACT.Exp, scale=-EXP_MINUS_HALF).then_inc(decay_ready, 1)
                act.activation(winv[:], csum[:], ACT.Exp, scale=EXP_MINUS_HALF).then_inc(decay_ready, 1)
                act.wait_ge(csum_ready, 2 * L + 2)
                act.activation(wprev[:], cprev[:], ACT.Exp, scale=-EXP_MINUS_HALF).then_inc(decay_ready, 1)
                for n, dst in enumerate((vtok, btok, ktok)):
                    act.wait_ge(tok_ps, 3 * L + n + 1)
                    act.copy(dst[:], PS[:, 2 * n:2 * n + 2]).then_inc(tok_ready, 1)
                for lv in range(1, LEVELS):
                    for g in range(4):
                        act.wait_ge(m_ps, 4 * (LEVELS * L + lv) + g + 1)
                        act.copy(PX[:, 4 * g:4 * g + 4], PS[:, g].rearrange("p (a b) -> p a b", a=4)).then_inc(px_ready, 1)
                    if lv == LEVELS - 1:
                        continue
                    for g in range(4):
                        act.wait_ge(x_ps, 4 * ((LEVELS - 2) * L + lv - 1) + g + 1)
                        act.copy(X[:, 4 * g:4 * g + 4], PS[:, 4 + g].rearrange("p (a b) -> p a b", a=4)).then_inc(x_made, 1)
                def squares(tb):
                    act.wait_ge(yc_ready, TB * L + tb + 1)
                    act.activation(ysq[:, tb], yc[:, tb], ACT.Square, scale=HD ** -0.5).then_inc(ysq_ready, 1)
                    act.wait_ge(yv_ready, TB * L + tb + 1)
                    act.activation(gvar[:, tb * NH:(tb + 1) * NH], gvar[:, tb * NH:(tb + 1) * NH], ACT.Sqrt).then_inc(ystd, 1)

                for c in range(NCHUNK):
                    o = 64 * (c % 2)
                    act.wait_ge(sa_ps, NCHUNK * L + c + 1)
                    act.copy(sa[o:o + 64], PS[o:o + 64, 1]).then_inc(sa_ready, 1)
                    act.wait_ge(y_ps, NCHUNK * L + c + 1)
                    act.copy(ytok[o:o + 64, c // 2], PS[o:o + 64, 2]).then_inc(y_ready, 1)
                    split(projection_tile(L, "out", c))
                    if c == 2:
                        squares(0)
                split(projection_tile(L, "out", 4))
                squares(1)
                for k in range(5, KT - 1):
                    split(projection_tile(L, "out", k))
                for n in range(2):
                    act.wait_ge(yg_ready, 2 * L + n + 1)
                    act.copy(hTh[:, 4 + 2 * n:6 + 2 * n], ytmp[:, 2 * n:2 * n + 2]).then_inc(yTr_hi, 1)
                split(projection_tile(L, "out", KT - 1))
                for k in range(4):
                    split(projection_tile(L, "wq", k))
                norm(3 * L + 1, V[:, C_GFFN:C_GFFN + KT])
                for m in range(HC):
                    tile = projection_tile(L, "wq", m)
                    act.wait_ge(part_used, tile.count + 1)
                    act.copy(qT[:, m], PS[:, 4 + m % 4, 0:SEQ]).then_inc(q_ready, 1)
                    if m + 4 < HC:
                        split(projection_tile(L, "wq", m + 4))
                for n in range(8):
                    act.wait_ge(psc_ps, 8 * L + n + 1)
                    act.copy(sc[:, n // 4, 4 * (n % 4):4 * (n % 4) + 4], PS[:, n].rearrange("p (a b) -> p a b", a=4)).then_inc(psc_ready, 1)

                def split_tile(count, j, place, half, fill):
                    act.wait_ge(part_used, c0[L] + count - DEEP + 1)
                    act.wait_ge(filled[place], fill)
                    act.copy(high[:, (c0[L] + j) % DEEP], ring[:, place, half * D:(half + 1) * D]).then_inc(part_hi, 1)

                def gelu(place, j):
                    act.activation(GA[:, bass.ds(place, 1)], PS[:, 6 + j % 2:7 + j % 2, 0:SEQ], ACT.Gelu).then_inc(ga_ready, 1)

                def split_u(i, j):
                    split_tile(8 * i + j, j, j // 2 % RING, j % 2, 16 * fills(L, S_PEER + j // 2) + 16 * i)

                def split_uv(i, j, v):
                    if v:
                        act.wait_ge(low_pool, POOL_ALL * L + HELD + 1 + RING * i + j)
                    split_tile(2 * RING * i + (C_UV + 2 * j + v), 2 * j + v, j % RING, v, 16 * fills(L, S_UV + j) + 16 * i)

                def split_vv(i, j):
                    split_tile(8 * i + (C_VV + j), j, j // 2 % RING, j % 2, 16 * fills(L, S_VV + j // 2) + 16 * i)

                def split_w(s, place, j, v_before):
                    act.wait_ge(part_used, c0[L] + 1 + v_before)
                    act.copy(WH[:, j % 2:j % 2 + 1], GA[:, bass.ds(place, 1)]).then_inc(w_hi, 1)

                def exponentials(tb):
                    act.wait_ge(bd_ready, TB * L + tb + 1)
                    act.activation(slot[:, 2, tb], slot[:, 2, tb], ACT.Exp).then_inc(bexp_ready, 1)

                for j in range(DEEP):
                    split_u(0, j)
                with act.Fori(0, A_FIRST // 8) as i:
                    for j in range(8):
                        split_u(i, j + DEEP)
                        gelu(8 * i + j, j)
                exponentials(0)
                with act.Fori(A_FIRST // 8, A_SECOND // 8) as i:
                    for j in range(8):
                        split_u(i, j + DEEP)
                        gelu(8 * i + j, j)
                for e in range(A_SECOND // 8 * 8, A_LOOP):
                    if e == A_SECOND:
                        exponentials(1)
                    if e == A_TOP:
                        act.wait_ge(slot_ps, L + 1)
                        act.copy(sT[:, 0:2, 0:SEQ], PS[:, 4].rearrange("p (a b) -> p a b", a=2))
                        act.copy(sT[:, 0:2, SEQ:], PS[:, 4].rearrange("p (a b) -> p a b", a=2)[:, :, 0:GROUP])
                        act.copy(sT[:, 2, 0:SEQ], PS[:, 5, 0:SEQ])
                        act.copy(sT[:, 2, SEQ:], PS[:, 5, 0:GROUP]).then_inc(slot_T, 1)
                    split_u((e + DEEP) // 8, (e + DEEP) % 8)
                    gelu(e, e)
                with act.Fori(A_LOOP // 8, HELD // 8 - 1) as i:
                    for j in range(8):
                        split_u(i, j + DEEP)
                        gelu(8 * i + j, j)
                for j in range(4):
                    split_u(HELD // 8 - 1, j + DEEP)
                    gelu(HELD - 8 + j, j)
                for j in range(4):
                    split_uv(0, j // 2, j % 2)
                    gelu(HELD - 4 + j, j)
                act.wait_ge(gated, NGROUPS * (NQ * L + 1))
                split_w(0, 0, 0, 0)

                def w_after_gates(s, place, j):
                    if isinstance(s, int) and s % QT == QT - 1:
                        act.wait_ge(gated, NGROUPS * (NQ * L + (s + 1) // QT + 1))
                    split_w(s + 1, place, j + 1, C_UV + 2 * s - 1)

                def step(i, j):
                    s = RING * i + j
                    act.wait_ge(w_lo, NSUB * L + 1 + s)
                    split_uv(i, j + 2, 0)
                    gelu(s, j)
                    w_after_gates(s, s + 1, j)
                    split_uv(i, j + 2, 1)

                with act.Fori(0, QT // RING - 1) as i:
                    for j in range(RING):
                        step(i, j)
                for j in range(RING):
                    step(QT // RING - 1, j)
                with act.Fori(QT // RING, HELD // RING - 1) as i:
                    for j in range(RING):
                        step(i, j)
                for s in range(HELD - RING, HELD):
                    act.wait_ge(w_lo, NSUB * L + 1 + s)
                    if s < HELD - 2:
                        split_uv(s // RING, s % RING + 2, 0)
                    else:
                        act.wait_ge(part_used, c0[L] + C_UV + 2 * s + 1)
                    gelu(s, s)
                    w_after_gates(s, (s + 1) % HELD, s)
                    if s < HELD - 2:
                        split_uv(s // RING, s % RING + 2, 1)
                    elif s == HELD - 2:
                        split_vv(0, 0)
                    else:
                        split_vv(0, 1)
                        split_vv(0, 2)
                def late(n, i, j, more=True):
                    if isinstance(n, int) and n == QT - 1:
                        act.wait_ge(gated, NGROUPS * NQ * (L + 1))
                    split_w(n, n + 1, j + 1, C_VV - 1 + n)
                    if more:
                        split_vv(i, j + 3)

                with act.Fori(0, QT // 8 - 1) as i:
                    for j in range(8):
                        late(8 * i + j, i, j)
                for j in range(8):
                    late(QT - 8 + j, QT // 8 - 1, j)
                with act.Fori(QT // 8, HELD // 8 - 1) as i:
                    for j in range(8):
                        late(8 * i + j, i, j)
                for j in range(7):
                    late(HELD - 8 + j, HELD // 8 - 1, j, j < 5)
                for k in range(4):
                    split(projection_tile(L, "ple", k))
                def early():
                    for k in range(4, 6):
                        split(projection_tile(L, "ple", k))

                norm(3 * L + 2, V[:, C_GPLE:C_GPLE + KT], early)
                for k in range(6, 10):
                    split(projection_tile(L, "ple", k))
                act.activation(ahead, minus_half, ACT.Sigmoid)
                if L < DEPTH - 1:
                    split(projection_tile(L + 1, "in", 0))
                act.wait_ge(part_used, projection_tile(L, "ple", KT + 1).count + 1)
                for n in range(4):
                    act.activation(sgm[:, n // 2, (n % 2) * 512:(n % 2 + 1) * 512], PS[:, n], ACT.Sigmoid).then_inc(sgm_ready, 1)
                if L < DEPTH - 1:
                    for k in range(1, 3):
                        split(projection_tile(L + 1, "in", k))
            norm(3 * DEPTH, None)

        @block.vector
        def _(dve):
            steps = [0]

            def link(ins):
                steps[0] += 1
                ins.then_inc(dve_step, 1)
                dve.wait_ge(dve_step, steps[0])

            def split(tile):
                dve.wait_ge(part_hi, tile.count + 1)
                b = tile.count % DEEP
                dve.tensor_tensor(low[:, b], raw(tile.slab, tile.half), high[:, b].bitcast(F32), ALU.subtract).then_inc(low_dve, 1)

            def norm(r, gain, meanwhile=None):
                for tb in range(TB):
                    dve.wait_ge(rms, TB * r + tb + 1)
                    dve.tensor_scalar(xn[:, tb], xres[:, tb], rstd[:, tb:tb + 1], None, ALU.mult).then_inc(xn_ready, 1)
                if meanwhile:
                    meanwhile()
                for k in range(KT):
                    dve.wait_ge(hT_hi, KT * r + k // 2 * 2 + 2)
                    dve.scalar_tensor_tensor(hTl[:, k], PS[:, k // 2, (k % 2) * SEQ:(k % 2 + 1) * SEQ], gain[:, k:k + 1],
                                             hTh[:, k].bitcast(F32), ALU.mult, ALU.subtract).then_inc(hT_lo, 1)

            def bc(col, n):
                return col.unsqueeze(2).broadcast_to([P, col.shape[1], n])

            for L in range(DEPTH):
                V = vec[:, L]
                def early():
                    if L:
                        split(projection_tile(L, "in", 1))
                    else:
                        for k in range(2):
                            split(projection_tile(L, "in", k))
                        dve.wait_ge(in_v, 16)

                norm(3 * L, V[:, C_GMIX:C_GMIX + KT], early)
                for k in range(2, 4):
                    split(projection_tile(L, "in", k))
                if L == 0:
                    dve.wait_ge(in_c2, 16)
                    dve.tensor_copy(iota_half[:], iota)
                if L == 0:
                    dve.wait_ge(p_hi, 1)
                    dve.tensor_tensor(pTl[:], praw[:], pTh[:].bitcast(F32), ALU.subtract).then_inc(p_lo, 1)
                dve.tensor_scalar(bq8, V[:, C_BIN:C_BIN + T_K], HD ** -0.5, None, ALU.mult).then_inc(bq_ready, 1)
                dve.memset(fpad[:, :, 0:1], 0.0).then_inc(dve_step, 1)
                steps[0] += 1
                dve.wait_ge(dve_step, steps[0])
                sinks = V[:, C_SINK:C_SINK + NH]

                def logits(tb, h0, h1, banks):
                    nk = P * (tb + 1)
                    dist = cst[:, K_DIST1:K_DIST1 + nk] if tb else cst[:, K_DIST0:K_DIST0 + nk]
                    for h in range(h0, h1):
                        at, per = (h - h0) * nk, 512 // nk
                        src = PS[:, banks[(h - h0) // per], at % 512:at % 512 + nk]
                        ins = dve.scalar_tensor_tensor((lg1 if tb else lg0)[:, h], dist, -SLOPES[h], src, ALU.mult, ALU.add)
                    ins.then_inc(lg_made, 1)

                def maxima(tb):
                    c = slice(tb * NH, (tb + 1) * NH)
                    link(dve.tensor_reduce(amax[:, c], (lg1 if tb else lg0)[:], AX.X, ALU.max))
                    link(dve.tensor_tensor(amax[:, c], amax[:, c], sinks, ALU.max))
                    dve.tensor_scalar(anm[:, c], amax[:, c], -1.0, None, ALU.mult)
                    dve.tensor_tensor(asink[:, c], sinks, amax[:, c], ALU.subtract).then_inc(nm_ready, 1)

                for m in range(IN_TILES):
                    if m + 4 < IN_TILES:
                        split(projection_tile(L, "in", m + 4))
                    if m < QKV_TILES:
                        continue
                    n = m - QKV_TILES
                    dve.wait_ge(in_evac, IN_TILES * L + m + 1)
                    link(dve.tensor_tensor(fm[:, n], fpad[:, n, 0:SEQ], fpad[:, n, 1:SEQ + 1], ALU.subtract))
                    ins = dve.scalar_tensor_tensor(fm[:, n], fm[:, n], V[:, C_MU + n:C_MU + n + 1], fpad[:, n, 1:SEQ + 1], ALU.mult, ALU.add)
                    if m == IN_TILES - 1:
                        ins.then_inc(mixed, 1)
                    if m == 8:
                        dve.wait_ge(sc_ps, 3 * L + 1)
                        logits(0, 0, NH, (1, 2))
                        dve.wait_ge(lg_made, 3 * L + 1)
                        maxima(0)
                    elif m == 9:
                        dve.wait_ge(sc_ps, 3 * L + 2)
                        logits(1, 0, 4, (3, 0))
                    elif m == 10:
                        dve.wait_ge(sc_ps, 3 * L + 3)
                        logits(1, 4, NH, (1, 2))
                        dve.wait_ge(lg_made, 3 * (L + 1))
                        maxima(1)
                    elif m == 16:
                        for tb in range(TB):
                            c = slice(tb * NH, (tb + 1) * NH)
                            dve.wait_ge(p_ready, TB * L + tb + 1)
                            link(dve.tensor_tensor(aden[:, c], arow[:, c], asink[:, c], ALU.add))
                            link(dve.reciprocal(aden[:, c], aden[:, c]))
                            dve.wait_ge(pv_ps, TB * L + tb + 1)
                            dve.tensor_tensor(ao[:, tb].rearrange("p (h d) -> p h d", h=NH),
                                              PS[:, 1 + tb].rearrange("p (h d) -> p h d", h=NH),
                                              bc(aden[:, c], HD), ALU.mult).then_inc(ao_ready, 1)
                    elif m == 18:
                        dve.wait_ge(ao_ssq, TB * (L + 1))
                        dve.tensor_scalar(assq, assq, 1.0 / 512, EPS, ALU.mult, ALU.add).then_inc(ao_ms, 1)
                        dve.wait_ge(ao_rms, L + 1)
                        for tb in range(TB):
                            ins = dve.tensor_scalar(ao[:, tb], ao[:, tb], arstd[:, tb:tb + 1], None, ALU.mult)
                        ins.then_inc(ao_normed, 1)
                for k in range(4):
                    dve.wait_ge(yTa_hi, 4 * L + k // 2 * 2 + 2)
                    ins = dve.scalar_tensor_tensor(hTl[:, k], PS[:, AOT_BANKS[k // 2], (k % 2) * SEQ:(k % 2 + 1) * SEQ], V[:, C_AN + k:C_AN + k + 1],
                                                   hTh[:, k].bitcast(F32), ALU.mult, ALU.subtract)
                ins.then_inc(yTa_ready, 1)
                for t in range(4):
                    ins = dve.tensor_scalar(kk[:, t], fm[:, 4 + t], V[:, C_KK + t:C_KK + t + 1], None, ALU.mult)
                dve.wait_ge(gates_ready, 2 * L + 1)
                for t in range(4):
                    ins = dve.tensor_tensor_scan(csum[:, t], cst[:, K_RESET:K_RESET + SEQ], sw[:, t], 0.0, ALU.mult, ALU.add)
                ins.then_inc(csum_ready, 1)
                dve.wait_ge(csum_ready, 2 * L + 1)
                dve.tensor_tensor(cprev[:], csum[:], sw[:], ALU.subtract).then_inc(csum_ready, 1)
                dve.wait_ge(kss_ps, L + 1)
                dve.tensor_scalar(rnorm[:], PS[:, 6:8].rearrange("p a (b c) -> p (a b) c", b=2), 1e-24, None, ALU.max).then_inc(kss_max, 1)
                dve.wait_ge(gates_ready, 2 * L + 2)
                for t in range(4):
                    ins = dve.tensor_scalar(kmod[:, t], avec[:, t], 1.0, V[:, C_KA + t:C_KA + t + 1], ALU.subtract, ALU.mult)
                link(ins)
                link(dve.scalar_tensor_tensor(kmod[:], kmod[:], 1.0, fm[:, 4:8], ALU.add, ALU.mult))
                for t in range(4):
                    ins = dve.scalar_tensor_tensor(rkprod[:, t], fm[:, t], V[:, C_RK + t:C_RK + t + 1], kmod[:, t], ALU.mult, ALU.mult)
                ins.then_inc(rk_ready, 1)
                dve.wait_ge(knorm, L + 1)
                link(dve.reciprocal(rnorm[:], rnorm[:]))
                link(dve.tensor_tensor(kk[:], kk[:], rnorm[:], ALU.mult))
                link(dve.tensor_tensor(bvec[:], kk[:], avec[:], ALU.mult))
                dve.wait_ge(decay_ready, 3 * (L + 1))
                v8 = lambda t: t[:].rearrange("p a (b c) -> p (a b) c", b=TB)
                dve.tensor_tensor(bt[:], bvec[:], winv[:], ALU.mult)
                dve.tensor_tensor(kt[:], kmod[:], winv[:], ALU.mult).then_inc(bkt_ready, 1)
                arv = ar[:].rearrange("p a b c d -> p (a b) c d")
                dve.scalar_tensor_tensor(arv[:, :, 0], v8(kk), -1.0, v8(wprev), ALU.mult, ALU.mult)
                dve.tensor_tensor(arv[:, :, 1], fm[:, 0:4].rearrange("p a (b c) -> p (a b) c", b=TB), v8(wcum), ALU.mult).then_inc(bkt_ready, 1)
                dve.wait_ge(bonus_ps, L + 1)
                dve.tensor_tensor(bonus_v[:], PS[:, 6:8].rearrange("p a (b c) -> p (a b) c", b=2), fm[:, 8:12], ALU.mult).then_inc(bonus_ready, 1)
                pm = cst[:, K_PMASK:K_PMASK + 256].unsqueeze(1).broadcast_to([P, 2, 256])
                for n in range(16):
                    dve.wait_ge(prod_ps, 16 * L + n + 1)
                    dve.tensor_tensor(prods[:, n].rearrange("p (a b) -> p a b", a=2),
                                      PS[:, 6 + n % 2].rearrange("p (a b) -> p a b", a=2), pm, ALU.mult).then_inc(prod_ready, 1)
                for lv in range(LEVELS):
                    for g in range(4):
                        gs = slice(4 * g, 4 * g + 4)
                        four = lambda a: a.rearrange("p (a b) -> p a b", a=4)
                        if lv == 0:
                            dve.wait_ge(m_ps, 4 * LEVELS * L + g + 1)
                            dve.wait_ge(mt_ready, (LEVELS + 3) * L + g + 1)
                            eye = ident.unsqueeze(1).broadcast_to([P, 4, P])
                            dve.tensor_tensor(XT[:, gs], Mt[:, 0, gs], eye, ALU.add)
                            dve.tensor_tensor(X[:, gs], four(PS[:, g]), eye, ALU.add).then_inc(xm_ready, 1)
                            continue
                        dve.wait_ge(xpt_ps, 4 * ((LEVELS - 1) * L + lv - 1) + g + 1)
                        dve.wait_ge(xm_ready, 4 * (LEVELS * L + lv - 1) + g + 1)
                        dve.tensor_tensor(XT[:, gs], XT[:, gs], four(PS[:, g]), ALU.add).then_inc(xm_ready, 1)
                dve.memset(rhs[:], 0.0)
                dve.memset(sa[:], 0.0)
                link(dve.memset(ST[:], 0.0))
                def group_norm(tb, part):
                    cs = slice(tb * NH, (tb + 1) * NH)
                    y8, yc8 = (v[:, tb].rearrange("p (h d) -> p h d", h=NH) for v in (ytok, yc))
                    if part == 0:
                        dve.wait_ge(y_ready, NCHUNK * L + 2 * (tb + 1))
                        link(dve.tensor_reduce(gmean[:, cs], y8, AX.X, ALU.add))
                        link(dve.tensor_scalar(gmean[:, cs], gmean[:, cs], -1.0 / HD, None, ALU.mult))
                        dve.tensor_tensor(yc8, y8, bc(gmean[:, cs], HD), ALU.add).then_inc(yc_ready, 1)
                    else:
                        dve.wait_ge(ysq_ready, TB * L + tb + 1)
                        link(dve.tensor_reduce(gvar[:, cs], ysq[:, tb].rearrange("p (h d) -> p h d", h=NH), AX.X, ALU.add))
                        dve.tensor_scalar(gvar[:, cs], gvar[:, cs], LNX_EPS, None, ALU.add).then_inc(yv_ready, 1)
                        dve.wait_ge(ystd, TB * L + tb + 1)
                        link(dve.reciprocal(gvar[:, cs], gvar[:, cs]))
                        dve.tensor_tensor(yc8, yc8, bc(gvar[:, cs], HD), ALU.mult).then_inc(yn_ready, 1)

                for c in range(NCHUNK):
                    o = 64 * (c % 2)
                    dve.wait_ge(rhs_ps, NCHUNK * L + c + 1)
                    dve.tensor_copy(rhs[o:o + 64], PS[o:o + 64, 0]).then_inc(rhs_ready, 1)
                    if c == NCHUNK - 1:
                        group_norm(0, 1)
                        continue
                    dve.wait_ge(st_ps, (NCHUNK - 1) * L + c + 1)
                    for b in range(2):
                        hr = slice(64 * b, 64 * b + 64)
                        src = PS[hr, 3, 0:4 * HD].rearrange("p (a b) -> p a b", a=4)
                        wend = wcum[hr, :, 64 * c + 63:64 * c + 64].broadcast_to([64, 4, HD])
                        state = ST[hr, c % 2, :, hr]
                        if c:
                            link(dve.tensor_tensor(state, ST[hr, (c - 1) % 2, :, hr], src, ALU.add))
                            ins = dve.tensor_tensor(state, state, wend, ALU.mult)
                        else:
                            ins = dve.tensor_tensor(state, src, wend, ALU.mult)
                    ins.then_inc(st_ready, 1)
                    if c:
                        split(projection_tile(L, "out", c - 1))
                    if c == 2:
                        group_norm(0, 0)
                for k in range(2, 4):
                    split(projection_tile(L, "out", k))
                group_norm(1, 0)
                split(projection_tile(L, "out", 4))
                group_norm(1, 1)
                for k in range(5, KT - 1):
                    split(projection_tile(L, "out", k))
                dve.wait_ge(yT_ps, L + 1)
                dve.wait_ge(g_ready, L + 1)
                for n in range(2):
                    ts = slice(2 * n, 2 * n + 2)
                    for t in range(2 * n, 2 * n + 2):
                        ins = dve.tensor_scalar(ytmp[:, t], PS[:, 4 + n, (t % 2) * SEQ:(t % 2 + 1) * SEQ],
                                                V[:, C_LNW + t:C_LNW + t + 1], V[:, C_LNB + t:C_LNB + t + 1], ALU.mult, ALU.add)
                    link(ins)
                    link(dve.tensor_tensor(ytmp[:, ts], ytmp[:, ts], bonus_v[:, ts], ALU.add))
                    dve.tensor_tensor(ytmp[:, ts], ytmp[:, ts], gT[:, ts], ALU.mult).then_inc(yg_ready, 1)
                for n in range(2):
                    dve.wait_ge(yTr_hi, 2 * L + n + 1)
                    ks = slice(4 + 2 * n, 6 + 2 * n)
                    dve.tensor_tensor(hTl[:, ks], ytmp[:, 2 * n:2 * n + 2], hTh[:, ks].bitcast(F32), ALU.subtract).then_inc(yTr_ready, 1)
                split(projection_tile(L, "out", KT - 1))
                for k in range(3):
                    split(projection_tile(L, "wq", k))
                dve.wait_ge(part_used, projection_tile(L, "out", KT - 1).count + 1)
                for n in range(4):
                    s = slice((n % 2) * 512, (n % 2 + 1) * 512)
                    ins = dve.tensor_tensor(xres[:, n // 2, s], xres[:, n // 2, s], PS[:, n], ALU.add)
                    if n % 2:
                        ins.then_inc(x_ready, 1)
                dve.wait_ge(x_ready, TB * (3 * L + 1))
                norm(3 * L + 1, V[:, C_GFFN:C_GFFN + KT], lambda: split(projection_tile(L, "wq", 3)))
                for k in range(4, HC):
                    split(projection_tile(L, "wq", k))
                def split_tile(count, j, place, half):
                    dve.wait_ge(part_hi, c0[L] + 1 + count)
                    b = (c0[L] + j) % DEEP
                    dve.tensor_tensor(low[:, b], ring[:, place, half * D:(half + 1) * D], high[:, b].bitcast(F32), ALU.subtract).then_inc(low_dve, 1)

                def top16(rows, n, values, vals, idx, scratch=None):
                    for r in range(rows):
                        ins = dve.max(vals[:, r, 0:8], values(r))
                    link(ins)
                    for r in range(rows):
                        dve.max_index(idx[:, r, 0:8], vals[:, r, 0:8], values(r))
                        ins = dve.match_replace(values(r), vals[:, r, 0:8], values(r), -3.0e38)
                    link(ins)
                    for r in range(rows):
                        ins = dve.max(vals[:, r, 8:16], values(r))
                    link(ins)
                    for r in range(rows):
                        ins = dve.max_index(idx[:, r, 8:16], vals[:, r, 8:16], values(r))
                    link(ins)

                for tb in range(TB):
                    dve.wait_ge(psc_ready, 8 * L + 4 * (tb + 1))
                    top16(HC, NSUB, lambda r: sc[:, tb, r], topv, topi)
                    link(dve.tensor_copy(topf[:], topi[:]))
                    tv = topv[:].rearrange("p (h c) k -> p h c k", c=2)
                    tf = topf[:].rearrange("p (h c) k -> p h c k", c=2)
                    link(dve.tensor_tensor(cand[:].rearrange("p h (a b) -> p h a b", a=TOPK),
                                           tv[:, :, 0].unsqueeze(3).broadcast_to([P, PH, TOPK, TOPK]),
                                           tv[:, :, 1].unsqueeze(2).broadcast_to([P, PH, TOPK, TOPK]), ALU.add))
                    top16(PH, TOPK * TOPK, lambda r: cand[:, r], bestv, bestc)
                    bflat = bestc[:].rearrange("p a b -> p (a b)")
                    dve.tensor_scalar(bestd[:, 0], bflat, 4, None, ALU.logical_shift_right)
                    link(dve.tensor_scalar(bestd[:, 1], bflat, 15, None, ALU.bitwise_and))
                    link(dve.tensor_copy(bestf[:].rearrange("p c a b -> p c (a b)"), bestd[:]))
                    for c in range(2):
                        link(dve.tensor_tensor(onehot[:], bestf[:, c].unsqueeze(3).broadcast_to([P, PH, TOPK, TOPK]),
                                               iota16.unsqueeze(1).unsqueeze(1).broadcast_to([P, PH, TOPK, TOPK]), ALU.is_equal))
                        link(dve.tensor_tensor(picked[:], onehot[:], tf[:, :, c].unsqueeze(2).broadcast_to([P, PH, TOPK, TOPK]), ALU.mult))
                        link(dve.tensor_reduce(slot[:, c, tb].rearrange("p (a b) -> p a b", a=PH), picked[:], AX.X, ALU.add))
                    s3 = slot[:, 2, tb].rearrange("p (a b) -> p a b", a=PH)
                    dve.tensor_tensor(s3, bestv[:], bestv[:, :, 0:1].broadcast_to([P, PH, TOPK]), ALU.subtract).then_inc(bd_ready, 1)
                    dve.wait_ge(bexp_ready, TB * L + tb + 1)
                    link(dve.tensor_reduce(gsum, s3, AX.X, ALU.add))
                    link(dve.reciprocal(gsum, gsum))
                    dve.tensor_tensor(s3, s3, bc(gsum, TOPK), ALU.mult).then_inc(slot_ready, 1)
                dve.wait_ge(slot_T, L + 1)
                link(dve.tensor_copy(gate_parts[:, :, 0], sT[:, 2]))
                link(dve.tensor_tensor(gate_rest[:], sT[:, 2], gate_parts[:, :, 0], ALU.subtract))
                link(dve.tensor_copy(gate_parts[:, :, 1], gate_rest[:]))
                link(dve.tensor_tensor(gate_parts[:, :, 2], gate_rest[:], gate_parts[:, :, 1], ALU.subtract))
                g0 = NGROUPS * NQ * L

                def one_hots(g, group, b, chunk):
                    if L or not isinstance(g, int) or g > 1:
                        dve.wait_ge(spread_ps, g0 - 1 + g)

                    dve.tensor_tensor(is_i2[:, b], iota[:, QT * chunk:QT * (chunk + 1)].unsqueeze(1).broadcast_to([P, GROUP, QT]),
                                      sT[:, 1, bass.ds(GROUP * group, GROUP)].unsqueeze(2).broadcast_to([P, GROUP, QT]), ALU.is_equal).then_inc(is_i2_made, 1)
                    for t in range(GROUP):
                        dve.tensor_scalar(hot1[:, b, t], iota_half[:], sT[:, 0, bass.ds(GROUP * group + t, 1)], None, ALU.is_equal)
                    dve.wait_ge(is_i2_made, g0 + 1 + g)
                    dve.tensor_tensor(hot2[:, b], is_i2[:, b].unsqueeze(2).broadcast_to([P, GROUP, 3, QT]),
                                      gate_parts[:, bass.ds(GROUP * group, GROUP)].unsqueeze(3).broadcast_to([P, GROUP, 3, QT]), ALU.mult).then_inc(hots_made, 1)

                def apply_gates(g, group, b, chunk):
                    dve.wait_ge(spread_ps, g0 + 1 + g)
                    acts = GA[:, chunk % 2 * QT:chunk % 2 * QT + QT, bass.ds(GROUP * group, GROUP)]
                    dve.tensor_tensor(acts, acts, PS[:, 4 + b, 0:GROUP * QT].rearrange("p (t i) -> p i t", t=GROUP), ALU.mult).then_inc(gated, 1)

                def split_w(s, place, j):
                    dve.wait_ge(w_hi, NSUB * L + 1 + s)
                    dve.tensor_tensor(WL[:, j % 2:j % 2 + 1], GA[:, bass.ds(place, 1)], WH[:, j % 2:j % 2 + 1].bitcast(F32), ALU.subtract).then_inc(w_lo, 1)

                def split_v(s, j):
                    split_tile(2 * s + (C_UV + 1), 2 * j + 1, j % RING, 1)

                def split_vv(n, j):
                    split_tile(n + C_VV, j, j // 2 % RING, j % 2)

                one_hots(0, 0, 0, 0)
                dve.wait_ge(ga_ready, NSUB * L + QT)

                def first_chunk(g, b, last=False):
                    one_hots(g + 1, g + 1, (b + 1) % 2, int(last))
                    apply_gates(g, g, b, 0)

                for b in range(2):
                    first_chunk(b, b)
                with dve.Fori(1, NGROUPS // 2 - 1) as i:
                    for b in range(2):
                        first_chunk(2 * i + b, b)
                for b in range(2):
                    first_chunk(NGROUPS - 2 + b, b, b == 1)
                split_v(0, 0)
                split_w(0, 0, 0)

                def step(s, j, group, chunk, last=False):
                    one_hots(s + (NGROUPS + 1), group + 1, (j + 1) % 2, chunk + last)
                    split_v(s + 1, j + 1)
                    apply_gates(s + NGROUPS, group, j % 2, chunk)
                    split_w(s + 1, s + 1, j + 1)

                for chunk in (1, 2):
                    s0 = QT * (chunk - 1)
                    dve.wait_ge(ga_ready, NSUB * L + QT * (chunk + 1))
                    with dve.Fori(0, QT // RING - 1) as i:
                        for j in range(RING):
                            step(RING * i + (j + s0), j, RING * i + j, chunk)
                    if chunk == 1:
                        for j in range(QT - RING, QT):
                            step(j, j, j, 1, j == QT - 1)
                for s in range(HELD - RING, HELD):
                    if s < HELD - 1:
                        step(s, s % RING, s % QT, 2)
                    else:
                        one_hots(s + NGROUPS + 1, s % QT + 1, 0, 3)
                        apply_gates(s + NGROUPS, s % QT, 1, 2)
                        split_w(s + 1, 0, 0)
                dve.wait_ge(ga_ready, NSUB * (L + 1))

                def last_chunk(n, j, last=False):
                    if not last:
                        one_hots(n + (HELD + NGROUPS + 1), n + 1, (j + 1) % 2, 3)
                    else:
                        split_vv(n + 1, j + 1)
                    apply_gates(n + (HELD + NGROUPS), n, j % 2, 3)
                    split_w(n + (HELD + 1), n + 1, j + 1)

                with dve.Fori(0, QT // 8 - 1) as i:
                    for j in range(8):
                        last_chunk(8 * i + j, j)
                for j in range(8):
                    last_chunk(QT - 8 + j, j, j == 7)
                with dve.Fori(QT // 8, HELD // 8 - 1) as i:
                    for j in range(8):
                        split_vv(8 * i + (j + 1), j + 1)
                        split_w(8 * i + (j + HELD + 1), 8 * i + (j + 1), j + 1)
                for j in range(7):
                    split_vv(HELD - 8 + j + 1, j + 1)
                    split_w(NSUB - 8 + j + 1, HELD - 8 + j + 1, j + 1)
                for k in range(4):
                    split(projection_tile(L, "ple", k))
                dve.wait_ge(peer_ps, L + 1)
                for n in range(4):
                    s = slice((n % 2) * 512, (n % 2 + 1) * 512)
                    ins = dve.tensor_tensor(xres[:, n // 2, s], xres[:, n // 2, s], PS[:, n], ALU.add)
                    if n % 2:
                        ins.then_inc(x_ready, 1)
                dve.wait_ge(x_ready, TB * (3 * L + 2))
                def early():
                    for k in range(4, 6):
                        split(projection_tile(L, "ple", k))

                norm(3 * L + 2, V[:, C_GPLE:C_GPLE + KT], early)
                for k in range(6, 10):
                    split(projection_tile(L, "ple", k))
                if L < DEPTH - 1:
                    split(projection_tile(L + 1, "in", 0))
                dve.wait_ge(part_used, projection_tile(L, "ple", KT + 1).count + 1)
                for n in range(4):
                    s = slice((n % 2) * 512, (n % 2 + 1) * 512)
                    dve.wait_ge(sgm_ready, 4 * L + n + 1)
                    link(dve.tensor_tensor(ptmp[:, n // 2, s], sgm[:, n // 2, s], PS[:, 4 + n], ALU.mult))
                    ins = dve.tensor_tensor(xres[:, n // 2, s], xres[:, n // 2, s], ptmp[:, n // 2, s], ALU.add)
                    if n % 2:
                        ins.then_inc(x_ready, 1)
                dve.wait_ge(x_ready, TB * 3 * (L + 1))
            dve.wait_ge(in_g, 16)
            for tb in range(TB):
                dve.wait_ge(rms, TB * 3 * DEPTH + tb + 1)
                dve.scalar_tensor_tensor(obuf[:, tb], xres[:, tb], rstd[:, tb:tb + 1], gfin[:], ALU.mult, ALU.mult).then_inc(out_ready, 1)

        @block.tensor
        def _(pe):
            mm = pe.matmul

            def norm(r):
                for tb in range(TB):
                    pe.wait_ge(xn_ready, TB * r + tb + 1)
                    for k in range(KT):
                        ins = pe.transpose(PS[:, k // 2, (k % 2) * SEQ + tb * P:(k % 2) * SEQ + (tb + 1) * P], xn[:, tb, k * P:(k + 1) * P], ident)
                        if tb == TB - 1 and k % 2:
                            ins.then_inc(xT_ps, 1)

            def keep_warm(bank, n):
                for _ in range(n):
                    mm(PS[:, bank], zeros[:], cst[:, 0:512], start=True, stop=True)

            def channel_rows(tile, dst, norm=None):
                pe.wait_ge(low_dve, tile.low + 1)
                b, n = tile.count % DEEP, 0
                for k in range(KT):
                    if norm is not None:
                        pe.wait_ge(hT_lo, KT * norm + k + 1)
                    ks = slice(k * P, (k + 1) * P)
                    for w, h in ((high, hTh), (high, hTl), (low, hTh)):
                        ins = mm(dst, w[:, b, ks], h[:, k], start=n == 0, stop=n == 3 * KT - 1)
                        n += 1
                ins.then_inc(part_used, 1)

            def token_rows(L, stage, k0, hi, lo, ktiles, bank0, norm=None, first=True, last=True):
                for k in range(ktiles):
                    tile = projection_tile(L, stage, k0 + k)
                    pe.wait_ge(low_dve, tile.low + 1)
                    if norm is not None:
                        pe.wait_ge(hT_lo, KT * (norm + 1))
                    b = tile.count % DEEP
                    for tb in range(TB):
                        for c, (h, w) in enumerate(((hi, high), (hi, low), (lo, high))):
                            for s in range(2):
                                ins = mm(PS[:, bank0 + 2 * tb + s], h[:, k, tb * P:(tb + 1) * P], w[:, b, s * 512:(s + 1) * 512],
                                         start=first and k == 0 and c == 0, stop=last and k == ktiles - 1 and c == 2)
                    ins.then_inc(part_used, 1)

            pe.wait_ge(in_c, 16)
            pe.wait_ge(zeros_made, 1)
            for L in range(DEPTH):
                V = vec[:, L]
                norm(3 * L)
                def scores(tb, h0, h1, banks):
                    nk = P * (tb + 1)
                    for h in range(h0, h1):
                        r = slice(64 * (h // 4), 64 * (h // 4) + 64)
                        at, per = (h - h0) * nk, 512 // nk
                        ins = mm(PS[:, banks[(h - h0) // per], at % 512:at % 512 + nk], aT[r, h % 4, tb * P:(tb + 1) * P], aT[r, T_K, 0:nk],
                                 start=True, stop=True)
                    ins.then_inc(sc_ps, 1)

                def transpose_weights(tb):
                    pe.wait_ge(p_ready, TB * L + tb + 1)
                    for h in range(NH):
                        for s in range(tb + 1):
                            i = h * (tb + 1) + s
                            n = (2 if tb else 0) + i // 4
                            if i % 4 == 0:
                                if n in (0, 1):
                                    pe.wait_ge(lg_made, 3 * L + 2)
                                elif n in (2, 3):
                                    pe.wait_ge(lg_made, 3 * L + 3)
                                else:
                                    pe.wait_ge(pT_ready, 6 * L + n - 3)
                            ins = pe.transpose(PS[:, PT_BANKS[n], (i % 4) * P:(i % 4 + 1) * P], (lg1 if tb else lg0)[:, h, s * P:(s + 1) * P], ident)
                            if i % 4 == 3:
                                ins.then_inc(pT_ps, 1)

                for m in range(IN_TILES):
                    if m >= 4:
                        pe.wait_ge(in_evac, IN_TILES * L + m - 3)
                    channel_rows(projection_tile(L, "in", m), PS[:, 4 + m % 4, 0:SEQ], None if m else 3 * L)
                    if m == 7:
                        pe.wait_ge(in_evac, IN_TILES * L + QKV_TILES)
                        pe.wait_ge(hT_lo, KT * (3 * L + 1))
                        for tb in range(TB):
                            ins = pe.transpose(PS[:, 0, tb * P:(tb + 1) * P], aT[:, T_V, tb * P:(tb + 1) * P], ident)
                        ins.then_inc(vtA_ps, 1)
                    elif m == 8:
                        scores(0, 0, NH, (1, 2))
                    elif m == 9:
                        pe.wait_ge(vtA_ready, L + 1)
                        scores(1, 0, 4, (3, 0))
                    elif m == 10:
                        pe.wait_ge(lg_made, 3 * L + 1)
                        scores(1, 4, NH, (1, 2))
                    elif m == 12:
                        transpose_weights(0)
                    elif m == 14:
                        transpose_weights(1)
                    elif m == 16:
                        for tb in range(TB):
                            pe.wait_ge(pT_ready, 6 * L + (6 if tb else 3))
                            for h in range(NH):
                                for s in range(tb + 1):
                                    ins = mm(PS[:, 1 + tb, h * HD:(h + 1) * HD], PT1[:, h, s] if tb else PT0[:, h],
                                             vtA[:, s, HD * (h // 4):HD * (h // 4 + 1)], start=s == 0, stop=s == tb)
                            ins.then_inc(pv_ps, 1)
                pe.wait_ge(pT_ready, 6 * (L + 1))
                pe.wait_ge(in_evac, IN_TILES * (L + 1))
                pe.wait_ge(ao_normed, L + 1)
                for k in range(4):
                    for tb in range(TB):
                        ins = pe.transpose(PS[:, AOT_BANKS[k // 2], (k % 2) * SEQ + tb * P:(k % 2) * SEQ + (tb + 1) * P], ao[:, tb, k * P:(k + 1) * P], ident)
                    if k % 2:
                        ins.then_inc(aoT_ps, 1)
                keep_warm(6, 4)
                pe.wait_ge(filled[S_LORA % RING], 16 * fills(L, S_LORA))
                w = ring[:, S_LORA % RING, :]
                pe.wait_ge(yTa_ready, L + 1)
                pe.wait_ge(lora_in, 2 * (L + 1))
                for t in range(4):
                    ins = mm(PS[:, t // 2, (t % 2) * SEQ:(t % 2 + 1) * SEQ], w[0:64, t * P:(t + 1) * P], xw_t[0:64], start=True, stop=True)
                ins.then_inc(lora_ps, 1)
                for t in range(4):
                    ins = mm(PS[:, 2 + t // 2, (t % 2) * SEQ:(t % 2 + 1) * SEQ], w[64:128, t * P:(t + 1) * P], fm[64:128, T_LORA], start=True, stop=True)
                ins.then_inc(lora_ps, 1)
                for t in range(4):
                    dst = PS[:, 4 + t // 2, (t % 2) * SEQ:(t % 2 + 1) * SEQ]
                    mm(dst, w[:, 512 + t * P:512 + (t + 1) * P], xg_s[:, 0], start=True, stop=False)
                    ins = mm(dst, w[0:32, 1024 + t * P:1024 + (t + 1) * P], xg_s[0:32, 1], start=False, stop=True)
                ins.then_inc(lora_ps, 1)
                pe.wait_ge(sqk_ready, L + 1)
                for n in range(2):
                    ins = mm(PS[:, 6 + n], ones2, sqk[:, 2 * n:2 * n + 2].rearrange("p a b -> p (a b)"), start=True, stop=True)
                ins.then_inc(kss_ps, 1)
                pe.wait_ge(kss_max, L + 1)
                keep_warm(6, 4)
                pe.wait_ge(rk_ready, L + 1)
                for n in range(2):
                    ins = mm(PS[:, 6 + n], ones2, rkprod[:, 2 * n:2 * n + 2].rearrange("p a b -> p (a b)"), start=True, stop=True)
                ins.then_inc(bonus_ps, 1)
                pe.wait_ge(gates_ready, 2 * (L + 1))
                pe.wait_ge(g_ready, L + 1)
                for n, src in enumerate((fm[:, 8:12], bt, kt)):
                    if n == 1:
                        keep_warm(2, 4)
                        pe.wait_ge(bkt_ready, 2 * L + 1)
                    for tb in range(TB):
                        for t in range(4):
                            ins = pe.transpose(PS[:, 2 * n + tb, t * P:(t + 1) * P], src[:, t, tb * P:(tb + 1) * P], ident)
                    ins.then_inc(tok_ps, 1)
                pe.wait_ge(bkt_ready, 2 * (L + 1))
                pe.wait_ge(bonus_ready, L + 1)
                for n in range(16):
                    tb, h = n // NH, n % NH
                    r = slice(64 * (h % 2), 64 * (h % 2) + 64)
                    if n >= 2:
                        pe.wait_ge(prod_ready, 16 * L + n - 1)
                    rhs2 = ar[r, h // 2, tb].rearrange("p a b -> p (a b)")
                    mm(PS[:, 6 + n % 2, 0:256], bt[r, h // 2, tb * P:(tb + 1) * P], rhs2, start=True, stop=True)
                    mm(PS[:, 6 + n % 2, 256:512], kt[r, h // 2, tb * P:(tb + 1) * P], rhs2, start=True, stop=True).then_inc(prod_ps, 1)
                pe.wait_ge(tok_ready, 3 * (L + 1))
                pe.wait_ge(prod_ready, 16 * (L + 1))
                for lv in range(LEVELS):
                    for g in range(4):
                        pe.wait_ge(mt_ready, (LEVELS + 3) * L + (3 + lv if lv else g) + 1)
                        if lv == 1:
                            pe.wait_ge(xm_ready, 4 * LEVELS * L + g + 1)
                        elif lv:
                            pe.wait_ge(x_made, 4 * ((LEVELS - 2) * L + lv - 2) + g + 1)
                        for n in range(4 * g, 4 * g + 4):
                            ins = mm(PS[:, g, (n % 4) * P:(n % 4 + 1) * P], Mt[:, lv % 2, n], X[:, n] if lv else ident, start=True, stop=True)
                        ins.then_inc(m_ps, 1)
                    if lv == 0:
                        continue
                    for g in range(4):
                        pe.wait_ge(px_ready, 4 * ((LEVELS - 1) * L + lv - 1) + g + 1)
                        for n in range(4 * g, 4 * g + 4):
                            ins = mm(PS[:, g, (n % 4) * P:(n % 4 + 1) * P], PX[:, n], XT[:, n], start=True, stop=True)
                        ins.then_inc(xpt_ps, 1)
                    if lv == LEVELS - 1:
                        continue
                    for g in range(4):
                        pe.wait_ge(xm_ready, 4 * (LEVELS * L + lv) + g + 1)
                        for n in range(4 * g, 4 * g + 4):
                            ins = pe.transpose(PS[:, 4 + g, (n % 4) * P:(n % 4 + 1) * P], XT[:, n], ident)
                        ins.then_inc(x_ps, 1)
                pe.wait_ge(xm_ready, 4 * LEVELS * (L + 1))
                for c in range(NCHUNK):
                    tb, o = c // 2, 64 * (c % 2)
                    rows, cols = slice(o, o + 64), slice(o, o + 64)
                    if c:
                        pe.wait_ge(st_ready, (NCHUNK - 1) * L + c)
                    for t in range(4):
                        if c:
                            mm(PS[rows, 0, t * P:(t + 1) * P], ar[:, t, tb, 0, cols], ST[:, (c - 1) % 2, t], start=True, stop=False)
                        for h in (2 * t, 2 * t + 1):
                            ins = mm(PS[rows, 0, h * HD:(h + 1) * HD], prods[:, tb * NH + h, 256 + o:256 + o + 64], vtok[:, tb, h * HD:(h + 1) * HD],
                                     start=c == 0, stop=c == 0 or h % 2 == 1)
                    ins.then_inc(rhs_ps, 1)
                    pe.wait_ge(rhs_ready, NCHUNK * L + c + 1)
                    for h in range(NH):
                        ins = mm(PS[rows, 1, h * HD:(h + 1) * HD], XT[:, tb * NH + h, cols], rhs[:, h * HD:(h + 1) * HD], start=True, stop=True)
                    ins.then_inc(sa_ps, 1)
                    pe.wait_ge(sa_ready, NCHUNK * L + c + 1)
                    if c < NCHUNK - 1:
                        for h in range(NH):
                            hr = slice(64 * (h % 2), 64 * (h % 2) + 64)
                            dst = PS[hr, 3, (h // 2) * HD:(h // 2 + 1) * HD]
                            mm(dst, btok[rows, tb, h * HD:(h + 1) * HD], sa[rows, h * HD:(h + 1) * HD], start=True, stop=False)
                            ins = mm(dst, ktok[rows, tb, h * HD:(h + 1) * HD], vtok[rows, tb, h * HD:(h + 1) * HD], start=False, stop=True)
                        ins.then_inc(st_ps, 1)
                    if c:
                        pe.wait_ge(y_ready, NCHUNK * L + c)
                    for t in range(4):
                        if c:
                            mm(PS[rows, 2, t * P:(t + 1) * P], ar[:, t, tb, 1, cols], ST[:, (c - 1) % 2, t], start=True, stop=False)
                        for h in (2 * t, 2 * t + 1):
                            dst = PS[rows, 2, h * HD:(h + 1) * HD]
                            mm(dst, prods[:, tb * NH + h, 128 + o:128 + o + 64], sa[:, h * HD:(h + 1) * HD], start=c == 0, stop=False)
                            ins = mm(dst, prods[:, tb * NH + h, 384 + o:384 + o + 64], vtok[:, tb, h * HD:(h + 1) * HD], start=False, stop=c == 0 or h % 2 == 1)
                    ins.then_inc(y_ps, 1)
                def transpose_y(tb):
                    pe.wait_ge(yn_ready, TB * L + tb + 1)
                    for t in range(4):
                        ins = pe.transpose(PS[:, 4 + t // 2, (t % 2) * SEQ + tb * P:(t % 2) * SEQ + (tb + 1) * P], yc[:, tb, t * P:(t + 1) * P], ident)
                    return ins

                transpose_y(0)
                pe.wait_ge(y_ready, NCHUNK * (L + 1))
                token_rows(L, "out", 0, hTh, hTl, 4, 0, last=False)
                transpose_y(1).then_inc(yT_ps, 1)
                for n in range(2):
                    pe.wait_ge(yTr_ready, 2 * L + n + 1)
                    ks = slice(4 + 2 * n, 6 + 2 * n)
                    token_rows(L, "out", 4 + 2 * n, hTh[:, ks], hTl[:, ks], 2, 0, first=False, last=n == 1)
                norm(3 * L + 1)
                for m in range(HC):
                    if m >= 4:
                        pe.wait_ge(q_ready, HC * L + m - 3)
                    channel_rows(projection_tile(L, "wq", m), PS[:, 4 + m % 4, 0:SEQ], None if m else 3 * L + 1)
                pe.wait_ge(q_ready, HC * (L + 1))
                for n in range(8):
                    for j in range(4):
                        hc = 4 * (n % 4) + j
                        keys = V[:, C_KEYS + (hc % 2) * NSUB:C_KEYS + (hc % 2 + 1) * NSUB]
                        ins = mm(PS[:, n, j * P:(j + 1) * P], qT[:, hc, (n // 4) * P:(n // 4 + 1) * P], keys, start=True, stop=True)
                    ins.then_inc(psc_ps, 1)
                pe.wait_ge(psc_ready, 8 * (L + 1))
                for n in range(4):
                    mm(PS[:, n], zeros[:], cst[:, 0:512], start=True, stop=False, skip_group_check=True)
                g0 = NGROUPS * NQ * L

                def hidden(e, j, b):
                    pe.wait_ge(low_pool, POOL_ALL * L + 1 + e)
                    if L or not isinstance(e, int) or e > 1:
                        pe.wait_ge(ga_ready, NSUB * L - 1 + e)
                    b, n = (c0[L] + b) % DEEP, 0
                    for k in range(KT):
                        ks = slice(k * P, (k + 1) * P)
                        for u, h in ((high, hTh), (high, hTl), (low, hTh)):
                            ins = mm(PS[:, 6 + j % 2, 0:SEQ], u[:, b, ks], h[:, k], start=n == 0, stop=n == 3 * KT - 1)
                            n += 1
                    ins.then_inc(part_used, 1)

                def spread(g, b):
                    pe.wait_ge(hots_made, g0 + 1 + g)
                    if L or not isinstance(g, int) or g > 1:
                        pe.wait_ge(gated, g0 - 1 + g)
                    for t in range(GROUP):
                        for part in range(3):
                            ins = mm(PS[:, 4 + b, t * QT:(t + 1) * QT], hot1[:, b, t], hot2[:, b, t, part], start=part == 0, stop=part == 2)
                    ins.then_inc(spread_ps, 1)

                def spend(e, j, b, pool=False, later=0):
                    if pool:
                        pe.wait_ge(low_pool, POOL_ALL * L + (NSUB - HELD + 1) + e)
                    else:
                        pe.wait_ge(low_dve, v0[L] + (1 - later) + e)
                    pe.wait_ge(w_lo, NSUB * L + 1 + e)
                    b = (c0[L] + b) % DEEP
                    for tb in range(TB):
                        for w, v in ((WH, high), (WH, low), (WL, high)):
                            for s in range(2):
                                ins = mm(PS[:, 2 * tb + s], w[:, j % 2, tb * P:(tb + 1) * P], v[:, b, s * 512:(s + 1) * 512],
                                         start=False, stop=False, skip_group_check=True)
                    ins.then_inc(part_used, 1)

                for e in range(4):
                    hidden(e, e, e)
                with pe.Fori(1, A_TOP // 4) as i:
                    for j in range(4):
                        hidden(4 * i + j, j, j)
                for e in range(A_TOP // 4 * 4, A_TOP):
                    hidden(e, e, e)
                pe.wait_ge(slot_ready, TB * (L + 1))
                for c in range(3):
                    for tb in range(TB):
                        at = (c % 2) * SEQ + tb * P
                        ins = pe.transpose(PS[:, 4 + c // 2, at:at + P], slot[:, c, tb], ident)
                ins.then_inc(slot_ps, 1)
                for e in range(A_TOP, A_LOOP + 4):
                    hidden(e, e, e)
                    if e in (A_LOOP, A_LOOP + 2):
                        spread(e // 2 - A_LOOP // 2, e // 2 % 2)
                with pe.Fori(0, (HELD - A_LOOP - 4) // 4) as i:
                    for j in range(4):
                        hidden(4 * i + (j + A_LOOP + 4), j, j)
                        spread(6 * i + (2 + 3 * j // 2), 3 * j // 2 % 2)
                        if j % 2:
                            spread(6 * i + (2 + 3 * j // 2 + 1), (3 * j // 2 + 1) % 2)
                with pe.Fori(0, HELD // 4) as i:
                    for j in range(4):
                        spread(4 * i + (j + NGROUPS), j % 2)
                        hidden(4 * i + (j + HELD), j, 2 * j)
                        spend(4 * i + j, j, 2 * j + 1)
                with pe.Fori(HELD // 4, (HELD + QT) // 4) as i:
                    for j in range(4):
                        spread(4 * i + (j + NGROUPS), j % 2)
                        spend(4 * i + j, j, j, pool=True)
                with pe.Fori((HELD + QT) // 4, NSUB // 4) as i:
                    for j in range(4):
                        spend(4 * i + j, j, j, later=QT)
                for n in range(4):
                    ins = mm(PS[:, n], zeros[:], cst[:, 0:512], start=False, stop=True, skip_group_check=True)
                ins.then_inc(peer_ps, 1)
                if L == 0:
                    pe.wait_ge(p_lo, 1)
                token_rows(L, "ple", 0, pTh[:, L], pTl[:, L], 2, 4)
                norm(3 * L + 2)
                token_rows(L, "ple", 2, hTh, hTl, KT, 0, 3 * L + 2)


def shape_constants():
    c = np.zeros((P, NCONST), np.float32)
    i = np.arange(P)
    s, t = i[:, None], i[None, :]
    same = s // CHUNK == t // CHUNK
    c[:, K_ID:K_ID + P] = s == t
    c[:, K_ONES:K_ONES + P] = s // HD == t // HD
    c[:, K_PMASK:K_PMASK + P] = same & (s < t)
    c[:, K_PMASK + P:K_PMASK + 2 * P] = same & (s <= t)
    for lv in range(LEVELS):
        bs, bt = s >> lv, t >> lv
        c[:, K_LMASK + lv * P:K_LMASK + (lv + 1) * P] = (bt % 2 == 1) & (bs == bt - 1)
    c[:, K_RESET:K_RESET + SEQ] = np.arange(SEQ)[None, :] % CHUNK != 0
    for k0, q0, nk in ((K_DIST0, 0, P), (K_DIST1, P, 2 * P)):
        q, key = q0 + i[:, None], np.arange(nk)[None, :]
        back = q // CHUNK - key // CHUNK
        c[:, k0:k0 + nk] = np.where((back >= 0) & (back <= 1), np.abs(q - key), 1e33)
    c[:, K_IOTA:K_IOTA + NSUB] = i[None, :]
    c[:, K_IOTA16:K_IOTA16 + TOPK] = np.arange(TOPK)[None, :]
    return c


def lay_out(a):
    f = np.float32
    A, RW = 768, 1824
    w_in, b_in = np.asarray(a["w_in"]), np.asarray(a["b_in"])
    q_order = np.concatenate([np.concatenate([np.arange(HD) + HD * t, np.arange(HD) + HD * (t + 4)]) for t in range(4)])

    def in_tiles(m):
        pad = np.zeros(m.shape[:-1] + (RW_TILES * P - RW,), f)
        return np.concatenate([m[..., q_order], m[..., 512:A], m[..., A:A + RW], pad], -1)

    def column_slabs(w):
        n = w.shape[1] // P
        s = w.reshape(KT, P, n, P).transpose(2, 1, 0, 3).reshape(n, P, D)
        if n % 2:
            s = np.concatenate([s, np.zeros((1, P, D), f)])
        return s.reshape(-1, 2, P, D).transpose(0, 2, 1, 3).reshape(-1, P, SLABW)

    def row_slabs(w):
        return w.reshape(-1, 2, P, D).transpose(0, 2, 1, 3).reshape(-1, P, SLABW)

    def cols(v):
        return v.reshape(-1, P).T

    slabs, vecs, peer = [], [], []
    for L in range(DEPTH):
        g = lambda n: np.asarray(a[n])[L]
        lora = np.zeros((P, SLABW), f)
        lora[0:64, 0:512], lora[64:128, 0:512] = g("rwkv_w_up"), g("rwkv_a_up")
        lora[:, 512:1024], lora[0:32, 1024:1536] = g("rwkv_g_up")[0:P], g("rwkv_g_up")[P:]
        slabs.append(np.concatenate([column_slabs(in_tiles(w_in[L])), lora[None], row_slabs(g("w_out")), column_slabs(g("peer_wq")),
                                     row_slabs(g("ple_proj")), row_slabs(g("ple_gate"))]))
        mu = np.concatenate([g("rwkv_mu"), np.zeros(RW_TILES * P - RW, f)])
        v = [cols(g("norm_mix")), cols(g("norm_ffn")), cols(g("norm_ple")), cols(in_tiles(b_in[L])), cols(mu)]
        v += [cols(g("rwkv_" + n).reshape(-1)) for n in ("w0", "a0", "k_k", "k_a", "r_k", "lnx_w", "lnx_b")]
        v += [cols(g("attn_out_norm")), np.broadcast_to(g("attn_sinks")[None], (P, NH))]
        v += [g("peer_keys")[c].T for c in range(2)]
        vecs.append(np.concatenate(v, 1))
        u = g("peer_u").reshape(NSUB, NSUB, KT, P).transpose(1, 3, 2, 0).reshape(NSUB, P, D)
        t = g("peer_v").reshape(NSUB, NSUB, D).transpose(1, 0, 2)
        pairs = lambda m: m.reshape(-1, 2, P, D).transpose(0, 2, 1, 3).reshape(-1, P, SLABW)
        peer.append(np.concatenate([pairs(u[:HELD]), np.concatenate([u[HELD:], t[:HELD]], 2), pairs(t[HELD:])]))
    p = np.asarray(a["p"])[:, 0]
    return {
        "x": np.asarray(a["x"])[0].reshape(TB, P, D).transpose(1, 0, 2),
        "w_slabs": np.stack(slabs),
        "peer_slabs": np.stack(peer),
        "vecs": np.stack(vecs, 1),
        "consts": shape_constants(),
        "p_t": p.transpose(0, 2, 1).reshape(DEPTH, 2, P, SEQ).transpose(2, 0, 1, 3),
        "g_final": np.broadcast_to(np.asarray(a["norm_final"])[None], (P, D)),
    }


def kernel(**inputs):
    from concourse import bacc
    from concourse.bass_utils import run_bass_kernel_spmd

    nc = bacc.Bacc("TRN2", target_bir_lowering=False, num_devices=1)
    arrays, args = {}, []
    for name, v in lay_out(inputs).items():
        v = np.ascontiguousarray(v)
        arrays[f"in_{name}"] = v
        args.append(nc.dram_tensor(f"in_{name}", v.shape, mybir.dt.from_np(v.dtype), kind="ExternalInput").ap())
    out = nc.dram_tensor("out", (P, TB, D), F32, kind="ExternalOutput").ap()
    hybrid_encoder(nc, *args, out)
    r = run_bass_kernel_spmd(nc, [arrays], core_ids=[0])
    return r.results[0]["out"].transpose(1, 0, 2).reshape(1, SEQ, D)
```
